# Optimizing a Trainium2 kernel written in Bass

```python
import jax
import jax.numpy as jnp
from jax import lax
import numpy as np
import math
import jax, jax.numpy as jnp

D_MODEL = 1024
BATCH = 1
SEQ = 256
DEPTH = 2

CTX_LEN = 256
GRID_W = 64
N_EVEN = (DEPTH + 1) // 2
N_ODD = DEPTH // 2
EPS = 1e-6

MLA_HEADS = 8
QK_NOPE = 64
QK_ROPE = 32
QK_HEAD = QK_NOPE + QK_ROPE
V_HEAD = 64
Q_LORA = 384
KV_LORA = 256
ROPE_BASE = 10000.0
Q_BLOCK = 128

FNET_GROUPS = 4
FNET_GROUP_W = 128
FNET_W = FNET_GROUPS * FNET_GROUP_W

CONF_GROUPS = 4
CONF_W = 512
CONF_WIDTH = 31
SC_W = 512
SC_WIDTH = 3

D_FF = -(-8 * D_MODEL // (3 * 256)) * 256

EVEN_KV_END = Q_LORA + KV_LORA + QK_ROPE
EVEN_IN = EVEN_KV_END + FNET_W
EVEN_MIX = MLA_HEADS * V_HEAD + FNET_W
ODD_IN = 2 * CONF_W + 3 * SC_W
ODD_MIX = CONF_W + SC_W


def rms_norm(x, g):
    xf = x.astype(jnp.float32)
    y = xf * lax.rsqrt(jnp.mean(jnp.square(xf), axis=-1, keepdims=True) + EPS)
    return (y * g.astype(jnp.float32)).astype(x.dtype)

def group_layer_norm(x, g, b, groups):
    bsz, n, w = x.shape
    xf = x.astype(jnp.float32).reshape(bsz, n, groups, w // groups)
    mu = jnp.mean(xf, axis=-1, keepdims=True)
    var = jnp.mean(jnp.square(xf - mu), axis=-1, keepdims=True)
    y = ((xf - mu) * lax.rsqrt(var + EPS)).reshape(bsz, n, w)
    return (y * g.astype(jnp.float32) + b.astype(jnp.float32)).astype(x.dtype)

def modulate(h, shift, scale):
    return h * (1.0 + scale) + shift

def ada_mod(cvec, w, b):
    return jnp.split(jax.nn.silu(cvec) @ w + b, 6, axis=-1)

def axial_rope_tables(n):
    rows = n // GRID_W
    row = jnp.broadcast_to(jnp.arange(rows, dtype=jnp.float32)[:, None], (rows, GRID_W)).reshape(n)
    col = jnp.broadcast_to(jnp.arange(GRID_W, dtype=jnp.float32)[None, :], (rows, GRID_W)).reshape(n)
    per_axis = QK_ROPE // 4
    inv_freq = ROPE_BASE ** (-jnp.arange(per_axis, dtype=jnp.float32) / per_axis)
    ang = jnp.concatenate([row[:, None] * inv_freq, col[:, None] * inv_freq], axis=-1)
    return jnp.cos(ang), jnp.sin(ang)

def rope_tail(t, rope):
    if rope is None:
        return t
    cos, sin = rope
    half = QK_ROPE // 2
    r = t[..., QK_NOPE:].astype(jnp.float32)
    r1, r2 = r[..., :half], r[..., half:]
    rot = jnp.concatenate([r1 * cos - r2 * sin, r2 * cos + r1 * sin], axis=-1).astype(t.dtype)
    return jnp.concatenate([t[..., :QK_NOPE], rot], axis=-1)

def mla_queries(cq, q_ln_g, w_uq, q_norm_g, rope):
    q = jnp.einsum('bsr,rhd->bshd', rms_norm(cq, q_ln_g), w_uq)
    return rope_tail(rms_norm(q, q_norm_g), rope)

def mla_keys_values(ckv, kr, kv_ln_g, w_uk, w_uv, k_norm_g, rope):
    ckv = rms_norm(ckv, kv_ln_g)
    k_nope = jnp.einsum('bsr,rhd->bshd', ckv, w_uk)
    v = jnp.einsum('bsr,rhd->bshd', ckv, w_uv)
    k_rope = jnp.broadcast_to(kr[:, :, None, :], k_nope.shape[:-1] + (QK_ROPE,))
    k = rope_tail(rms_norm(jnp.concatenate([k_nope, k_rope], axis=-1), k_norm_g), rope)
    return k, v

def latent_attention(q, k, v, k_ctx, v_ctx):
    bsz, n, heads, dq = q.shape
    kt = jnp.concatenate([k_ctx, k], axis=1).transpose(0, 2, 1, 3)
    vt = jnp.concatenate([v_ctx, v], axis=1).transpose(0, 2, 1, 3)
    qb = q.reshape(bsz, n // Q_BLOCK, Q_BLOCK, heads, dq).transpose(1, 0, 2, 3, 4)
    scale = dq ** -0.5

    def block(qi):
        s = jnp.einsum('bqhd,bhkd->bhqk', qi, kt).astype(jnp.float32) * scale
        p = jax.nn.softmax(s, axis=-1).astype(vt.dtype)
        return jnp.einsum('bhqk,bhkd->bqhd', p, vt)

    o = lax.map(block, qb)
    return o.transpose(1, 0, 2, 3, 4).reshape(bsz, n, heads * V_HEAD)

def context_attention(q, k, v):
    bsz, n, heads, dq = q.shape
    s = jnp.einsum('bqhd,bkhd->bhqk', q, k).astype(jnp.float32) * (dq ** -0.5)
    p = jax.nn.softmax(s, axis=-1).astype(v.dtype)
    return jnp.einsum('bhqk,bkhd->bqhd', p, v).reshape(bsz, n, heads * V_HEAD)

def fourier_mix(u):
    bsz, n, _ = u.shape
    ug = u.astype(jnp.float32).reshape(bsz, n, FNET_GROUPS, FNET_GROUP_W)
    y = jnp.fft.fft2(ug, axes=(1, 3), norm='ortho').real
    return y.reshape(bsz, n, FNET_W).astype(u.dtype)

def depthwise_conv(u, w):
    width, ch = w.shape
    pad = (width - 1) // 2
    return lax.conv_general_dilated(
        u, w[:, None, :].astype(u.dtype), window_strides=(1,), padding=[(pad, pad)],
        dimension_numbers=('NWC', 'WIO', 'NWC'), feature_group_count=ch)

def odd_mixer(u, conf_dw, conf_dw_b, conf_ln_g, conf_ln_b, sc_dw):
    a, gate, sb, scc, sx = jnp.split(
        u, [CONF_W, 2 * CONF_W, 2 * CONF_W + SC_W, 2 * CONF_W + 2 * SC_W], axis=-1)
    conf = a * jax.nn.sigmoid(gate)
    conf = depthwise_conv(conf, conf_dw) + conf_dw_b
    conf = jax.nn.silu(group_layer_norm(conf, conf_ln_g, conf_ln_b, CONF_GROUPS))
    sc = sb * depthwise_conv(scc * sx, sc_dw)
    return jnp.concatenate([conf, sc], axis=-1)

def swiglu(h, w1, w3, w2):
    return (jax.nn.silu(h @ w1) * (h @ w3)) @ w2

def first_inputs(seed: int = 0) -> dict:
    key = jax.random.key(seed)
    keys = iter(jax.random.split(key, 40))

    def normal(shape, scale):
        return jax.random.normal(next(keys), shape, jnp.float32) * scale

    def gain(shape):
        return 1.0 + 0.05 * jax.random.normal(next(keys), shape, jnp.float32)

    E, O, L, D = N_EVEN, N_ODD, DEPTH, D_MODEL
    return {
        'x': normal((BATCH, SEQ, D), 1.0),
        'c': normal((BATCH, D), 1.0),
        'ctx': normal((BATCH, CTX_LEN, D), 1.0),
        'c_ctx': normal((D,), 1.0),
        'ada_w': normal((L, D, 6 * D), 0.5 * D ** -0.5),
        'ada_b': normal((L, 6 * D), 0.02),
        'norm1_g': gain((L, D)),
        'norm2_g': gain((L, D)),
        'ffn_w1': normal((L, D, D_FF), D ** -0.5),
        'ffn_w3': normal((L, D, D_FF), D ** -0.5),
        'ffn_w2': normal((L, D_FF, D), D_FF ** -0.5),
        'a_w_in': normal((E, D, EVEN_IN), D ** -0.5),
        'a_q_ln_g': gain((E, Q_LORA)),
        'a_kv_ln_g': gain((E, KV_LORA)),
        'a_w_uq': normal((E, Q_LORA, MLA_HEADS, QK_HEAD), Q_LORA ** -0.5),
        'a_w_uk': normal((E, KV_LORA, MLA_HEADS, QK_NOPE), KV_LORA ** -0.5),
        'a_w_uv': normal((E, KV_LORA, MLA_HEADS, V_HEAD), KV_LORA ** -0.5),
        'a_q_norm_g': gain((E, QK_HEAD)),
        'a_k_norm_g': gain((E, QK_HEAD)),
        'a_w_out': normal((E, EVEN_MIX, D), EVEN_MIX ** -0.5),
        'b_w_in': normal((O, D, ODD_IN), D ** -0.5),
        'b_conf_dw': normal((O, CONF_WIDTH, CONF_W), CONF_WIDTH ** -0.5),
        'b_conf_dw_b': normal((O, CONF_W), 0.02),
        'b_conf_ln_g': gain((O, CONF_W)),
        'b_conf_ln_b': normal((O, CONF_W), 0.02),
        'b_sc_dw': normal((O, SC_WIDTH, SC_W), SC_WIDTH ** -0.5),
        'b_w_out': normal((O, ODD_MIX, D), ODD_MIX ** -0.5),
    }

def first_block(x, c, ctx, c_ctx, ada_w, ada_b, norm1_g, norm2_g, ffn_w1, ffn_w3, ffn_w2,
              a_w_in, a_q_ln_g, a_kv_ln_g, a_w_uq, a_w_uk, a_w_uv, a_q_norm_g, a_k_norm_g, a_w_out,
              b_w_in, b_conf_dw, b_conf_dw_b, b_conf_ln_g, b_conf_ln_b, b_sc_dw, b_w_out):
    n = x.shape[1]
    cos, sin = axial_rope_tables(n)
    rope = (cos[:, None, :], sin[:, None, :])
    for i in range(DEPTH):
        ctx_needed = any(l % 2 == 0 for l in range(i + 1, DEPTH))
        j = i // 2
        sh1, sc1, g1, sh2, sc2, g2 = [t[:, None, :] for t in ada_mod(c, ada_w[i], ada_b[i])]
        h = modulate(rms_norm(x, norm1_g[i]), sh1, sc1)
        if i % 2 == 0 or ctx_needed:
            csh1, csc1, cg1, csh2, csc2, cg2 = ada_mod(c_ctx, ada_w[i], ada_b[i])
            hc = modulate(rms_norm(ctx, norm1_g[i]), csh1, csc1)
        if i % 2 == 0:
            w_in = a_w_in[j]
            u = h @ w_in
            ukc = hc @ w_in[:, Q_LORA:EVEN_KV_END]
            k_c, v_c = mla_keys_values(ukc[..., :KV_LORA], ukc[..., KV_LORA:], a_kv_ln_g[j],
                                       a_w_uk[j], a_w_uv[j], a_k_norm_g[j], None)
            k, v = mla_keys_values(u[..., Q_LORA:Q_LORA + KV_LORA], u[..., Q_LORA + KV_LORA:EVEN_KV_END],
                                   a_kv_ln_g[j], a_w_uk[j], a_w_uv[j], a_k_norm_g[j], rope)
            q = mla_queries(u[..., :Q_LORA], a_q_ln_g[j], a_w_uq[j], a_q_norm_g[j], rope)
            o = jnp.concatenate([latent_attention(q, k, v, k_c, v_c), fourier_mix(u[..., EVEN_KV_END:])], axis=-1)
            mix = o @ a_w_out[j]
            if ctx_needed:
                q_c = mla_queries(hc @ w_in[:, :Q_LORA], a_q_ln_g[j], a_w_uq[j], a_q_norm_g[j], None)
                oc = jnp.concatenate([context_attention(q_c, k_c, v_c),
                                      fourier_mix(hc @ w_in[:, EVEN_KV_END:])], axis=-1)
                mix_c = oc @ a_w_out[j]
        else:
            mix = odd_mixer(h @ b_w_in[j], b_conf_dw[j], b_conf_dw_b[j], b_conf_ln_g[j],
                            b_conf_ln_b[j], b_sc_dw[j]) @ b_w_out[j]
            if ctx_needed:
                mix_c = odd_mixer(hc @ b_w_in[j], b_conf_dw[j], b_conf_dw_b[j], b_conf_ln_g[j],
                                  b_conf_ln_b[j], b_sc_dw[j]) @ b_w_out[j]
        x = x + g1 * mix
        x = x + g2 * swiglu(modulate(rms_norm(x, norm2_g[i]), sh2, sc2), ffn_w1[i], ffn_w3[i], ffn_w2[i])
        if ctx_needed:
            ctx = ctx + cg1 * mix_c
            ctx = ctx + cg2 * swiglu(modulate(rms_norm(ctx, norm2_g[i]), csh2, csc2),
                                     ffn_w1[i], ffn_w3[i], ffn_w2[i])
    return x


N_HEADS = 16
HEAD_DIM = D_MODEL // N_HEADS
D_FF_2 = 4 * D_MODEL
N_A_LAYERS = DEPTH // 2
N_B_LAYERS = DEPTH - N_A_LAYERS
MOBA_BLOCK = 256
MOBA_TOPK = 3
MOBA_Q_CHUNK = 16
FOX_Q_BLOCK = 128
RMS_EPS = 1e-6
NEG_INF = -1e30


def rms_norm_2(x, g):
    xf = x.astype(jnp.float32)
    y = xf * lax.rsqrt(jnp.mean(xf * xf, axis=-1, keepdims=True) + RMS_EPS)
    return (y * g.astype(jnp.float32)).astype(x.dtype)

def alibi_slopes(n):
    return jnp.asarray(2.0 ** (-8.0 * np.arange(1, n + 1) / n), dtype=jnp.float32)

def split_heads(t):
    b, s, _ = t.shape
    return t.reshape(b, s, N_HEADS, HEAD_DIM).transpose(0, 2, 1, 3)

def merge_heads(t):
    b, h, s, d = t.shape
    return t.transpose(0, 2, 1, 3).reshape(b, s, h * d)

def squared_relu_mlp(x, w_up, w_down):
    return jnp.square(jax.nn.relu(x @ w_up)) @ w_down

def moba_attention(q, k, v):
    b, h, s, d = q.shape
    nb = -(-s // MOBA_BLOCK)
    pad = ((0, 0), (0, 0), (0, nb * MOBA_BLOCK - s), (0, 0))
    kb = jnp.pad(k, pad).reshape(b, h, nb, MOBA_BLOCK, d)
    vb = jnp.pad(v, pad).reshape(b, h, nb, MOBA_BLOCK, d)
    scale = 1.0 / math.sqrt(d)
    slopes = alibi_slopes(h)[None, :, None, None]
    n_sel = min(MOBA_TOPK, nb - 1)
    own_blk = jnp.arange(s) // MOBA_BLOCK
    bi = jnp.arange(b)[:, None, None, None]
    hi = jnp.arange(h)[None, :, None, None]

    if n_sel > 0:
        k_mean = jnp.mean(kb.astype(jnp.float32), axis=3)
        gate = jnp.einsum('bhsd,bhnd->bhsn', q.astype(jnp.float32), k_mean)
        past = jnp.arange(nb)[None, :] < own_blk[:, None]
        gate = jnp.where(past, gate, NEG_INF)
        _, sel = lax.top_k(gate, n_sel)
        sel_valid = jnp.arange(n_sel)[None, :] < own_blk[:, None]

    n_chunks = s // MOBA_Q_CHUNK
    blk_offs = jnp.arange(MOBA_BLOCK)

    def chunk(ci):
        t0 = ci * MOBA_Q_CHUNK
        qc = lax.dynamic_slice_in_dim(q, t0, MOBA_Q_CHUNK, axis=2)
        tq = t0 + jnp.arange(MOBA_Q_CHUNK)
        blk = t0 // MOBA_BLOCK
        k_own = lax.dynamic_index_in_dim(kb, blk, axis=2, keepdims=False)
        v_own = lax.dynamic_index_in_dim(vb, blk, axis=2, keepdims=False)
        ks_own = blk * MOBA_BLOCK + blk_offs
        dist_own = (tq[:, None] - ks_own[None, :]).astype(jnp.float32)
        s_own = (jnp.einsum('bhcd,bhkd->bhck', qc, k_own).astype(jnp.float32) * scale
                 - slopes * dist_own)
        s_own = jnp.where(dist_own >= 0, s_own, NEG_INF)
        if n_sel > 0:
            sel_c = lax.dynamic_slice_in_dim(sel, t0, MOBA_Q_CHUNK, axis=2)
            valid_c = lax.dynamic_slice_in_dim(sel_valid, t0, MOBA_Q_CHUNK, axis=0)
            k_sel = kb[bi, hi, sel_c]
            v_sel = vb[bi, hi, sel_c]
            ks_sel = sel_c[..., None] * MOBA_BLOCK + blk_offs
            dist_sel = (tq[:, None, None] - ks_sel).astype(jnp.float32)
            s_sel = (jnp.einsum('bhcd,bhcnkd->bhcnk', qc, k_sel).astype(jnp.float32) * scale
                     - slopes[..., None] * dist_sel)
            s_sel = jnp.where(valid_c[:, :, None], s_sel, NEG_INF)
            scores = jnp.concatenate(
                [s_sel.reshape(b, h, MOBA_Q_CHUNK, n_sel * MOBA_BLOCK), s_own], axis=-1)
            p = jax.nn.softmax(scores, axis=-1)
            p_sel = p[..., :n_sel * MOBA_BLOCK].reshape(b, h, MOBA_Q_CHUNK, n_sel, MOBA_BLOCK).astype(v.dtype)
            p_own = p[..., n_sel * MOBA_BLOCK:].astype(v.dtype)
            return (jnp.einsum('bhcnk,bhcnkd->bhcd', p_sel, v_sel)
                    + jnp.einsum('bhck,bhkd->bhcd', p_own, v_own))
        p_own = jax.nn.softmax(s_own, axis=-1).astype(v.dtype)
        return jnp.einsum('bhck,bhkd->bhcd', p_own, v_own)

    outs = lax.map(chunk, jnp.arange(n_chunks))
    return outs.transpose(1, 2, 0, 3, 4).reshape(b, h, s, d)

def shared_kv(h, kv_norm, w_kv, w_f, b_f):
    hn = rms_norm_2(h, kv_norm)
    k, v = jnp.split(hn @ w_kv, 2, axis=-1)
    log_f = jax.nn.log_sigmoid((hn @ w_f + b_f).astype(jnp.float32))
    c = jnp.cumsum(log_f, axis=1).transpose(0, 2, 1)
    return split_heads(k), split_heads(v), c

def forgetting_attention(q, k, v, c):
    b, h, s, d = q.shape
    scale = 1.0 / math.sqrt(d)
    kpos = jnp.arange(s)

    def block(qi):
        t0 = qi * FOX_Q_BLOCK
        qb = lax.dynamic_slice_in_dim(q, t0, FOX_Q_BLOCK, axis=2)
        cq = lax.dynamic_slice_in_dim(c, t0, FOX_Q_BLOCK, axis=2)
        tq = t0 + jnp.arange(FOX_Q_BLOCK)
        sc = (jnp.einsum('bhqd,bhkd->bhqk', qb, k).astype(jnp.float32) * scale
              + cq[..., None] - c[:, :, None, :])
        sc = jnp.where(kpos[None, :] <= tq[:, None], sc, NEG_INF)
        p = jax.nn.softmax(sc, axis=-1).astype(v.dtype)
        return jnp.einsum('bhqk,bhkd->bhqd', p, v)

    outs = lax.map(block, jnp.arange(s // FOX_Q_BLOCK))
    return outs.transpose(1, 2, 0, 3, 4).reshape(b, h, s, d)

def second_inputs(seed: int = 0) -> dict:
    key = jax.random.key(seed)
    ks = jax.random.split(key, 14)
    D, F, H = D_MODEL, D_FF_2, N_HEADS
    nrm = lambda k, shape, fan_in, gain=1.0: (gain * fan_in ** -0.5) * jax.random.normal(k, shape, jnp.float32)
    return {
        "x": jax.random.normal(ks[0], (BATCH, SEQ, D), jnp.float32),
        "attn_norm": 1.0 + 0.02 * jax.random.normal(ks[1], (DEPTH, D), jnp.float32),
        "moba_w_qkv": nrm(ks[2], (N_A_LAYERS, D, 3 * D), D),
        "fox_w_q": nrm(ks[3], (N_B_LAYERS, D, D), D),
        "w_o": nrm(ks[4], (DEPTH, D, D), D, 0.5),
        "kv_norm": 1.0 + 0.02 * jax.random.normal(ks[5], (D,), jnp.float32),
        "w_kv": nrm(ks[6], (D, 2 * D), D),
        "w_f": nrm(ks[7], (D, H), D),
        "b_f": 3.0 + 0.5 * jax.random.normal(ks[8], (H,), jnp.float32),
        "mlp_norm": 1.0 + 0.02 * jax.random.normal(ks[9], (DEPTH, D), jnp.float32),
        "w_up": nrm(ks[10], (DEPTH, D, F), D),
        "w_down": nrm(ks[11], (DEPTH, F, D), F, 0.5),
        "final_norm": 1.0 + 0.02 * jax.random.normal(ks[12], (D,), jnp.float32),
    }

def second_block(x, attn_norm, moba_w_qkv, fox_w_q, w_o, kv_norm, w_kv, w_f, b_f,
              mlp_norm, w_up, w_down, final_norm):
    h = x
    k_sh = v_sh = c_sh = None
    for layer in range(DEPTH):
        if layer == N_A_LAYERS:
            k_sh, v_sh, c_sh = shared_kv(h, kv_norm, w_kv, w_f, b_f)
        hn = rms_norm_2(h, attn_norm[layer])
        if layer < N_A_LAYERS:
            q, k, v = jnp.split(hn @ moba_w_qkv[layer], 3, axis=-1)
            mix = moba_attention(split_heads(q), split_heads(k), split_heads(v))
        else:
            q = split_heads(hn @ fox_w_q[layer - N_A_LAYERS])
            mix = forgetting_attention(q, k_sh, v_sh, c_sh)
        h = h + merge_heads(mix) @ w_o[layer]
        h = h + squared_relu_mlp(rms_norm_2(h, mlp_norm[layer]), w_up[layer], w_down[layer])
    return rms_norm_2(h, final_norm)


def setup_inputs(seed=0):
    out = dict(first_inputs(seed))
    for name, value in second_inputs(seed + 1).items():
        if name != "x":
            out[name + "_2"] = value
    return out


def reference(
    x, c, ctx, c_ctx, ada_w, ada_b, norm1_g, norm2_g, ffn_w1, ffn_w3, ffn_w2, a_w_in, a_q_ln_g,
    a_kv_ln_g, a_w_uq, a_w_uk, a_w_uv, a_q_norm_g, a_k_norm_g, a_w_out, b_w_in, b_conf_dw,
    b_conf_dw_b, b_conf_ln_g, b_conf_ln_b, b_sc_dw, b_w_out, attn_norm_2, moba_w_qkv_2,
    fox_w_q_2, w_o_2, kv_norm_2, w_kv_2, w_f_2, b_f_2, mlp_norm_2, w_up_2, w_down_2,
    final_norm_2,
):
    x = first_block(
        x, c, ctx, c_ctx, ada_w, ada_b, norm1_g, norm2_g, ffn_w1, ffn_w3, ffn_w2, a_w_in,
        a_q_ln_g, a_kv_ln_g, a_w_uq, a_w_uk, a_w_uv, a_q_norm_g, a_k_norm_g, a_w_out, b_w_in,
        b_conf_dw, b_conf_dw_b, b_conf_ln_g, b_conf_ln_b, b_sc_dw, b_w_out,
    )
    return second_block(
        x, attn_norm_2, moba_w_qkv_2, fox_w_q_2, w_o_2, kv_norm_2, w_kv_2, w_f_2, b_f_2,
        mlp_norm_2, w_up_2, w_down_2, final_norm_2,
    )


_drawn_inputs = setup_inputs


def setup_inputs(seed=0):
    import zlib

    import numpy as np

    out = dict(_drawn_inputs(seed))
    spreads = {}
    factors = {'ctx': 4.243,
     'a_q_ln_g': 8.0,
     'a_kv_ln_g': 8.0,
     'a_w_uk': 2.842,
     'a_q_norm_g': 8.0,
     'a_k_norm_g': 8.0,
     'b_conf_dw_b': 8.0,
     'b_conf_ln_g': 6.907,
     'b_conf_ln_b': 8.0,
     'attn_norm_2': 8.0,
     'kv_norm_2': 8.0,
     'mlp_norm_2': 3.794,
     'final_norm_2': 2.852}
    for name, (base, spread) in spreads.items():
        noise = np.random.default_rng([zlib.crc32(name.encode()), seed]).standard_normal(out[name].shape)
        drawn = base * np.exp(spread * noise) if base else spread * noise
        out[name] = jnp.asarray(drawn.astype(out[name].dtype))
    for name, factor in factors.items():
        out[name] = (out[name] * factor).astype(out[name].dtype)
    return out
```

```python
from contextlib import ExitStack

import numpy as np

import concourse.bass as bass
from concourse import mybir

F32 = mybir.dt.float32
F32R = mybir.dt.float32r
ALU = mybir.AluOpType
ACT = mybir.ActivationFunctionType
AX = mybir.AxisListType.X
ds = bass.ds

P = 128
D = 1024
KT = D // P
T = 256
TT = T // P
CH = KT * 2 * P
EPS = 1e-6

MLA_H, NOPE, ROPE, QKH, VH = 8, 64, 32, 96, 64
CQ, CKV = 3, 2
FG = 4
CONV, SCONV = 31, 3
PAD = (CONV - 1) // 2
DFF = 2816
UT1 = DFF // P
DFF2 = 4096
UT2 = DFF2 // P
H2, HD = 16, 64
ADA = 6 * D // P
RAW, SPL, AR = 4, 2, 2

STAGES = [("w_in", 5), ("w_uk", 1), ("w_uq", 2), ("w_uv", 1), ("w_out0", 4),
          ("up0", 2 * (UT1 // 2)), ("down0", 12),
          ("b_in", 10), ("w_out1", 4), ("up1", 2 * (UT1 // 2)), ("down1", 12),
          ("moba_qk", 8), ("moba_v", 4), ("w_o0", 4), ("up2", 16), ("down2", 16),
          ("fox_k", 4), ("fox_v", 4), ("fox_q", 4), ("w_o1", 4), ("up3", 16), ("down3", 16)]
FIRST = {}
_n = 0
for _name, _count in STAGES:
    FIRST[_name] = _n
    _n += _count
NCH = _n
LAYERS = [("w_out0", "up0", "down0"), ("w_out1", "up1", "down1"),
          ("w_o0", "up2", "down2"), ("w_o1", "up3", "down3")]
NADA = 24
ADA1 = 8

COLS = [("norm1", 2 * KT), ("norm2", 2 * KT), ("ada_b", 2 * ADA), ("q_ln", CQ), ("kv_ln", CKV),
        ("q_norm", 1), ("k_norm", 1), ("conf_dw", 4 * CONV), ("conf_b", 4), ("ln_g", 4), ("ln_b", 4),
        ("sc_dw", 4 * SCONV), ("attn_norm", 2 * KT), ("kv_norm", KT), ("mlp_norm", 2 * KT),
        ("final", KT), ("b_f", H2), ("c", 2 * KT), ("w_f", KT * H2)]
COL = {}
_n = 0
for _name, _count in COLS:
    COL[_name] = _n
    _n += _count
NCOL = _n

CONSTS = [("ident", P), ("ones", P), ("dft_c", 2 * P), ("dft_n", 4 * T), ("rot", P), ("rope_c", T),
          ("rope_s", T), ("alibi", 3 * P), ("mask", 3 * P), ("tri", T), ("onehot", H2), ("eps", 1)]
CON = {}
_n = 0
for _name, _count in CONSTS:
    CON[_name] = _n
    _n += _count
NCON = _n
NEG = -1e30




def numbered(names):
    return {name: i + 1 for i, name in enumerate(names)}


def tiles(name, n=KT):
    return [f"{name}_{k}" for k in range(n)]


T_ORDER = tiles("n0") + tiles("ckv", CKV) + tiles("cq", CQ) + tiles("n1") + tiles("n2") + tiles("sc", 4) + tiles("n3") + tiles("n4") + tiles("n5") \
    + tiles("n6") + tiles("n6q") + tiles("n7")
TN = numbered(T_ORDER)
H_ORDER = tiles("n0") + tiles("ckv", CKV) + tiles("cq", CQ) \
    + [f"{k}_{g}" for g in range(4) for k in "yo"] + tiles("n1") + tiles("n2") + tiles("sc", 4) \
    + tiles("conf", 4) + tiles("n3") + tiles("n4") + tiles("o2") + tiles("n5") + tiles("n6") \
    + tiles("n6q") + tiles("o3") + tiles("n7")
HN = numbered(H_ORDER)
U0 = [0, UT1 // 2, UT1, UT1 + UT2 // 2]


class Use:
    def __init__(self, b, fill, chunk, before, drain):
        self.b, self.fill, self.chunk, self.before, self.drain = b, fill, chunk, before, drain


class Banks:

    def __init__(self):
        self.fills, self.drains, self.last, self.of = [0] * 8, [0] * 8, [None] * 8, {}

    def claim(self, name, b, chunk=None, drain=None, times=1):
        own = drain or ("drained", b, self.drains[b] + 1)
        self.of[name] = Use(b, self.fills[b] + 1, chunk, self.last[b], own)
        if drain is None:
            self.drains[b] += times
            self.last[b] = ("drained", b, self.drains[b])
        else:
            self.last[b] = drain
        if chunk is None:
            self.fills[b] += times


def plan():
    k = Banks()
    k.claim("ms_0", 4)
    k.claim("ada_a", 5, chunk=-1)
    c = FIRST["w_in"]
    t = lambda name: ("t_ready", None, TN[name])
    lo = lambda name: ("h_lo_s", None, HN[name])
    count = lambda sem, n: (sem, None, n)
    k.claim("ckv0", 0, None, t("ckv_0"))
    k.claim("ckv1", 1, c, t("ckv_1"))
    k.claim("kr", 2, None, count("krg_s", 3))
    k.claim("cq01", 3, None, t("cq_1"))
    k.claim("ms_kv", 4)
    k.claim("cq2", 6, c + 2, t("cq_2"))
    k.claim("krot", 4)
    k.claim("f01", 7, c + 3)
    k.claim("ms_cq", 4)
    k.claim("f23", 5, c + 4)
    for h in range(MLA_H):
        k.claim(f"k{h}", h % 4, FIRST["w_uk"] if h == MLA_H - 1 else None, count("kT_s", h + 1))
        k.claim(f"ms_k{h}", (4, 6)[h % 2])
    for j in range(MLA_H // 2):
        k.claim(f"q{j}", j, FIRST["w_uq"] + j // 2 if j % 2 else None, count("qsq_s", j + 1))
        k.claim(f"ms_q{j}", (4, 6)[j % 2])
        k.claim(f"qrot{j}", (5, 7)[j % 2])
    for n in range(4):
        k.claim(f"v0_{n}", n, FIRST["w_uv"] if n == 3 else None)
    k.claim("ada_b", 5, chunk=-1)
    for s in range(2 * MLA_H):
        k.claim(f"s0_{s}", s % 2, None, count("p_s", s + 1))
        k.claim(f"pT0_{s}", 2 + s % 2, None, count("pT_s", s + 1))
        if s % 4 == 0:
            k.claim(f"o0_{s // 4}", (4, 6)[s // 4 % 2], None, lo(f"o_{s // 4}"))
    for g in range(FG):
        k.claim(f"dft_a{g}", 7)
        k.claim(f"dft_y{g}", 7, None, lo(f"y_{g}"))
    for r, (mix, up, down) in enumerate(LAYERS):
        if r == 1:
            for n in range(4):
                k.claim(f"b_a{n}", n, FIRST["b_in"] + n)
            for n in range(4):
                k.claim(f"b_s{n}", n, FIRST["b_in"] + 4 + n)
            for n in range(2):
                k.claim(f"b_b{n}", n, FIRST["b_in"] + 8 + n, t(f"sc_{2 * n + 1}"))
            for n in range(4):
                k.claim(f"ms_conf{n}", 6, None, count("cen_s", n + 1))
                k.claim(f"var_conf{n}", 7)
        if r >= 2:
            base = 16 * (r - 1)
            for n in range(8 if r == 2 else 4):
                k.claim(f"qk{r}_{n}", n % 4, FIRST[("moba_qk", "fox_k")[r - 2]] + n)
            for n in range(4):
                k.claim(f"v{r}_{n}", n, FIRST[("moba_v", "fox_v")[r - 2]] + n)
            if r == 3:
                k.claim("z", 5)
                for n in range(4):
                    k.claim(f"qq_{n}", n, FIRST["fox_q"] + n)
                k.claim("cum_col", 5)
                k.claim("cum_row", 6)
            for h in range(H2):
                k.claim(f"s{r}_{h}", h % 2)
                k.claim(f"pT{r}_{h}", 2 + h % 2, None, count("pT_s", base + h + 1))
                if h % 2 == 0:
                    k.claim(f"o{r}_{h // 2}", (4, 6)[h // 2 % 2], None, lo(f"o{r}_{h // 2}"))
        for n in range(4):
            k.claim(f"{mix}_{n}", n, FIRST[mix] + n, count("res_ready", 8 * r + n + 1))
        k.claim(f"ms_{2 * r + 1}", 4)
        if r == 0:
            k.claim("ada_c", 5, chunk=-1)
        for b in range(4):
            k.claim(f"{up}_{b}", b, FIRST[up] + b, times=5 if r < 2 else 4)
        if r < 2:
            for b in range(2):
                k.claim(f"{up}_{4 + b}", b, FIRST[up] + 20 + b)
        for n in range(4):
            k.claim(f"{down}_{n}", n, FIRST[down] + (8 if r < 2 else 12) + n,
                    count("res_ready", 8 * r + 4 + n + 1))
        k.claim(f"ms_{2 * r + 2}", 4)
    return k.of


POOL_LO = (FIRST["b_in"], FIRST["w_out1"] + 4)


def program(nc, stream, ada_stream, xT_d, ctxT_d, cols_d, con_d, out):
    bank_use = plan()
    ctx = ExitStack()
    with ctx:
        def sb(name, shape, dt=F32, where=ctx):
            return where.enter_context(nc.sbuf_tensor(name, shape, dt))

        def sem(name):
            return ctx.enter_context(nc.semaphore(name))

        def scratch(*specs, where=None):
            s = ExitStack()
            made = [sb(*spec, where=s) for spec in specs]
            s.close() if where is None else where.callback(s.close)
            return made

        raw = sb("raw", [P, RAW, CH])
        w_hi = sb("w_hi", [P, SPL, CH], F32R)
        w_lo = sb("w_lo", [P, SPL, CH], F32R)
        ada_w = sb("ada_w", [P, AR, CH])
        x = sb("x", [P, KT, T])
        h_hi = sb("h_hi", [P, KT, T], F32R)
        h_lo = sb("h_lo", [P, KT, T], F32R)
        sq = sb("sq", [P, 2 * T])
        acc = sb("acc", [P, 2 * T])
        rstd = sb("rstd", [P, 2 * T])
        tmp = sb("tmp", [P, 3, 2 * T])
        cols = sb("cols", [P, NCOL])
        con = sb("con", [P, NCON])
        cs = sb("cs", [P, 2 * KT])
        ada = sb("ada", [P, 3, ADA])
        gain = sb("gain", [P, 2, KT])
        stat = sb("stat", [P, 4 * 2 * H2])

        u_hi, u_lo, silu_b, u_t = scratch(
            ("u_hi", [P, UT2, T], F32R), ("u_lo", [P, UT2, T], F32R),
            ("silu_b", [P, 2 * T]), ("u_t", [P, 2, 2 * T]))
        m0 = ExitStack()
        cq_hi, cq_lo, krg, kr, ksq, rs_b, qg, v0, uF, ab, acc_c = scratch(
            ("cq_hi", [P, CQ, T], F32R), ("cq_lo", [P, CQ, T], F32R), ("krg", [P, 2 * T]),
            ("kr", [P, 2 * T]), ("ksq", [P, 2, 2 * T]), ("rs_b", [P, 2, 2 * T]),
            ("qg", [P, 2, 2 * T]), ("v0", [P, 4, MLA_H * VH]), ("uF", [P, FG, T]),
            ("ab", [P, 2, TT, 2 * P]), ("acc_c", [P, 2 * T]), where=m0)
        ctxT, hc_hi, hc_lo = scratch(("ctxT", [P, KT, T]), ("hc_hi", [P, KT, T], F32R),
                                     ("hc_lo", [P, KT, T], F32R))
        qT, kT = scratch(("qT", [P, MLA_H, T]), ("kT", [P, MLA_H, 2 * T]), where=m0)
        ckv_hi, ckv_lo = scratch(("ckv_hi", [P, CKV, 2 * T], F32R), ("ckv_lo", [P, CKV, 2 * T], F32R))
        p0, pT0 = scratch(("p0", [P, 2, 2 * T]), ("pT0", [P, 2, 2 * T]), where=m0)
        m0.close()
        m_hi, m_lo, conf, cacc, scin, scacc, sig, cln = scratch(
            ("m_hi", [P, KT, T], F32R), ("m_lo", [P, KT, T], F32R),
            ("conf", [P, 4, T + 2 * PAD]), ("cacc", [P, 4, T]), ("scin", [P, 4, T + 2]),
            ("scacc", [P, 4, T]), ("sig", [P, 2, T]), ("cln", [P, 4, T]))
        h2_hi, h2_lo, q2, k2, v2, st, p2, pT2, crow, ccol, lf, wf_hi, wf_lo = scratch(
            ("h2_hi", [P, KT, T], F32R), ("h2_lo", [P, KT, T], F32R),
            ("q2", [P, KT, T]), ("k2", [P, KT, T]), ("v2", [P, TT, D]), ("st", [P, 2, 3 * P]),
            ("p2", [P, 2, 3 * P]), ("pT2", [P, 2, 3 * P]), ("crow", [P, T]), ("ccol", [P, TT * H2]),
            ("lf", [P, 3, TT * H2]), ("wf_hi", [P, KT * H2], F32R), ("wf_lo", [P, KT * H2], F32R))

        banks = [ctx.enter_context(nc.psum_tensor(f"bank{b}", [P, 2 * T], F32))[:, :] for b in range(8)]

        loaded = [sem(f"loaded{s}") for s in range(RAW)]
        ada_loaded = [sem(f"ada_loaded{s}") for s in range(AR)]
        cols_in, con_in, x_in, ctx_in = sem("cols_in"), sem("con_in"), sem("x_in"), sem("ctx_in")
        hi_ready = sem("hi_ready")
        lo_ready = sem("lo_ready")
        lo_pool = sem("lo_pool")
        chunk_used = sem("chunk_used")
        ada_used = sem("ada_used")
        filled = [sem(f"filled{b}") for b in range(8)]
        drained = [sem(f"drained{b}") for b in range(8)]
        cs_ready = sem("cs_ready")
        res_ready = sem("res_ready")
        sq_ready = sem("sq_ready")
        acc_ready = sem("acc_ready")
        t_ready = sem("t_ready")
        h_hi_s, h_lo_s = sem("h_hi_s"), sem("h_lo_s")
        ut_s = sem("ut_s")
        u_hi_s, u_lo_s = sem("u_hi_s"), sem("u_lo_s")
        a_own, v_own = sem("a_own"), sem("v_own")
        lat_sq = sem("lat_sq")
        krg_s = sem("krg_s")
        kr_s = sem("kr_s")
        ksq_s, qsq_s = sem("ksq_s"), sem("qsq_s")
        krs_s = sem("krs_s")
        kT_s, kTr_s = sem("kT_s"), sem("kTr_s")
        qT_s = sem("qT_s")
        nb_s = sem("nb_s")
        p_s = sem("p_s")
        pn_s = sem("pn_s")
        ri_s = sem("ri_s")
        pT_s = sem("pT_s")
        sig_s = sem("sig_s")
        conv_s = sem("conv_s")
        cen_s, csq_s = sem("cen_s"), sem("csq_s")
        cn_s, cact_s = sem("cn_s"), sem("cact_s")
        wf_s = sem("wf_s")
        lfa_s, lf_s = sem("lfa_s"), sem("lf_s")
        sent = sem("sent")

        signals = {"t_ready": t_ready, "h_lo_s": h_lo_s, "krg_s": krg_s, "kT_s": kT_s, "qsq_s": qsq_s,
                   "p_s": p_s, "pT_s": pT_s, "cen_s": cen_s, "res_ready": res_ready}

        def C(name, a=0, n=None):
            n = dict(CONSTS)[name] - a if n is None else n
            return con[:, CON[name] + a:CON[name] + a + n]

        def V(name, j, rows=slice(0, P)):
            return cols[rows, COL[name] + j:COL[name] + j + 1]

        def stat_(kind, i, n=1):
            return stat[:, kind * 2 * H2 + i:kind * 2 * H2 + i + n]

        def lo_done(eng, c, it=0):
            first, end = POOL_LO
            if first <= c < end:
                eng.wait_ge(lo_pool, c - first + 1 + 4 * it)
            else:
                eng.wait_ge(lo_ready, c + 1 - (end - first if c >= end else 0) + 4 * it)

        block = ctx.enter_context(nc.Block())

        def wait_full(eng, name, it=0):
            use = bank_use[name]
            if use.chunk is None:
                eng.wait_ge(filled[use.b], use.fill + it)
            else:
                eng.wait_ge(chunk_used, use.chunk + 1 + 4 * it)
            return banks[use.b]

        def wait_drain(eng, drain, it=0):
            name, b, n = drain
            eng.wait_ge(drained[b] if b is not None else signals[name], n + it)

        def wait_drained(eng, name, it=0):
            wait_drain(eng, bank_use[name].drain, it)

        def drain_of(name):
            sem_name, b, _ = bank_use[name].drain
            return drained[b] if b is not None else signals[sem_name]

        @block.sync
        def _(sp):
            sp.dma_start(cols[:, :], cols_d).then_inc(cols_in, 16)
            sp.dma_start(x[:, :, :], xT_d).then_inc(x_in, 16)
            sp.dma_start(ctxT[:, :, :], ctxT_d).then_inc(ctx_in, 16)

            def load_ada(a, it=0):
                if a >= AR:
                    sp.wait_ge(ada_used, a - AR + 1 + 4 * it)
                sp.dma_start(ada_w[:, a % AR, :], ada_stream[ds(a + 4 * it, 1), :, :]
                             .rearrange("o p n -> p (o n)")).then_inc(ada_loaded[a % AR], 16)

            def load(c, it=0):
                if c >= RAW:
                    lo_done(sp, c - RAW, it)
                sp.dma_start(raw[:, c % RAW, :], stream[ds(c + 4 * it, 1), :, :]
                             .rearrange("o p n -> p (o n)")).then_inc(loaded[c % RAW], 16)

            load_ada(0)
            load_ada(1)
            sp.dma_start(con[:, :], con_d).then_inc(con_in, 16)
            for a in range(AR, ADA1):
                load_ada(a)
            for c in range(FIRST["up0"]):
                load(c)
            for a in range(ADA1, NADA):
                load_ada(a)
            c0 = FIRST["up0"]
            with sp.Fori(0, 5) as i:
                for j in range(4):
                    load(c0 + j, i)
                    load_ada(NADA + j, i)
            for j in range(4):
                load(c0 + 20 + j)
                load_ada(NADA + 20 + j)
            c = c0 + 24
            for end in (POOL_LO[0] + RAW, POOL_LO[1] + RAW, NCH):
                steps = (end - c) // RAW
                with sp.Fori(0, steps) as i:
                    for j in range(RAW):
                        load(c + j, i)
                for c in range(c + RAW * steps, end):
                    load(c)
                c = end
            for k in range(KT):
                sp.wait_ge(res_ready, 32 + k + 1)
                sp.dma_start(out[k, :, :], x[:, k, :]).then_inc(sent, 16)
            sp.wait_ge(sent, 16 * KT)

        @block.tensor
        def _(pe):
            def fill(name):
                use = bank_use[name]
                if use.before is not None:
                    wait_drain(pe, use.before)
                return banks[use.b]

            def refill(name, it):
                use = bank_use[name]
                pe.wait_ge(drained[use.b], use.drain[2] - 1 + it)
                return banks[use.b]

            def full(ins, name):
                assert bank_use[name].chunk is None
                ins.then_inc(filled[bank_use[name].b], 1)

            def product(dst, whi, wlo, xhi, xlo, c, kts, need=None, it=0, start=True):
                pe.wait_ge(hi_ready, c + 1 + 4 * it)
                for i, k in enumerate(kts):
                    if need is not None:
                        need(k)
                    pe.matmul(dst, whi(k), xhi(k), start=start and i == 0, stop=False,
                              skip_group_check=True)
                    pe.matmul(dst, whi(k), xlo(k), start=False, stop=False, skip_group_check=True)
                lo_done(pe, c, it)
                for k in kts:
                    last = pe.matmul(dst, wlo(k), xhi(k), start=False, stop=k == kts[-1],
                                     skip_group_check=True)
                return last

            def wtile(c, j, width=2 * P):
                return [(lambda k, b=b: b[:, c % SPL, k * width + j * P:k * width + (j + 1) * P])
                        for b in (w_hi, w_lo)]

            def split_need(name):
                def need(k):
                    pe.wait_ge(h_hi_s, HN[f"{name}_{k}"])
                    pe.wait_ge(h_lo_s, HN[f"{name}_{k}"])
                return need

            hh = (lambda k: h_hi[:, k, :], lambda k: h_lo[:, k, :])
            hc = (lambda k: hc_hi[:, k, :], lambda k: hc_lo[:, k, :])
            hm = (lambda k: m_hi[:, k, :], lambda k: m_lo[:, k, :])
            hq = (lambda k: h2_hi[:, k, :], lambda k: h2_lo[:, k, :])

            def two_tiles(c, name, need, operand=hh, it=None):
                dst = fill(name) if it is None else refill(name, it)
                it = 0 if it is None else it
                for j in range(2):
                    last = product(dst[:, j * T:(j + 1) * T], *wtile(c, j), *operand, c, range(KT),
                                   need, it)
                last.then_inc(chunk_used, 1)

            def modulation(a, dst, n, it=0):
                pe.wait_ge(ada_loaded[a % AR], 16 * (a // AR + 1) + 32 * it)
                for j in range(2):
                    for k in range(KT):
                        last = pe.matmul(dst(j), ada_w[:, a % AR, (2 * k + j) * P:(2 * k + j + 1) * P],
                                         cs[:, 2 * k:2 * k + n], start=k == 0, stop=k == KT - 1,
                                         skip_group_check=True)
                last.then_inc(ada_used, 1)

            def mean_square(name, *parts):
                dst = fill(name)
                for where, srcs in parts:
                    rows = srcs[0].shape[0]
                    for i, src in enumerate(srcs):
                        last = pe.matmul(dst[0:rows, where], C("ones")[0:rows, 0:rows], src,
                                         start=i == 0, stop=i == len(srcs) - 1, skip_group_check=True)
                full(last, name)

            halves = lambda a: [a[:, 0:T], a[:, T:2 * T]]

            def norm(r):
                pe.wait_ge(acc_ready, 3 * r + 6)
                mean_square(f"ms_{r}", (slice(0, T), halves(acc)))

            pe.wait_ge(cs_ready, 1)
            pair = banks[5][:, 0:2 * ADA].rearrange("p (v t) -> p t v", v=2)
            for a in range(ADA1):
                if a == 4:
                    pe.wait_ge(con_in, 16)
                    pe.wait_ge(acc_ready, 6)
                    mean_square("ms_0", (slice(0, T), halves(acc_c)), (slice(T, 2 * T), halves(acc)))
                modulation(a, lambda j: pair[:, 2 * a + j, :], 2)

            need = split_need("n0")
            c = FIRST["w_in"]

            def ctx_and_x(c, j, name):
                dst = fill(name)
                for half, op in ((0, hc), (1, hh)):
                    last = product(dst[:, half * T:(half + 1) * T], *wtile(c, j), *op, c, range(KT), need)
                return last

            full(ctx_and_x(c, 0, "ckv0"), "ckv0")
            ctx_and_x(c, 1, "ckv1").then_inc(chunk_used, 1)
            full(ctx_and_x(c + 1, 0, "kr"), "kr")
            cq = fill("cq01")
            product(cq[:, 0:T], *wtile(c + 1, 1), *hh, c + 1, range(KT)).then_inc(chunk_used, 1)
            pe.wait_ge(lat_sq, CKV)
            mean_square("ms_kv", (slice(0, 2 * T), [qg[:, 0, :], qg[:, 1, :]]))
            full(product(cq[:, T:2 * T], *wtile(c + 2, 0), *hh, c + 2, range(KT)), "cq01")
            product(fill("cq2")[:, 0:T], *wtile(c + 2, 1), *hh, c + 2, range(KT)).then_inc(chunk_used, 1)
            pe.wait_ge(krg_s, 1)
            full(pe.matmul(fill("krot")[0:QKH, 0:T], C("rot")[NOPE:QKH, 0:QKH], krg[NOPE:QKH, T:2 * T],
                           start=True, stop=True), "krot")
            two_tiles(c + 3, "f01", None)
            pe.wait_ge(lat_sq, CKV + 2)
            mean_square("ms_cq", (slice(0, T), [qg[:, 0, 0:T], qg[:, 0, T:2 * T], qg[:, 1, 0:T]]))
            two_tiles(c + 4, "f23", None)

            c = FIRST["w_uk"]
            ckv = (lambda k: ckv_hi[:, k, :], lambda k: ckv_lo[:, k, :])

            def key_square(h):
                pe.wait_ge(ksq_s, h + 1)
                mean_square(f"ms_k{h}", (slice(0, 2 * T), [ksq[0:QKH, h % 2, :]]))

            for h in range(MLA_H):
                last = product(fill(f"k{h}"), *wtile(c, h, MLA_H * P), *ckv, c, range(CKV),
                               split_need("ckv"))
                if h < MLA_H - 1:
                    full(last, f"k{h}")
                else:
                    last.then_inc(chunk_used, 1)
                if h == 0:
                    pe.wait_ge(krg_s, 3)
                else:
                    key_square(h - 1)
            key_square(MLA_H - 1)

            cqx = (lambda k: cq_hi[:, k, :], lambda k: cq_lo[:, k, :])

            def query_square(j):
                pe.wait_ge(qsq_s, j + 1)
                mean_square(f"ms_q{j}", (slice(0, 2 * T), [ksq[0:QKH, j % 2, :]]))
                full(pe.matmul(fill(f"qrot{j}")[0:QKH, :], C("rot")[0:QKH, 0:QKH], qg[0:QKH, j % 2, :],
                               start=True, stop=True), f"qrot{j}")

            for j in range(MLA_H // 2):
                c = FIRST["w_uq"] + j // 2
                dst = fill(f"q{j}")
                for i in range(2):
                    last = product(dst[:, i * T:(i + 1) * T], *wtile(c, 2 * (j % 2) + i, 4 * P), *cqx, c,
                                   range(CQ), split_need("cq"))
                if j % 2:
                    last.then_inc(chunk_used, 1)
                else:
                    full(last, f"q{j}")
                if j:
                    query_square(j - 1)
            query_square(MLA_H // 2 - 1)

            def values(dst, c, width, xs, t, kts, it=0):
                pe.wait_ge(hi_ready, c + 1 + 4 * it)
                lo_done(pe, c, it)
                n = 0
                for k in kts:
                    xhi, xlo = (f(k)[:, t * P:(t + 1) * P] for f in xs)
                    whi, wlo = (b[:, c % SPL, k * width:(k + 1) * width] for b in (w_hi, w_lo))
                    for a, b in ((xhi, whi), (xhi, wlo), (xlo, whi)):
                        n += 1
                        last = pe.matmul(dst, a, b, start=n == 1, stop=n == 3 * len(kts),
                                         skip_group_check=True)
                return last

            c = FIRST["w_uv"]
            for t in range(4):
                last = values(fill(f"v0_{t}"), c, MLA_H * VH, ckv, t, range(CKV))
                if t < 3:
                    full(last, f"v0_{t}")
                else:
                    last.then_inc(chunk_used, 1)

            mod_b = fill("ada_b")

            def score0(s):
                h, t = divmod(s, 2)
                pe.wait_ge(kT_s, h + 1)
                pe.wait_ge(kTr_s, h + 1)
                pe.wait_ge(qT_s, h // 2 + 1)
                full(pe.matmul(fill(f"s0_{s}"), qT[0:QKH, h, t * P:(t + 1) * P], kT[0:QKH, h, :],
                               start=True, stop=True), f"s0_{s}")

            def weigh0(s):
                h, t = divmod(s, 2)
                name = f"o0_{s // 4}"
                dst = banks[bank_use[name].b] if s % 4 else fill(name)
                pe.wait_ge(pT_s, s + 1)
                if s == 0:
                    for n in range(4):
                        wait_drained(pe, f"v0_{n}")
                rows = slice(VH * (h % 2), VH * (h % 2) + VH)
                for k in range(4):
                    last = pe.matmul(dst[rows, t * P:(t + 1) * P], v0[:, k, h * VH:(h + 1) * VH],
                                     pT0[:, s % 2, k * P:(k + 1) * P], start=k == 0, stop=k == 3,
                                     skip_group_check=True)
                if s % 4 == 3:
                    full(last, name)

            def fourier(g, step):
                if step == 0:
                    wait_drained(pe, ("f01", "f23")[g // 2])
                    dst = fill(f"dft_a{g}")
                    for t in range(TT):
                        last = pe.matmul(dst[:, t * T:(t + 1) * T], uF[:, g, t * P:(t + 1) * P],
                                         C("dft_c"), start=True, stop=True, skip_group_check=True)
                    full(last, f"dft_a{g}")
                else:
                    wait_drained(pe, f"dft_a{g}")
                    dst = fill(f"dft_y{g}")
                    for n, (t, part) in enumerate((t, part) for t in range(TT) for part in range(2)):
                        last = pe.matmul(dst[:, 0:T], ab[:, g % 2, t, part * P:(part + 1) * P],
                                         C("dft_n", (2 * part + t) * T, T), start=n == 0, stop=n == 3,
                                         skip_group_check=True)
                    full(last, f"dft_y{g}")

            steps = 2 * MLA_H
            score0(0)
            score0(1)
            for s in range(steps + 1):
                if s < steps:
                    a = ADA1 + s
                    modulation(a, lambda j: mod_b[:, 2 * a + j:2 * a + j + 1], 1)
                    if s % 4 < 2:
                        fourier(s // 4, s % 4)
                    dst = fill(f"pT0_{s}")
                    pe.wait_ge(pn_s, s + 1)
                    for k in range(4):
                        last = pe.transpose(dst[:, k * P:(k + 1) * P], p0[:, s % 2, k * P:(k + 1) * P],
                                            C("ident"))
                    full(last, f"pT0_{s}")
                if s + 2 < steps:
                    score0(s + 2)
                if s:
                    weigh0(s - 1)

            def mixer_order(k):
                pe.wait_ge(h_hi_s, HN[f"o_{k}" if k < 4 else f"y_{k - 4}"])
                pe.wait_ge(h_lo_s, HN[f"o_{k}" if k < 4 else f"y_{k - 4}"])

            for n in range(4):
                two_tiles(FIRST["w_out0"] + n, f"w_out0_{n}", mixer_order)

            def ffn(r):
                _, up, down = LAYERS[r]
                c = FIRST[up]
                need = split_need(f"n{2 * r + 1}")
                rounds = 5 if r < 2 else 4
                if r == 0:
                    mod_c = fill("ada_c")
                for j in range(4):
                    fill(f"{up}_{j}")
                with pe.Fori(0, rounds) as i:
                    for j in range(4):
                        two_tiles(c + j, f"{up}_{j}", need, it=i)
                        if r == 0:
                            modulation(NADA + j, lambda q: mod_c[:, ds(8 * i + (2 * j + q), 1)], 1, i)
                if r < 2:
                    for j in range(2):
                        two_tiles(c + 20 + j, f"{up}_{4 + j}", need)
                    if r == 0:
                        for j in range(4):
                            modulation(NADA + 20 + j, lambda q: mod_c[:, 40 + 2 * j + q:41 + 2 * j + q], 1)

                c = FIRST[down]
                base = U0[r]

                def depth(kg, n_k, g=None):
                    first = isinstance(kg, int) and kg == 0
                    it = 0 if isinstance(kg, int) and g is None else g
                    for n in range(4):
                        cc = c + n + (4 * kg if isinstance(kg, int) else 4)
                        dst = fill(f"{down}_{n}") if first else banks[n]
                        pe.wait_ge(hi_ready, cc + 1 + 4 * it)
                        if n == 0:
                            pairs = 4 * kg + n_k // 2 if isinstance(kg, int) else 8 + 4 * it
                            pe.wait_ge(u_hi_s, base + pairs)
                            pe.wait_ge(u_lo_s, base + pairs)
                        for part in range(2):
                            if part:
                                lo_done(pe, cc, it)
                            for j in range(2):
                                whi, wlo = wtile(cc, j)
                                out_ = dst[:, j * T:(j + 1) * T]
                                for k in range(n_k):
                                    if isinstance(kg, int):
                                        hi, lo = u_hi[:, 8 * kg + k, :], u_lo[:, 8 * kg + k, :]
                                    else:
                                        hi, lo = (u[:, ds(8 + k + 8 * it, 1), :]
                                                  .rearrange("p o t -> p (o t)") for u in (u_hi, u_lo))
                                    fresh = first and not part and j == 0 and k == 0
                                    if part == 0:
                                        pe.matmul(out_, whi(k), hi, start=fresh, stop=False,
                                                  skip_group_check=True)
                                        pe.matmul(out_, whi(k), lo, start=False, stop=False,
                                                  skip_group_check=True)
                                    else:
                                        last = pe.matmul(out_, wlo(k), hi, start=False, stop=True,
                                                         skip_group_check=True)
                        last.then_inc(chunk_used, 1)

                depth(0, 8)
                if r < 2:
                    depth(1, 8)
                    depth(2, UT1 - 16)
                else:
                    with pe.Fori(0, 3) as g:
                        depth(None, 8, g)

            norm(1)
            ffn(0)

            norm(2)
            need = split_need("n2")

            def group_norm(n):
                pe.wait_ge(conv_s, n + 1)
                mean_square(f"ms_conf{n}", (slice(0, T), [cacc[:, n, :]]))
                pe.wait_ge(csq_s, n + 1)
                mean_square(f"var_conf{n}", (slice(0, T), [sig[:, n % 2, :]]))

            c = FIRST["b_in"]
            for n in range(4):
                two_tiles(c + n, f"b_a{n}", need)
            for n in range(4):
                two_tiles(c + 4 + n, f"b_s{n}", need)
            for n in range(2):
                two_tiles(c + 8 + n, f"b_b{n}", need)
            for n in range(4):
                group_norm(n)

            def mixer1_order(k):
                pe.wait_ge(h_hi_s, HN[f"conf_{k}" if k < 4 else f"sc_{k - 4}"])
                pe.wait_ge(h_lo_s, HN[f"conf_{k}" if k < 4 else f"sc_{k - 4}"])

            for n in range(4):
                two_tiles(FIRST["w_out1"] + n, f"w_out1_{n}", mixer1_order, hm)
            norm(3)
            ffn(1)

            def attention(r):
                base = 16 * (r - 1)

                def score(h):
                    rows = slice(HD * (h % 2), HD * (h % 2) + HD)
                    dst = fill(f"s{r}_{h}")
                    for t, (a, n) in enumerate(((0, P), (P, 2 * P))):
                        last = pe.matmul(dst[:, a:a + n], q2[rows, h // 2, t * P:(t + 1) * P],
                                         k2[rows, h // 2, 0:n], start=True, stop=r == 2,
                                         skip_group_check=True)
                        if r == 3:
                            last = pe.matmul(dst[:, a:a + n],
                                             C("onehot", h, 1)[0:H2, :].to_broadcast([H2, P]),
                                             crow[0:H2, 0:n], start=False, stop=True,
                                             skip_group_check=True)
                    full(last, f"s{r}_{h}")

                def weigh(h):
                    name = f"o{r}_{h // 2}"
                    dst = banks[bank_use[name].b] if h % 2 else fill(name)
                    pe.wait_ge(pT_s, base + h + 1)
                    rows = slice(HD * (h % 2), HD * (h % 2) + HD)
                    pe.matmul(dst[rows, 0:T], v2[:, 0, h * HD:(h + 1) * HD], pT2[:, h % 2, 0:T],
                              start=True, stop=False, skip_group_check=True)
                    last = pe.matmul(dst[rows, P:T], v2[:, 1, h * HD:(h + 1) * HD],
                                     pT2[:, h % 2, T:3 * P], start=False, stop=True,
                                     skip_group_check=True)
                    if h % 2:
                        full(last, name)

                score(0)
                score(1)
                for h in range(H2 + 1):
                    if h < H2:
                        dst = fill(f"pT{r}_{h}")
                        pe.wait_ge(pn_s, base + h + 1)
                        for k in range(3):
                            last = pe.transpose(dst[:, k * P:(k + 1) * P],
                                                p2[:, h % 2, k * P:(k + 1) * P], C("ident"))
                        full(last, f"pT{r}_{h}")
                    if h + 2 < H2:
                        score(h + 2)
                    if h:
                        weigh(h - 1)

            norm(4)
            need = split_need("n4")
            for n in range(8):
                two_tiles(FIRST["moba_qk"] + n, f"qk2_{n}", need)

            def value_blocks(r):
                for n in range(4):
                    c = FIRST[("moba_v", "fox_v")[r - 2]] + n
                    dst = fill(f"v{r}_{n}")
                    for t in range(TT):
                        last = values(dst[:, t * T:(t + 1) * T], c, 2 * P, hh, t, range(KT))
                    last.then_inc(chunk_used, 1)

            value_blocks(2)
            for n in range(4):
                for name in (f"qk2_{n}", f"qk2_{n + 4}", f"v2_{n}"):
                    wait_drained(pe, name)
            attention(2)
            need = split_need("o2")
            for n in range(4):
                two_tiles(FIRST["w_o0"] + n, f"w_o0_{n}", need)
            norm(5)
            ffn(2)

            norm(6)
            need = split_need("n6")
            for n in range(4):
                two_tiles(FIRST["fox_k"] + n, f"qk3_{n}", need)
            value_blocks(3)
            pe.wait_ge(wf_s, 2)
            dst = fill("z")
            for t in range(TT):
                n = 0
                for k in range(KT):
                    xhi, xlo = (b[:, k, t * P:(t + 1) * P] for b in (h_hi, h_lo))
                    whi, wlo = (b[:, k * H2:(k + 1) * H2] for b in (wf_hi, wf_lo))
                    for a, b in ((xhi, whi), (xhi, wlo), (xlo, whi)):
                        n += 1
                        last = pe.matmul(dst[:, t * H2:(t + 1) * H2], a, b, start=n == 1,
                                         stop=n == 3 * KT, skip_group_check=True)
            full(last, "z")
            need = split_need("n6q")
            for n in range(4):
                two_tiles(FIRST["fox_q"] + n, f"qq_{n}", need, hq)
            pe.wait_ge(lf_s, 1)
            dst = fill("cum_col")
            lf0, lf1 = lf[:, 0, 0:H2], lf[:, 0, H2:2 * H2]
            pe.matmul(dst[:, 0:H2], C("tri", 0, P), lf0, start=True, stop=True, skip_group_check=True)
            pe.matmul(dst[:, H2:2 * H2], C("tri", P, P), lf0, start=True, stop=False,
                      skip_group_check=True)
            full(pe.matmul(dst[:, H2:2 * H2], C("tri", 0, P), lf1, start=False, stop=True,
                           skip_group_check=True), "cum_col")
            dst = fill("cum_row")
            pe.matmul(dst[0:H2, 0:T], lf0, C("tri"), start=True, stop=False, skip_group_check=True)
            full(pe.matmul(dst[0:H2, P:T], lf1, C("tri", 0, P), start=False, stop=True,
                           skip_group_check=True), "cum_row")
            for n in range(4):
                for name in (f"qk3_{n}", f"v3_{n}", f"qq_{n}"):
                    wait_drained(pe, name)
            wait_drained(pe, "cum_row")
            attention(3)
            need = split_need("o3")
            for n in range(4):
                two_tiles(FIRST["w_o1"] + n, f"w_o1_{n}", need)
            norm(7)
            ffn(3)
            norm(8)

        @block.scalar
        def _(act):
            def split_hi(c, it=0):
                act.wait_ge(loaded[c % RAW], 16 * (c // RAW + 1) + 16 * it)
                if c >= SPL:
                    act.wait_ge(chunk_used, c - SPL + 1 + 4 * it)
                act.copy(w_hi[:, c % SPL, :], raw[:, c % RAW, :]).then_inc(hi_ready, 1)

            def split_after(c, it=0):
                if c + SPL < NCH:
                    split_hi(c + SPL, it)

            def squares(src, q, n, total):
                if q >= 2:
                    act.wait_ge(res_ready, 4 * (q - 2) + n + 1)
                if n == 0 and q >= 2:
                    wait_full(act, f"ms_{q - 2}")
                if 3 * q + n > 1 and n:
                    act.wait_ge(acc_ready, 3 * q + n - 1)
                act.activation(total[:, :] if n == 0 else sq[:, :],
                               src[:, 2 * n:2 * n + 2, :].rearrange("p a t -> p (a t)"),
                               ACT.Square).then_inc(sq_ready, 1)

            def root(name, dst, width, count):
                src = wait_full(act, name)
                rows = dst.shape[0]
                act.activation(dst, src[0:rows, 0:width], ACT.Sqrt, bias=C("eps")[0:rows, :],
                               scale=1.0 / count).then_inc(drain_of(name), 1)

            def hi_of(name, dst, src, shift=None):
                act.wait_ge(t_ready, TN[name])
                if shift is None:
                    act.copy(dst, src).then_inc(h_hi_s, 1)
                else:
                    act.activation(dst, src, ACT.Identity, bias=shift).then_inc(h_hi_s, 1)

            def norm_tiles(r, shift=None, name=None, hi=None):
                name, hi = name or f"n{r}", h_hi if hi is None else hi
                for k in range(KT):
                    hi_of(f"{name}_{k}", hi[:, k, :], tmp[:, k % 3, 0:T],
                          None if shift is None else shift(k))

            def norm(r, shift=None):
                root(f"ms_{r}", rstd[:, 0:T], T, D)
                norm_tiles(r, shift)

            act.wait_ge(cols_in, 16)
            act.activation(cs[:, :], cols[:, COL["c"]:COL["c"] + 2 * KT], ACT.Silu).then_inc(cs_ready, 1)
            act.wait_ge(ctx_in, 16)
            for n in range(4):
                squares(ctxT, 0, n, acc_c)
            act.wait_ge(x_in, 16)
            for n in range(4):
                squares(x, 1, n, acc)
            split_hi(0)
            split_hi(1)
            act.wait_ge(con_in, 16)
            root("ms_0", rstd[:, :], 2 * T, D)
            wait_drained(act, "ada_a")
            for k in range(KT):
                act.wait_ge(t_ready, TN[f"n0_{k}"])
                act.activation(hc_hi[:, k, :], tmp[:, k % 3, 0:T], ACT.Identity, bias=ada[:, 1, k:k + 1])
                act.activation(h_hi[:, k, :], tmp[:, k % 3, T:2 * T], ACT.Identity,
                               bias=ada[:, 0, k:k + 1]).then_inc(h_hi_s, 1)

            c = FIRST["w_in"]
            for j in range(CKV):
                src = wait_full(act, f"ckv{j}")
                act.activation(qg[:, j, :], src[:, :], ACT.Square).then_inc(lat_sq, 1)
            split_after(c)
            rope = slice(NOPE, QKH)
            src = wait_full(act, "kr")
            act.activation(krg[rope, :], src[rope, :], ACT.Identity,
                           scale=V("k_norm", 0, rope)).then_inc(krg_s, 1)
            for i in range(2):
                act.activation(ksq[rope, i, :], src[rope, :], ACT.Square).then_inc(krg_s, 1)
            split_after(c + 1)
            root("ms_kv", rstd[:, :], 2 * T, CKV * P)
            for j in range(CKV):
                hi_of(f"ckv_{j}", ckv_hi[:, j, :], tmp[:, j, :])
            src = wait_full(act, "cq01")
            act.activation(qg[:, 0, :], src[:, :], ACT.Square).then_inc(lat_sq, 1)
            src = wait_full(act, "cq2")
            act.activation(qg[:, 1, 0:T], src[:, 0:T], ACT.Square).then_inc(lat_sq, 1)
            split_after(c + 2)

            def fourier_input(name, g):
                src = wait_full(act, name)
                act.copy(uF[:, g:g + 2, :].rearrange("p g t -> p (g t)"), src[:, :])\
                   .then_inc(drain_of(name), 1)

            fourier_input("f01", 0)
            split_after(c + 3)
            root("ms_cq", rstd[:, 0:T], T, CQ * P)
            for j in range(CQ):
                hi_of(f"cq_{j}", cq_hi[:, j, :], tmp[:, j, 0:T])
            fourier_input("f23", 2)
            split_after(c + 4)

            def key_root(h):
                if h >= 2:
                    act.wait_ge(kT_s, h - 1)
                    act.wait_ge(kTr_s, h - 1)
                root(f"ms_k{h}", rs_b[0:QKH, h % 2, :], 2 * T, QKH)

            for h in range(MLA_H):
                src = wait_full(act, f"k{h}")
                if h >= 2:
                    wait_full(act, f"ms_k{h - 2}")
                act.activation(ksq[0:NOPE, h % 2, :], src[0:NOPE, :], ACT.Square).then_inc(ksq_s, 1)
                if h:
                    key_root(h - 1)
            key_root(MLA_H - 1)
            split_after(FIRST["w_uk"])

            def query_root(j):
                if j >= 2:
                    act.wait_ge(qT_s, j - 1)
                else:
                    act.wait_ge(kT_s, MLA_H - 1 + j)
                    act.wait_ge(kTr_s, MLA_H - 1 + j)
                root(f"ms_q{j}", rs_b[0:QKH, j % 2, :], 2 * T, QKH)

            for j in range(MLA_H // 2):
                src = wait_full(act, f"q{j}")
                if j >= 2:
                    act.wait_ge(qT_s, j - 1)
                act.activation(qg[0:QKH, j % 2, :], src[0:QKH, :], ACT.Identity,
                               scale=V("q_norm", 0, slice(0, QKH)))
                wait_full(act, f"ms_q{j - 2}" if j >= 2 else f"ms_k{MLA_H - 2 + j}")
                act.activation(ksq[0:QKH, j % 2, :], src[0:QKH, :], ACT.Square).then_inc(qsq_s, 1)
                if j:
                    query_root(j - 1)
                if j % 2:
                    split_after(FIRST["w_uq"] + j // 2)
            query_root(MLA_H // 2 - 1)

            for t in range(4):
                src = wait_full(act, f"v0_{t}")
                act.copy(v0[:, t, :], src[:, :]).then_inc(drain_of(f"v0_{t}"), 1)
            split_after(FIRST["w_uv"])

            def hi_from(name, dst, bank_name):
                src = wait_full(act, bank_name)
                act.copy(dst, src[:, 0:T]).then_inc(h_hi_s, 1)

            S0 = float(QKH) ** -0.5
            steps = 2 * MLA_H
            for s in range(steps + 2):
                if s < steps:
                    act.wait_ge(nb_s, s + 1)
                    if s >= 2:
                        wait_full(act, f"pT0_{s - 2}")
                    src = wait_full(act, f"s0_{s}")
                    act.activation(p0[:, s % 2, :], src[:, :], ACT.Exp, bias=stat_(1, s), scale=S0,
                                   accum_out=stat_(2, s)).then_inc(p_s, 1)
                if s and s <= steps:
                    src = wait_full(act, f"pT0_{s - 1}")
                    act.copy(pT0[:, (s - 1) % 2, :], src[:, :]).then_inc(pT_s, 1)
                g = s // 4
                if s % 4 == 0 and g < FG:
                    src = wait_full(act, f"dft_a{g}")
                    act.copy(ab[:, g % 2, :, :].rearrange("p t c -> p (t c)"), src[:, :])\
                       .then_inc(drain_of(f"dft_a{g}"), 1)
                if s % 4 == 1:
                    if g:
                        hi_from(f"o_{g - 1}", h_hi[:, g - 1, :], f"o0_{g - 1}")
                    if g < FG:
                        hi_from(f"y_{g}", h_hi[:, 4 + g, :], f"dft_y{g}")

            def residual(stage, c):
                for n in range(4):
                    squares(x, stage + 2, n, acc)
                    if n < 3:
                        split_after(c + n)

            def ffn(r):
                _, up, down = LAYERS[r]
                c = FIRST[up]

                def pair_hi(j, pair, it):
                    if r < 2:
                        wait_drained(act, f"{up}_{j}", it)
                    else:
                        act.wait_ge(ut_s, 16 * (r - 2) + j + 1 + 4 * it)
                    act.copy(u_hi[:, pair, :], u_t[:, (j // 2 if r < 2 else j) % 2, :]
                             .rearrange("p (a t) -> p a t", a=2)).then_inc(u_hi_s, 1)

                def step(j, cc, it, pair):
                    if r < 2:
                        if j % 2 == 0:
                            src = wait_full(act, f"{up}_{j}", it)
                            act.activation(silu_b[:, :], src[:, :], ACT.Silu)\
                               .then_inc(drain_of(f"{up}_{j}"), 1)
                            split_after(cc, it)
                        else:
                            split_after(cc, it)
                            pair_hi(j, pair, it)
                    else:
                        src = wait_full(act, f"{up}_{j}", it)
                        act.activation(silu_b[:, :], src[:, :], ACT.Relu)\
                           .then_inc(drain_of(f"{up}_{j}"), 1)
                        split_after(cc, it)
                        pair_hi(j, pair, it)

                act.preload_act_table(ACT.Silu if r < 2 else ACT.Relu)
                with act.Fori(0, 5 if r < 2 else 4) as i:
                    for j in range(4):
                        step(j, c + j, i, ds(4 * i + 2 * (j // 2), 2) if r < 2 else ds(8 * i + 2 * j, 2))
                if r < 2:
                    for j in range(2):
                        step(4 + j, c + 20 + j, 0, slice(20, 22))
                c = FIRST[down]
                if r < 2:
                    for kc in range(8):
                        split_after(c + kc)
                    residual(2 * r + 1, c + 8)
                else:
                    with act.Fori(0, 3) as i:
                        for n in range(4):
                            split_after(c + n, i)
                    residual(2 * r + 1, c + 12)

            residual(0, FIRST["w_out0"])
            norm(1, lambda k: ada[:, 0, 3 * KT + k:3 * KT + k + 1])
            split_after(FIRST["w_out0"] + 3)
            ffn(0)

            wait_drained(act, "ada_c")
            norm(2, lambda k: ada[:, 2, k:k + 1])
            split_after(FIRST["down0"] + 11)
            c = FIRST["b_in"]
            for n in range(8):
                name = f"b_a{n}" if n < 4 else f"b_s{n - 4}"
                src = wait_full(act, name)
                if n >= 2:
                    wait_drained(act, f"b_a{n - 2}" if n < 6 else f"b_s{n - 6}")
                if n < 4:
                    act.activation(sig[:, n % 2, :], src[:, T:2 * T], ACT.Sigmoid).then_inc(sig_s, 1)
                else:
                    act.copy(sig[:, n % 2, :], src[:, T:2 * T]).then_inc(sig_s, 1)
                split_after(c + n)
            for n in range(4):
                hi_of(f"sc_{n}", m_hi[:, 4 + n, :], tmp[:, n % 3, 0:T])
                if n % 2:
                    split_after(c + 8 + n // 2)
            for n in range(5):
                if n < 4:
                    act.wait_ge(cen_s, n + 1)
                    if n >= 2:
                        wait_full(act, f"var_conf{n - 2}")
                    else:
                        wait_drained(act, f"b_s{n + 2}")
                    act.activation(sig[:, n % 2, :], cln[:, n, :], ACT.Square).then_inc(csq_s, 1)
                if n > 2:
                    act.wait_ge(cn_s, n - 2)
                if n:
                    root(f"var_conf{n - 1}", rstd[:, ((n - 1) % 2) * T:((n - 1) % 2 + 1) * T], T, P)
            for n in range(4):
                act.wait_ge(cn_s, n + 1)
                act.activation(cln[:, n, :], cacc[:, n, :], ACT.Silu, bias=V("ln_b", n))\
                   .then_inc(cact_s, 1)
                act.wait_ge(cact_s, n + 1)
                act.copy(m_hi[:, n, :], cln[:, n, :]).then_inc(h_hi_s, 1)
            residual(2, FIRST["w_out1"])
            norm(3, lambda k: ada[:, 2, 3 * KT + k:3 * KT + k + 1])
            split_after(FIRST["w_out1"] + 3)
            ffn(1)

            def copy_out(name, dst):
                src = wait_full(act, name)
                act.copy(dst, src[:, :].rearrange("p (a t) -> p a t", a=2)).then_inc(drain_of(name), 1)

            def attention(r):
                base = 16 * (r - 1)
                for h in range(H2 + 2):
                    if h < H2:
                        act.wait_ge(nb_s, base + h + 1)
                        if h >= 2:
                            wait_full(act, f"pT{r}_{h - 2}")
                        for t, (a, n) in enumerate(((0, P), (P, 2 * P))):
                            last = act.activation(p2[:, h % 2, a:a + n], st[:, h % 2, a:a + n], ACT.Exp,
                                                  bias=stat_(1, 2 * h + t), scale=HD ** -0.5,
                                                  accum_out=stat_(2, 2 * h + t))
                        last.then_inc(p_s, 1)
                    if h and h <= H2:
                        src = wait_full(act, f"pT{r}_{h - 1}")
                        act.copy(pT2[:, (h - 1) % 2, :], src[:, 0:3 * P]).then_inc(pT_s, 1)
                    if h % 2 == 1 and h > 1:
                        j = h // 2 - 1
                        hi_from(f"o{r}_{j}", h_hi[:, j, :], f"o{r}_{j}")

            norm(4)
            split_after(FIRST["down1"] + 11)
            for n in range(8):
                copy_out(f"qk2_{n}", (q2, k2)[n // 4][:, 2 * (n % 4):2 * (n % 4) + 2, :])
                split_after(FIRST["moba_qk"] + n)
            for n in range(4):
                copy_out(f"v2_{n}", v2[:, :, n * T:(n + 1) * T])
                split_after(FIRST["moba_v"] + n)
            attention(2)
            residual(4, FIRST["w_o0"])
            norm(5)
            split_after(FIRST["w_o0"] + 3)
            ffn(2)

            norm(6)
            split_after(FIRST["down2"] + 15)
            act.copy(wf_hi[:, :], cols[:, COL["w_f"]:COL["w_f"] + KT * H2]).then_inc(wf_s, 1)
            norm_tiles(6, name="n6q", hi=h2_hi)
            for n in range(4):
                copy_out(f"qk3_{n}", k2[:, 2 * n:2 * n + 2, :])
                split_after(FIRST["fox_k"] + n)
            for n in range(4):
                copy_out(f"v3_{n}", v2[:, :, n * T:(n + 1) * T])
                split_after(FIRST["fox_v"] + n)
            wait_drained(act, "z")
            act.activation(lf[:, 2, :], lf[:, 1, :], ACT.Abs).then_inc(lfa_s, 1)
            act.wait_ge(lfa_s, 1)
            act.activation(lf[:, 0, :], lf[:, 2, :], ACT.Exp, scale=-1.0).then_inc(lfa_s, 1)
            act.wait_ge(lfa_s, 2)
            act.activation(lf[:, 2, :], lf[:, 0, :], ACT.Ln, bias=C("ones", 0, 1)).then_inc(lfa_s, 1)
            for n in range(4):
                copy_out(f"qq_{n}", q2[:, 2 * n:2 * n + 2, :])
                split_after(FIRST["fox_q"] + n)
            attention(3)
            residual(6, FIRST["w_o1"])
            norm(7)
            split_after(FIRST["w_o1"] + 3)
            ffn(3)
            root("ms_8", rstd[:, 0:T], T, D)

        @block.vector
        def _(dve):
            order = [0]

            def link(ins):
                order[0] += 1
                ins.then_inc(v_own, 1)
                dve.wait_ge(v_own, order[0])

            def split_lo(c, it=0):
                if POOL_LO[0] <= c < POOL_LO[1]:
                    return
                dve.wait_ge(hi_ready, c + 1 + 4 * it)
                dve.tensor_tensor(w_lo[:, c % SPL, :], raw[:, c % RAW, :],
                                  w_hi[:, c % SPL, :].bitcast(F32), ALU.subtract).then_inc(lo_ready, 1)

            def split_after(c, it=0):
                if c + SPL < NCH:
                    split_lo(c + SPL, it)

            def add_squares(q, n, total):
                dve.wait_ge(sq_ready, 4 * q + n + 1)
                if n > 1:
                    dve.wait_ge(acc_ready, 3 * q + n - 1)
                dve.tensor_tensor(total[:, :], total[:, :], sq[:, :], ALU.add).then_inc(acc_ready, 1)

            def inverse(name, buf):
                wait_drained(dve, name)
                link(dve.reciprocal(buf, buf))

            def lo_of(name, dst, src, hi, shift=None):
                dve.wait_ge(h_hi_s, HN[name])
                dve.wait_ge(t_ready, TN[name])
                if shift is None:
                    dve.tensor_tensor(dst, src, hi.bitcast(F32), ALU.subtract).then_inc(h_lo_s, 1)
                else:
                    dve.scalar_tensor_tensor(dst, src, shift, hi.bitcast(F32), ALU.add,
                                             ALU.subtract).then_inc(h_lo_s, 1)

            def norm_tiles(name, scale, shift=None, hi=h_hi, lo=h_lo):
                dve.wait_ge(h_lo_s, HN[f"{name}_0"] - 1)
                for k in range(KT + 1):
                    if 3 <= k < KT:
                        dve.wait_ge(h_lo_s, HN[f"{name}_{k - 3}"])
                    if k < KT:
                        dve.scalar_tensor_tensor(tmp[:, k % 3, 0:T], x[:, k, :], scale(k), rstd[:, 0:T],
                                                 ALU.mult, ALU.mult).then_inc(t_ready, 1)
                    if k:
                        lo_of(f"{name}_{k - 1}", lo[:, k - 1, :], tmp[:, (k - 1) % 3, 0:T],
                              hi[:, k - 1, :], None if shift is None else shift(k - 1))

            def norm(r, scale, shift=None):
                inverse(f"ms_{r}", rstd[:, 0:T])
                norm_tiles(f"n{r}", scale, shift)

            def modulation(name, v, a, n, src_at):
                layer = v // 2
                last = dve.tensor_tensor(ada[:, v, a:a + n], banks[5][:, src_at:src_at + n],
                                         cols[:, COL["ada_b"] + layer * ADA + a:
                                              COL["ada_b"] + layer * ADA + a + n], ALU.add)
                return last

            def gains(v, norm_name, layer, at):
                return dve.scalar_tensor_tensor(
                    gain[:, 1 if v == 1 else 0, :], ada[:, v, at:at + KT], 1.0,
                    cols[:, COL[norm_name] + layer * KT:COL[norm_name] + (layer + 1) * KT],
                    ALU.add, ALU.mult)

            for n in range(1, 4):
                add_squares(0, n, acc_c)
            for n in range(1, 4):
                add_squares(1, n, acc)
            dve.wait_ge(cols_in, 16)
            dve.wait_ge(ada_used, ADA1)
            link(modulation("ada_a", 1, 0, 2 * KT, ADA))
            modulation("ada_a", 0, 0, 2 * KT, 0).then_inc(drain_of("ada_a"), 1)
            wait_drained(dve, "ada_a")
            link(gains(1, "norm1", 0, KT))
            link(gains(0, "norm1", 0, KT))
            split_lo(0)
            split_lo(1)
            inverse("ms_0", rstd[:, :])
            dve.wait_ge(x_in, 16)
            dve.wait_ge(ctx_in, 16)
            for k in range(KT + 1):
                if 3 <= k < KT:
                    dve.wait_ge(h_lo_s, HN[f"n0_{k - 3}"])
                if k < KT:
                    dve.scalar_tensor_tensor(tmp[:, k % 3, 0:T], ctxT[:, k, :], gain[:, 1, k:k + 1],
                                             rstd[:, 0:T], ALU.mult, ALU.mult)
                    dve.scalar_tensor_tensor(tmp[:, k % 3, T:2 * T], x[:, k, :], gain[:, 0, k:k + 1],
                                             rstd[:, T:2 * T], ALU.mult, ALU.mult).then_inc(t_ready, 1)
                if k:
                    j = k - 1
                    dve.wait_ge(h_hi_s, HN[f"n0_{j}"])
                    dve.wait_ge(t_ready, TN[f"n0_{j}"])
                    dve.scalar_tensor_tensor(hc_lo[:, j, :], tmp[:, j % 3, 0:T], ada[:, 1, j:j + 1],
                                             hc_hi[:, j, :].bitcast(F32), ALU.add, ALU.subtract)
                    dve.scalar_tensor_tensor(h_lo[:, j, :], tmp[:, j % 3, T:2 * T], ada[:, 0, j:j + 1],
                                             h_hi[:, j, :].bitcast(F32), ALU.add,
                                             ALU.subtract).then_inc(h_lo_s, 1)

            def latents(name, n, width, gain_name, src, hi, lo):
                dve.wait_ge(h_lo_s, HN[f"{name}_0"] - 1)
                for j in range(n):
                    dve.scalar_tensor_tensor(tmp[:, j, 0:width], src(j), V(gain_name, j),
                                             rstd[:, 0:width], ALU.mult, ALU.mult).then_inc(t_ready, 1)
                for j in range(n):
                    lo_of(f"{name}_{j}", lo[:, j, :], tmp[:, j, 0:width], hi[:, j, :])

            c = FIRST["w_in"]
            split_after(c)
            split_after(c + 1)
            inverse("ms_kv", rstd[:, :])
            latents("ckv", CKV, 2 * T, "kv_ln", lambda j: banks[j][:, :], ckv_hi, ckv_lo)
            rope = slice(NOPE, QKH)
            src = wait_full(dve, "krot")
            dve.wait_ge(krg_s, 1)
            link(dve.tensor_tensor(kr[rope, 0:T], src[rope, 0:T], C("rope_s")[rope, :], ALU.mult))
            link(dve.tensor_tensor(kr[rope, T:2 * T], krg[rope, T:2 * T], C("rope_c")[rope, :], ALU.mult))
            dve.tensor_tensor(kr[rope, T:2 * T], kr[rope, T:2 * T], kr[rope, 0:T], ALU.add)\
               .then_inc(drain_of("krot"), 1)
            wait_drained(dve, "krot")
            dve.tensor_copy(kr[rope, 0:T], krg[rope, 0:T]).then_inc(kr_s, 1)
            split_after(c + 2)
            split_after(c + 3)
            inverse("ms_cq", rstd[:, 0:T])
            latents("cq", CQ, T, "q_ln", lambda j: (banks[3][:, 0:T], banks[3][:, T:2 * T],
                                                     banks[6][:, 0:T])[j], cq_hi, cq_lo)
            split_after(c + 4)

            for h in range(MLA_H):
                rs = rs_b[0:QKH, h % 2, :]
                wait_drained(dve, f"ms_k{h}")
                dve.reciprocal(rs, rs).then_inc(krs_s, 1)
                dve.wait_ge(krs_s, h + 1)
                src = wait_full(dve, f"k{h}")
                dve.wait_ge(ksq_s, h + 1)
                dve.scalar_tensor_tensor(kT[0:NOPE, h, :], src[0:NOPE, :], V("k_norm", 0, slice(0, NOPE)),
                                         rs_b[0:NOPE, h % 2, :], ALU.mult, ALU.mult).then_inc(kT_s, 1)
            split_after(FIRST["w_uk"])

            for j in range(MLA_H // 2):
                two = lambda a: a.rearrange("p (i t) -> p i t", i=2)
                table = lambda name: C(name)[0:QKH, :].rearrange("p (o t) -> p o t", o=1)\
                    .broadcast_to([QKH, 2, T])
                src = wait_full(dve, f"qrot{j}")
                dve.wait_ge(qsq_s, j + 1)
                if j:
                    dve.wait_ge(qT_s, j)
                else:
                    dve.wait_ge(h_lo_s, HN[f"cq_{CQ - 1}"])
                dve.tensor_tensor(two(tmp[0:QKH, 0, :]), two(qg[0:QKH, j % 2, :]), table("rope_c"),
                                  ALU.mult)
                dve.tensor_tensor(two(tmp[0:QKH, 1, :]), two(src[0:QKH, :]), table("rope_s"), ALU.mult)\
                   .then_inc(drain_of(f"qrot{j}"), 1)
                wait_drained(dve, f"qrot{j}")
                link(dve.tensor_tensor(tmp[0:QKH, 0, :], tmp[0:QKH, 0, :], tmp[0:QKH, 1, :], ALU.add))
                inverse(f"ms_q{j}", rs_b[0:QKH, j % 2, :])
                dve.tensor_tensor(qT[0:QKH, 2 * j:2 * j + 2, :].rearrange("p i t -> p (i t)"),
                                  tmp[0:QKH, 0, :], rs_b[0:QKH, j % 2, :], ALU.mult).then_inc(qT_s, 1)
                if j % 2:
                    split_after(FIRST["w_uq"] + j // 2)
            split_after(FIRST["w_uv"])

            def lo_from(name, dst, hi, bank_name):
                dve.wait_ge(h_hi_s, HN[name])
                src = banks[bank_use[bank_name].b]
                dve.tensor_tensor(dst, src[:, 0:T], hi.bitcast(F32), ALU.subtract).then_inc(h_lo_s, 1)

            def maximum0(s):
                src = wait_full(dve, f"s0_{s}")
                link(dve.reduce_max(stat_(0, s), src[:, :], AX))
                dve.tensor_scalar(stat_(1, s), stat_(0, s), -float(QKH) ** -0.5, None, ALU.mult)\
                   .then_inc(nb_s, 1)

            steps = 2 * MLA_H
            maximum0(0)
            for s in range(steps + 2):
                if s + 1 < steps:
                    maximum0(s + 1)
                if s < steps:
                    dve.wait_ge(p_s, s + 1)
                    dve.reciprocal(stat_(3, s), stat_(2, s)).then_inc(ri_s, 1)
                g = s // 4
                if s % 4 == 1:
                    if g:
                        lo_from(f"o_{g - 1}", h_lo[:, g - 1, :], h_hi[:, g - 1, :], f"o0_{g - 1}")
                    if g < FG:
                        lo_from(f"y_{g}", h_lo[:, 4 + g, :], h_hi[:, 4 + g, :], f"dft_y{g}")
            dve.wait_ge(ada_used, NADA)
            modulation("ada_b", 0, 2 * KT, ADA - 2 * KT, 2 * KT).then_inc(drain_of("ada_b"), 1)
            wait_drained(dve, "ada_b")

            def residual(stage, c, names, gate=None):
                for n in range(4):
                    src = wait_full(dve, names[n])
                    if gate is None:
                        two = x[:, 2 * n:2 * n + 2, :].rearrange("p a t -> p (a t)")
                        dve.tensor_tensor(two, two, src[:, :], ALU.add).then_inc(res_ready, 1)
                    else:
                        for j in range(2):
                            last = dve.scalar_tensor_tensor(
                                x[:, 2 * n + j, :], src[:, j * T:(j + 1) * T], gate(2 * n + j),
                                x[:, 2 * n + j, :], ALU.mult, ALU.add)
                        last.then_inc(res_ready, 1)
                    if n < 3:
                        split_after(c + n)
                    if n:
                        add_squares(stage + 2, n, acc)

            def ffn(r, gate=None):
                _, up, down = LAYERS[r]
                c = FIRST[up]

                def step(j, cc, it, pair, count):
                    if r < 2 and j % 2 == 0:
                        split_after(cc, it)
                        return
                    slot = (j // 2 if r < 2 else j) % 2
                    dve.wait_ge(u_lo_s, count - 1)
                    if r < 2:
                        wait_drained(dve, f"{up}_{j - 1}", it)
                        src = wait_full(dve, f"{up}_{j}", it)
                        dve.tensor_tensor(u_t[:, slot, :], silu_b[:, :], src[:, :], ALU.mult)\
                           .then_inc(drain_of(f"{up}_{j}"), 1)
                    else:
                        wait_drained(dve, f"{up}_{j}", it)
                        dve.tensor_tensor(u_t[:, slot, :], silu_b[:, :], silu_b[:, :], ALU.mult)\
                           .then_inc(ut_s, 1)
                    split_after(cc, it)
                    dve.wait_ge(u_hi_s, count)
                    dve.tensor_tensor(u_lo[:, pair, :],
                                      u_t[:, slot, :].rearrange("p (a t) -> p a t", a=2),
                                      u_hi[:, pair, :].bitcast(F32), ALU.subtract).then_inc(u_lo_s, 1)

                with dve.Fori(0, 5 if r < 2 else 4) as i:
                    for j in range(4):
                        if r < 2:
                            step(j, c + j, i, ds(4 * i + 2 * (j // 2), 2), U0[r] + j // 2 + 1 + 2 * i)
                        else:
                            step(j, c + j, i, ds(8 * i + 2 * j, 2), U0[r] + j + 1 + 4 * i)
                if r < 2:
                    for j in range(2):
                        step(4 + j, c + 20 + j, 0, slice(20, 22), U0[r] + 11)
                c = FIRST[down]
                names = [f"{down}_{n}" for n in range(4)]
                if r < 2:
                    for kc in range(8):
                        split_after(c + kc)
                    residual(2 * r + 1, c + 8, names, gate)
                else:
                    with dve.Fori(0, 3) as i:
                        for n in range(4):
                            split_after(c + n, i)
                    residual(2 * r + 1, c + 12, names, gate)

            col = lambda v, a: (lambda k: ada[:, v, a * KT + k:a * KT + k + 1])
            own = lambda name, layer=0: (lambda k: V(name, layer * KT + k))
            link(gains(0, "norm2", 0, 4 * KT))
            residual(0, FIRST["w_out0"], [f"w_out0_{n}" for n in range(4)], col(0, 2))
            norm(1, lambda k: gain[:, 0, k:k + 1], col(0, 3))
            split_after(FIRST["w_out0"] + 3)
            ffn(0, col(0, 5))

            dve.wait_ge(ada_used, 2 * NADA)
            modulation("ada_c", 2, 0, ADA, 0).then_inc(drain_of("ada_c"), 1)
            wait_drained(dve, "ada_c")
            link(gains(2, "norm1", 1, KT))
            norm(2, lambda k: gain[:, 0, k:k + 1], col(2, 0))
            split_after(FIRST["down0"] + 11)
            for a in range(2):
                dve.memset(conf[:, :, a * (PAD + T):a * (PAD + T) + PAD], 0.0)
                link(dve.memset(scin[:, :, a * (T + 1):a * (T + 1) + 1], 0.0))

            def gated(n, name, dst):
                src = wait_full(dve, name)
                dve.wait_ge(sig_s, n + 1)
                dve.tensor_tensor(dst, src[:, 0:T], sig[:, n % 2, :], ALU.mult)\
                   .then_inc(drain_of(name), 1)
                wait_drained(dve, name)

            def convolve(dst, src, taps, tap, bias):
                if bias is None:
                    link(dve.tensor_scalar(dst, src(0), tap(0), None, ALU.mult))
                else:
                    link(dve.tensor_scalar(dst, src(0), tap(0), bias, ALU.mult, ALU.add))
                for i in range(1, taps):
                    ins = dve.scalar_tensor_tensor(dst, src(i), tap(i), dst, ALU.mult, ALU.add)
                    if i < taps - 1:
                        link(ins)
                return ins

            def conf_tile(n):
                gated(n, f"b_a{n}", conf[:, n, PAD:PAD + T])
                convolve(cacc[:, n, :], lambda i: conf[:, n, i:i + T], CONV,
                         lambda i: V("conf_dw", 4 * i + n), V("conf_b", n)).then_inc(conv_s, 1)

            for n in range(3):
                conf_tile(n)
            gated(3, "b_a3", conf[:, 3, PAD:PAD + T])
            for n in range(4):
                gated(4 + n, f"b_s{n}", scin[:, n, 1:1 + T])
                link(convolve(scacc[:, n, :], lambda i: scin[:, n, i:i + T], SCONV,
                              lambda i: V("sc_dw", 4 * i + n), None))
            convolve(cacc[:, 3, :], lambda i: conf[:, 3, i:i + T], CONV,
                     lambda i: V("conf_dw", 4 * i + 3), V("conf_b", 3)).then_inc(conv_s, 1)
            for n in range(4):
                src = wait_full(dve, f"b_b{n // 2}")
                dve.wait_ge(h_lo_s, HN["sc_0"] - 1 + n // 3)
                dve.tensor_tensor(tmp[:, n % 3, 0:T], src[:, (n % 2) * T:(n % 2 + 1) * T],
                                  scacc[:, n, :], ALU.mult).then_inc(t_ready, 1)
                lo_of(f"sc_{n}", m_lo[:, 4 + n, :], tmp[:, n % 3, 0:T], m_hi[:, 4 + n, :])
            for n in range(4):
                src = wait_full(dve, f"ms_conf{n}")
                dve.scalar_tensor_tensor(cln[:, n, :], src[:, 0:T], -1.0 / P, cacc[:, n, :], ALU.mult,
                                         ALU.add).then_inc(cen_s, 1)
            for n in range(4):
                half = rstd[:, (n % 2) * T:(n % 2 + 1) * T]
                inverse(f"var_conf{n}", half)
                dve.wait_ge(cen_s, n + 1)
                dve.scalar_tensor_tensor(cacc[:, n, :], cln[:, n, :], V("ln_g", n), half, ALU.mult,
                                         ALU.mult).then_inc(cn_s, 1)
            for n in range(4):
                dve.wait_ge(h_hi_s, HN[f"conf_{n}"])
                dve.tensor_tensor(m_lo[:, n, :], cln[:, n, :], m_hi[:, n, :].bitcast(F32),
                                  ALU.subtract).then_inc(h_lo_s, 1)
            link(gains(2, "norm2", 1, 4 * KT))
            residual(2, FIRST["w_out1"], [f"w_out1_{n}" for n in range(4)], col(2, 2))
            norm(3, lambda k: gain[:, 0, k:k + 1], col(2, 3))
            split_after(FIRST["w_out1"] + 3)
            ffn(1, col(2, 5))

            def attention(r):
                base = 16 * (r - 1)

                def maximum(h):
                    src = wait_full(dve, f"s{r}_{h}")
                    if h >= 2:
                        dve.wait_ge(p_s, base + h - 1)
                    if r == 2:
                        dve.scalar_tensor_tensor(st[:, h % 2, :], C("alibi"),
                                                 2.0 ** (-8.0 * (h + 1) / H2) * HD ** 0.5,
                                                 src[:, 0:3 * P], ALU.mult, ALU.add)\
                           .then_inc(drain_of(f"s{r}_{h}"), 1)
                    else:
                        for t, (a, n) in enumerate(((0, P), (P, 2 * P))):
                            last = dve.scalar_tensor_tensor(
                                st[:, h % 2, a:a + n], src[:, a:a + n],
                                ccol[:, t * H2 + h:t * H2 + h + 1], C("mask", a, n), ALU.add, ALU.add)
                        last.then_inc(drain_of(f"s{r}_{h}"), 1)
                    wait_drained(dve, f"s{r}_{h}")
                    for t, (a, n) in enumerate(((0, P), (P, 2 * P))):
                        last = dve.reduce_max(stat_(0, 2 * h + t), st[:, h % 2, a:a + n], AX)
                    link(last)
                    dve.tensor_scalar(stat_(1, 2 * h, 2), stat_(0, 2 * h, 2), -HD ** -0.5, None,
                                      ALU.mult).then_inc(nb_s, 1)

                maximum(0)
                for h in range(H2 + 2):
                    if h + 1 < H2:
                        maximum(h + 1)
                    if h < H2:
                        dve.wait_ge(p_s, base + h + 1)
                        dve.reciprocal(stat_(3, 2 * h, 2), stat_(2, 2 * h, 2)).then_inc(ri_s, 1)
                    if h % 2 == 1 and h > 1:
                        j = h // 2 - 1
                        lo_from(f"o{r}_{j}", h_lo[:, j, :], h_hi[:, j, :], f"o{r}_{j}")

            norm(4, own("attn_norm", 0))
            split_after(FIRST["down1"] + 11)
            for n in range(8):
                split_after(FIRST["moba_qk"] + n)
            for n in range(4):
                split_after(FIRST["moba_v"] + n)
            attention(2)
            residual(4, FIRST["w_o0"], [f"w_o0_{n}" for n in range(4)])
            norm(5, own("mlp_norm", 0))
            split_after(FIRST["w_o0"] + 3)
            ffn(2)

            norm(6, own("kv_norm"))
            split_after(FIRST["down2"] + 15)
            dve.wait_ge(wf_s, 1)
            dve.tensor_tensor(wf_lo[:, :], cols[:, COL["w_f"]:COL["w_f"] + KT * H2],
                              wf_hi[:, :].bitcast(F32), ALU.subtract).then_inc(wf_s, 1)
            norm_tiles("n6q", own("attn_norm", 1), None, h2_hi, h2_lo)
            for n in range(4):
                split_after(FIRST["fox_k"] + n)
            for n in range(4):
                split_after(FIRST["fox_v"] + n)
            src = wait_full(dve, "z")
            for t in range(TT):
                last = dve.tensor_tensor(lf[:, 1, t * H2:(t + 1) * H2], src[:, t * H2:(t + 1) * H2],
                                         cols[:, COL["b_f"]:COL["b_f"] + H2], ALU.add)
            last.then_inc(drain_of("z"), 1)
            dve.wait_ge(lfa_s, 3)
            dve.scalar_tensor_tensor(lf[:, 0, :], lf[:, 1, :], 0.0, lf[:, 2, :], ALU.min,
                                     ALU.subtract).then_inc(lf_s, 1)
            for n in range(4):
                split_after(FIRST["fox_q"] + n)
            src = wait_full(dve, "cum_col")
            dve.tensor_scalar(ccol[:, :], src[:, 0:TT * H2], HD ** 0.5, None, ALU.mult)\
               .then_inc(drain_of("cum_col"), 1)
            src = wait_full(dve, "cum_row")
            dve.tensor_scalar(crow[0:H2, :], src[0:H2, 0:T], -HD ** 0.5, None, ALU.mult)\
               .then_inc(drain_of("cum_row"), 1)
            wait_drained(dve, "cum_row")
            attention(3)
            residual(6, FIRST["w_o1"], [f"w_o1_{n}" for n in range(4)])
            norm(7, own("mlp_norm", 1))
            split_after(FIRST["w_o1"] + 3)
            ffn(3)
            inverse("ms_8", rstd[:, 0:T])
            for k in range(KT):
                dve.scalar_tensor_tensor(x[:, k, :], x[:, k, :], V("final", k), rstd[:, 0:T],
                                         ALU.mult, ALU.mult).then_inc(res_ready, 1)

        @block.gpsimd
        def _(pool):
            pool.wait_ge(kr_s, 1)
            rope = slice(NOPE, QKH)
            for h in range(MLA_H):
                pool.wait_ge(krs_s, h + 1)
                pool.tensor_tensor(kT[rope, h, :], kr[rope, :], rs_b[rope, h % 2, :], ALU.mult)\
                    .then_inc(kTr_s, 1)
            for s in range(2 * MLA_H):
                pool.wait_ge(ri_s, s + 1)
                pool.tensor_scalar(p0[:, s % 2, :], p0[:, s % 2, :], stat_(3, s), None, ALU.mult)\
                    .then_inc(pn_s, 1)
            first, end = POOL_LO
            for c in range(first, end):
                pool.wait_ge(hi_ready, c + 1)
                pool.tensor_tensor(w_lo[:, c % SPL, :], raw[:, c % RAW, :],
                                   w_hi[:, c % SPL, :].bitcast(F32), ALU.subtract).then_inc(lo_pool, 1)
            for r in (2, 3):
                base = 16 * (r - 1)
                for h in range(H2):
                    pool.wait_ge(ri_s, base + h + 1)
                    for t, (a, n) in enumerate(((0, P), (P, 2 * P))):
                        last = pool.tensor_scalar(p2[:, h % 2, a:a + n], p2[:, h % 2, a:a + n],
                                                  stat_(3, 2 * h + t), None, ALU.mult)
                    last.then_inc(pn_s, 1)


def columns(vector):
    v = np.asarray(vector, np.float32).reshape(-1, P)
    return v.T


def full_depth(w):
    return w.reshape(KT, P, -1, 2 * P).transpose(2, 1, 0, 3).reshape(-1, P, CH)


def by_depth(w):
    k = -(-w.shape[0] // D)
    w = np.concatenate([w, np.zeros((k * D - w.shape[0], D), w.dtype)])
    return w.reshape(k, KT, P, 4, 2 * P).transpose(0, 3, 2, 1, 4).reshape(-1, P, CH)


def padded(w):
    return np.concatenate([w, np.zeros((P, CH - w.shape[1]), w.dtype)], 1)[None]


def pad_last(w, before, after):
    return np.pad(w, [(0, 0)] * (w.ndim - 1) + [(before, after)])


def constants():
    con = np.zeros((P, NCON), np.float32)

    def put(name, value, a=0):
        con[:value.shape[0], CON[name] + a:CON[name] + a + value.shape[1]] = value

    put("ident", np.eye(P))
    put("ones", np.ones((P, P)))
    i, t = np.arange(P), np.arange(T)
    w = 2 * np.pi * np.outer(i, i) / P
    put("dft_c", np.concatenate([np.cos(w), np.sin(w)], 1))
    w = 2 * np.pi * np.outer(t, t) / T
    for part, m in enumerate((np.cos(w), -np.sin(w))):
        for j in range(TT):
            put("dft_n", m[j * P:(j + 1) * P] / np.sqrt(T * P), (2 * part + j) * T)
    half = ROPE // 2
    rot = np.zeros((QKH, QKH))
    for j in range(half):
        rot[NOPE + half + j, NOPE + j] = -1
        rot[NOPE + j, NOPE + half + j] = 1
    put("rot", rot)
    inv = (10000.0 ** (-np.arange(ROPE // 4, dtype=np.float32) / (ROPE // 4))).astype(np.float32)
    angle = np.concatenate([np.outer(inv, t // 64), np.outer(inv, t % 64)]).astype(np.float32)
    put("rope_c", np.concatenate([np.ones((NOPE, T)), np.cos(angle), np.cos(angle)]))
    put("rope_s", np.concatenate([np.zeros((NOPE, T)), np.sin(angle), np.sin(angle)]))
    q = np.concatenate([i[:, None] - i[None], P + i[:, None] - t[None]], 1)
    put("alibi", np.where(q < 0, NEG, -q))
    put("mask", np.where(q < 0, NEG, 0.0))
    put("tri", (i[:, None] <= t[None]).astype(np.float32))
    put("onehot", np.eye(H2))
    put("eps", np.full((P, 1), EPS))
    return con


def kernel(**inputs):
    import concourse.bacc as bacc
    from concourse.bass_utils import run_bass_kernel_spmd

    a = {name: np.asarray(value) for name, value in inputs.items()}
    w_in = a["a_w_in"][0]
    z = lambda n: np.zeros((D, n), w_in.dtype)
    latents = w_in[:, 0:672]
    first = np.concatenate([latents[:, 384:640], z(64), latents[:, 640:672], z(32), latents[:, 0:384],
                            w_in[:, 672:]], 1)
    heads = lambda w, k: pad_last(w, 0, P - w.shape[-1]).reshape(k, P, -1)
    w_uk = heads(a["a_w_uk"][0], CKV).transpose(1, 0, 2).reshape(P, -1)
    w_uq = heads(a["a_w_uq"][0], CQ).reshape(CQ, P, 2, 4 * P).transpose(2, 1, 0, 3).reshape(2, P, -1)
    w_uv = a["a_w_uv"][0].reshape(CKV, P, -1).transpose(1, 0, 2).reshape(P, -1)

    def two_by_two(*ws):
        n = ws[0].shape[1] // P
        return full_depth(np.stack([w.reshape(D, n, P) for w in ws], 2).reshape(D, -1))

    def swiglu_up(layer):
        one, three = full_depth(a["ffn_w1"][layer]), full_depth(a["ffn_w3"][layer])
        return np.stack([one, three], 1).reshape(-1, P, CH)

    b_in = np.split(a["b_w_in"][0], 5, 1)
    qkv, kv = a["moba_w_qkv_2"][0], a["w_kv_2"]
    stream = np.concatenate([
        full_depth(first), padded(w_uk), padded(w_uq[0]), padded(w_uq[1]), padded(w_uv),
        full_depth(a["a_w_out"][0]), swiglu_up(0), by_depth(a["ffn_w2"][0]),
        two_by_two(b_in[0], b_in[1]), two_by_two(b_in[3], b_in[4]), full_depth(b_in[2]),
        full_depth(a["b_w_out"][0]), swiglu_up(1), by_depth(a["ffn_w2"][1]),
        full_depth(qkv), full_depth(a["w_o_2"][0]), full_depth(a["w_up_2"][0]), by_depth(a["w_down_2"][0]),
        full_depth(kv), full_depth(a["fox_w_q_2"][0]), full_depth(a["w_o_2"][1]),
        full_depth(a["w_up_2"][1]), by_depth(a["w_down_2"][1])])
    assert stream.shape[0] == NCH
    ada_stream = np.concatenate([full_depth(w) for w in a["ada_w"]])

    parts = {"norm1": columns(a["norm1_g"]), "norm2": columns(a["norm2_g"]), "ada_b": columns(a["ada_b"]),
             "q_ln": columns(a["a_q_ln_g"]), "kv_ln": columns(a["a_kv_ln_g"]),
             "q_norm": columns(pad_last(a["a_q_norm_g"], 0, P - QKH)),
             "k_norm": columns(pad_last(a["a_k_norm_g"], 0, P - QKH)),
             "conf_dw": columns(a["b_conf_dw"][0]), "conf_b": columns(a["b_conf_dw_b"]),
             "ln_g": columns(a["b_conf_ln_g"]), "ln_b": columns(a["b_conf_ln_b"]),
             "sc_dw": columns(a["b_sc_dw"][0]), "attn_norm": columns(a["attn_norm_2"]),
             "kv_norm": columns(a["kv_norm_2"]), "mlp_norm": columns(a["mlp_norm_2"]),
             "final": columns(a["final_norm_2"]), "b_f": np.repeat(a["b_f_2"][None], P, 0),
             "c": np.stack([columns(a["c"][0]), columns(a["c_ctx"])], 2).reshape(P, -1),
             "w_f": a["w_f_2"].reshape(KT, P, H2).transpose(1, 0, 2).reshape(P, -1)}
    by_tile = lambda t: t[0].T.reshape(KT, P, T).transpose(1, 0, 2)
    arrays = {"stream": stream, "ada_stream": ada_stream, "x": by_tile(a["x"]), "ctx": by_tile(a["ctx"]),
              "cols": np.concatenate([parts[name] for name, _ in COLS], 1), "con": constants()}
    arrays = {f"in_{name}": np.ascontiguousarray(v) for name, v in arrays.items()}

    nc = bacc.Bacc("TRN2", target_bir_lowering=False, num_devices=1)
    args = [nc.dram_tensor(name, v.shape, F32, kind="ExternalInput").ap() for name, v in arrays.items()]
    out = nc.dram_tensor("out_0", (KT, P, T), F32, kind="ExternalOutput").ap()
    program(nc, *args, out)
    got = run_bass_kernel_spmd(nc, [arrays], core_ids=[0]).results[0]["out_0"]
    return np.ascontiguousarray(np.asarray(got).reshape(D, T).T.reshape(1, T, D))
```

```python
from contextlib import ExitStack

import numpy as np

import concourse.bass as bass
from concourse import mybir

F32 = mybir.dt.float32
F32R = mybir.dt.float32r
ALU = mybir.AluOpType
ACT = mybir.ActivationFunctionType
AX = mybir.AxisListType.X
ds = bass.ds

P = 128
D = 1024
KT = D // P
T = 256
TT = T // P
CH = KT * 2 * P
EPS = 1e-6

BCAST = ("k0", "q0", "k1", "k2", "q1", "k3", "k4", "q2", "k5", "k6", "q3", "k7")
MLA_H, NOPE, ROPE, QKH, VH = 8, 64, 32, 96, 64
CQ, CKV = 3, 2
FG = 4
CONV, SCONV = 31, 3
PAD = (CONV - 1) // 2
DFF = 2816
UT1 = DFF // P
DFF2 = 4096
UT2 = DFF2 // P
H2, HD = 16, 64
ADA = 6 * D // P
RAW, SPL, AR = 4, 2, 2

STAGES = [("w_in", 5), ("w_uk", 1), ("w_uq", 2), ("w_uv", 1), ("w_out0", 4),
          ("up0", 2 * (UT1 // 2)), ("down0", 12),
          ("b_in", 10), ("w_out1", 4), ("up1", 2 * (UT1 // 2)), ("down1", 12),
          ("moba_qk", 8), ("moba_v", 4), ("w_o0", 4), ("up2", 16), ("down2", 16),
          ("fox_k", 4), ("fox_v", 4), ("fox_q", 4), ("w_o1", 4), ("up3", 16), ("down3", 16)]
FIRST = {}
_n = 0
for _name, _count in STAGES:
    FIRST[_name] = _n
    _n += _count
NCH = _n
LAYERS = [("w_out0", "up0", "down0"), ("w_out1", "up1", "down1"),
          ("w_o0", "up2", "down2"), ("w_o1", "up3", "down3")]
NADA = 24
ADA1 = 8
ADA_DVE = (1, 3, 5)
ADA_ALT = 16
ADA2, ADA3 = 28, 38
PAIR_AT = [1, 3, 5, 8, 11]
MOD_SUM_AT = [1, 3, 5, 8, 11]

COLS = [("norm1", 2 * KT), ("norm2", 2 * KT), ("ada_b", 2 * ADA), ("q_ln", CQ), ("kv_ln", CKV),
        ("q_norm", 1), ("k_norm", 1), ("conf_dw", 4 * CONV), ("conf_b", 4), ("ln_g", 4), ("ln_b", 4),
        ("sc_dw", 4 * SCONV), ("attn_norm", 2 * KT), ("kv_norm", KT), ("mlp_norm", 2 * KT),
        ("final", KT), ("b_f", H2), ("c", 2 * KT), ("w_f", KT * H2)]
COL = {}
_n = 0
for _name, _count in COLS:
    COL[_name] = _n
    _n += _count
NCOL = _n

CONSTS = [("ones", P), ("eps", 1), ("ident", P), ("dft_c", 2 * P), ("dft_n", 4 * T), ("rot", P), ("rope_c", T),
          ("rope_s", T), ("alibi", 3 * P), ("mask", 3 * P), ("tri", T), ("onehot", H2), ("sel", 23)]
CON = {}
_n = 0
for _name, _count in CONSTS:
    CON[_name] = _n
    _n += _count
NCON = _n
NEARLY = P + 1
NEG = -1e30




def numbered(names):
    return {name: i + 1 for i, name in enumerate(names)}


def tiles(name, n=KT):
    return [f"{name}_{k}" for k in range(n)]


T_ORDER = tiles("n0") + tiles("ckv", CKV) + tiles("cq", CQ) + tiles("n1") + tiles("n2") + tiles("sc", 4) \
    + tiles("n3")
TN = numbered(T_ORDER)
H_ORDER = tiles("n0") + tiles("ckv", CKV) + tiles("cq", CQ) \
    + [f"{k}_{g}" for g in range(4) for k in "yo"] + tiles("n1") + tiles("n2") + tiles("sc", 4) \
    + tiles("conf", 4) + tiles("n3") + tiles("n4") + tiles("o2") + tiles("n5") + tiles("n6") \
    + tiles("n6q") + tiles("o3") + tiles("n7")
HN = numbered(H_ORDER)
U0 = [0, UT1 // 2, UT1, UT1 + UT2 // 2]


class Use:
    def __init__(self, b, fill, chunk, before, drain):
        self.b, self.fill, self.chunk, self.before, self.drain = b, fill, chunk, before, drain


class Banks:

    def __init__(self):
        self.fills, self.drains, self.last, self.of = [0] * 8, [0] * 8, [None] * 8, {}

    def claim(self, name, b, chunk=None, drain=None, times=1):
        own = drain or ("drained", b, self.drains[b] + 1)
        self.of[name] = Use(b, self.fills[b] + 1, chunk, self.last[b], own)
        if drain is None:
            self.drains[b] += times
            self.last[b] = ("drained", b, self.drains[b])
        else:
            self.last[b] = drain
        if chunk is None:
            self.fills[b] += times


def plan():
    k = Banks()
    k.claim("ms_0", 4)
    k.claim("ada_a", 5, chunk=-1)
    c = FIRST["w_in"]
    t = lambda name: ("t_ready", None, TN[name])
    lo = lambda name: ("h_lo_s", None, HN[name])
    count = lambda sem, n: (sem, None, n)
    k.claim("ada_b", 5, chunk=-1)
    k.claim("ckv0", 0, None, t("ckv_0"))
    k.claim("ckv1", 1, c, t("ckv_1"))
    k.claim("kr", 2, None, count("krg_s", 3))
    k.claim("cq01", 3, None, t("cq_1"))
    k.claim("ms_kv", 4)
    k.claim("cq2", 6, c + 2, t("cq_2"))
    k.claim("krot", 4)
    k.claim("f01", 7, c + 3)
    k.claim("ms_cq", 4)
    k.claim("f23", 2, c + 4)
    k.claim("ms_kq", 6)
    for h in range(MLA_H):
        k.claim(f"k{h}", h % 4, FIRST["w_uk"] if h == MLA_H - 1 else None)
    for j in range(MLA_H // 2):
        k.claim(f"q{j}", j, FIRST["w_uq"] + j // 2 if j % 2 else None, count("qsq_s", j + 1))
        k.claim(f"qrot{j}", 7)
    for n in range(4):
        k.claim(f"v0_{n}", n, FIRST["w_uv"] if n == 3 else None)
    for n, name in enumerate(BCAST):
        k.claim(f"rs_{name}", (4, 6, 7)[n % 3], None, count(f"{name[0]}T_s", int(name[1]) + 1))
    for s in range(2 * MLA_H):
        k.claim(f"s0_{s}", (0, 1, 6)[s % 3], None, count("p_s", s + 1))
        k.claim(f"pT0_{s}", 2 + s % 2, None, count("pT_s", s + 1))
        if s % 4 == 0:
            k.claim(f"o0_{s // 4}", 4, None, lo(f"o_{s // 4}"))
    for g in range(FG):
        k.claim(f"dft_a{g}", 7)
        k.claim(f"dft_y{g}", 7, None, lo(f"y_{g}"))
    for r, (mix, up, down) in enumerate(LAYERS):
        if r == 1:
            for n in range(4):
                k.claim(f"b_a{n}", n, FIRST["b_in"] + n)
            k.claim("conv0", 4, None, count("conv_s", 1))
            for n in range(4):
                k.claim(f"b_s{n}", n, FIRST["b_in"] + 4 + n)
            for n in range(2):
                k.claim(f"b_b{n}", n, FIRST["b_in"] + 8 + n, t(f"sc_{2 * n + 1}"))
            for n in range(4):
                k.claim(f"ms_conf{n}", (6, 5)[n % 2], None, count("cen_s", n + 1))
                k.claim(f"var_conf{n}", (7, 4)[n % 2])
        if r >= 2:
            base = 16 * (r - 1)
            for n in range(8 if r == 2 else 4):
                k.claim(f"qk{r}_{n}", n % 4, FIRST[("moba_qk", "fox_k")[r - 2]] + n)
            for n in range(4):
                k.claim(f"v{r}_{n}", n, FIRST[("moba_v", "fox_v")[r - 2]] + n)
            if r == 3:
                k.claim("z", 5)
                for n in range(4):
                    k.claim(f"qq_{n}", n, FIRST["fox_q"] + n)
                k.claim("cum_col", 5)
                k.claim("cum_row", 6)
            for h in range(H2):
                k.claim(f"s{r}_{h}", (0, 1, 5, 7)[h % 4])
                k.claim(f"pT{r}_{h}", 2 + h % 2, None, count("pT_s", base + h + 1))
                if h % 2 == 0:
                    k.claim(f"o{r}_{h // 2}", (4, 6)[h // 2 % 2], None, lo(f"o{r}_{h // 2}"))
        for n in range(4):
            k.claim(f"{mix}_{n}", n, FIRST[mix] + n, count("res_ready", 8 * r + n + 1))
        k.claim(f"ms_{2 * r + 1}", 4)
        if r == 0:
            k.claim("ada_c", 5, chunk=-1)
        for b in range(4):
            k.claim(f"{up}_{b}", b, FIRST[up] + b, times=5 if r < 2 else 4)
        if r < 2:
            for b in range(2):
                k.claim(f"{up}_{4 + b}", b, FIRST[up] + 20 + b)
        for n in range(4):
            k.claim(f"{down}_{n}", n, FIRST[down] + (8 if r < 2 else 12) + n,
                    count("res_ready", 8 * r + 4 + n + 1))
        k.claim(f"ms_{2 * r + 2}", 4)
    return k.of


POOL_LO = (FIRST["b_in"], FIRST["w_out1"] + 4)


def program(nc, stream, ada_stream, xT_d, ctxT_d, cols_d, con_d, out):
    bank_use = plan()
    ctx = ExitStack()
    with ctx:
        def sb(name, shape, dt=F32, where=ctx):
            return where.enter_context(nc.sbuf_tensor(name, shape, dt))

        def sem(name):
            return ctx.enter_context(nc.semaphore(name))

        def scratch(*specs, where=None):
            s = ExitStack()
            made = [sb(*spec, where=s) for spec in specs]
            s.close() if where is None else where.callback(s.close)
            return made

        raw = sb("raw", [P, RAW, CH])
        w_hi = sb("w_hi", [P, SPL, CH], F32R)
        w_lo = sb("w_lo", [P, SPL, CH], F32R)
        ada_w = sb("ada_w", [P, AR, CH])
        x = sb("x", [P, KT, T])
        h_hi = sb("h_hi", [P, KT, T], F32R)
        h_lo = sb("h_lo", [P, KT, T], F32R)
        sq = sb("sq", [P, 2 * T])
        acc = sb("acc", [P, 2 * T])
        rstd = sb("rstd", [P, 2 * T])
        tmp = sb("tmp", [P, 3, 2 * T])
        cols = sb("cols", [P, NCOL])
        con = sb("con", [P, NCON])
        macc = sb("macc", [P, 2, 2 * P])
        one = sb("one", [P, 1])
        cs = sb("cs", [P, 2 * KT])
        ada = sb("ada", [P, 3, ADA])
        gain = sb("gain", [P, 2, KT])
        stat = sb("stat", [P, 4 * 2 * H2])

        u_hi, u_lo, silu_b, u_t = scratch(
            ("u_hi", [P, UT2, T], F32R), ("u_lo", [P, UT2, T], F32R),
            ("silu_b", [P, 2 * T]), ("u_t", [P, 2, 2 * T]))
        m0 = ExitStack()
        cq_hi, cq_lo, krg, kr, ksq, rs_b, qg, v0, uF, ab, acc_c = scratch(
            ("cq_hi", [P, CQ, T], F32R), ("cq_lo", [P, CQ, T], F32R), ("krg", [P, 2 * T]),
            ("kr", [P, 2 * T]), ("ksq", [P, 2, 2 * T]), ("rs_b", [P, 2 * T]),
            ("qg", [P, 2, 2 * T]), ("v0", [P, 4, MLA_H * VH]), ("uF", [P, FG, T]),
            ("ab", [P, 2, TT, 2 * P]), ("acc_c", [P, 2 * T]), where=m0)
        ctxT, hc_hi, hc_lo = scratch(("ctxT", [P, KT, T]), ("hc_hi", [P, KT, T], F32R),
                                     ("hc_lo", [P, KT, T], F32R))
        qT, kT = scratch(("qT", [P, MLA_H, T]), ("kT", [P, MLA_H, 2 * T]), where=m0)
        ckv_hi, ckv_lo = scratch(("ckv_hi", [P, CKV, 2 * T], F32R), ("ckv_lo", [P, CKV, 2 * T], F32R))
        (p0,) = scratch(("p0", [P, 3, 2 * T]), where=m0)
        pT0 = qg
        m0.close()
        m_hi, m_lo, conf, cacc, scin, scacc, sig, cln, csq, taps = scratch(
            ("m_hi", [P, KT, T], F32R), ("m_lo", [P, KT, T], F32R),
            ("conf", [P, 4, T + 2 * PAD]), ("cacc", [P, 4, T]), ("scin", [P, 4, T + 2]),
            ("scacc", [P, 4, T]), ("sig", [P, 2, T]), ("cln", [P, 4, T]), ("csq", [P, 2, T]),
            ("taps", [P, CONV, P]))
        h2_hi, h2_lo, q2, k2, v2, p2, pT2, crow, ccol, lf, wf_hi, wf_lo = scratch(
            ("h2_hi", [P, KT, T], F32R), ("h2_lo", [P, KT, T], F32R),
            ("q2", [P, KT, T]), ("k2", [P, KT, T]), ("v2", [P, TT, D]), ("p2", [P, 4, 3 * P]),
            ("pT2", [P, 2, 3 * P]), ("crow", [P, T]), ("ccol", [P, TT * H2]),
            ("lf", [P, 3, TT * H2]), ("wf_hi", [P, KT * H2], F32R), ("wf_lo", [P, KT * H2], F32R))

        banks = [ctx.enter_context(nc.psum_tensor(f"bank{b}", [P, 2 * T], F32))[:, :] for b in range(8)]

        loaded = [sem(f"loaded{s}") for s in range(RAW)]
        ada_loaded = [sem(f"ada_loaded{s}") for s in range(AR)]
        cols_in, con_in, x_in, ctx_in = sem("cols_in"), sem("con_in"), sem("x_in"), sem("ctx_in")
        ones_in = sem("ones_in")
        hi_ready = sem("hi_ready")
        lo_ready = sem("lo_ready")
        lo_pool = sem("lo_pool")
        chunk_used = sem("chunk_used")
        ada_early = [sem(f"ada_early{s}") for s in range(RAW)]
        ada_used = sem("ada_used")
        ada_pool, ada_dve = sem("ada_pool"), sem("ada_dve")
        pool_own, dve_own = sem("pool_own"), sem("dve_own")
        filled = [sem(f"filled{b}") for b in range(8)]
        drained = [sem(f"drained{b}") for b in range(8)]
        cs_ready = sem("cs_ready")
        res_ready = sem("res_ready")
        sq_ready = sem("sq_ready")
        acc_ready = sem("acc_ready")
        t_ready = sem("t_ready")
        h_hi_s, h_lo_s = sem("h_hi_s"), sem("h_lo_s")
        u_hi_s, u_lo_s = sem("u_hi_s"), sem("u_lo_s")
        v_own = sem("v_own")
        lat_sq = sem("lat_sq")
        krg_s = sem("krg_s")
        kr_s = sem("kr_s")
        ksq_s, qsq_s = sem("ksq_s"), sem("qsq_s")
        kq_sum = sem("kq_sum")
        krs_s = sem("krs_s")
        kT_s, kTr_s = sem("kT_s"), sem("kTr_s")
        qrot_s = sem("qrot_s")
        qT_s = sem("qT_s")
        rs_s = sem("rs_s")
        nb_s = sem("nb_s")
        p_s = sem("p_s")
        pn_s = sem("pn_s")
        pT_s = sem("pT_s")
        sig_s = sem("sig_s")
        taps_s = sem("taps_s")
        conv_s = sem("conv_s")
        cen_s, csq_s = sem("cen_s"), sem("csq_s")
        cn_s, cact_s = sem("cn_s"), sem("cact_s")
        wf_s = sem("wf_s")
        lfa_s, lf_s = sem("lfa_s"), sem("lf_s")
        sent = sem("sent")

        signals = {"t_ready": t_ready, "h_lo_s": h_lo_s, "krg_s": krg_s, "kT_s": kT_s, "qT_s": qT_s,
                   "qsq_s": qsq_s,
                   "p_s": p_s, "pT_s": pT_s, "cen_s": cen_s, "conv_s": conv_s, "res_ready": res_ready}

        def C(name, a=0, n=None):
            n = dict(CONSTS)[name] - a if n is None else n
            return con[:, CON[name] + a:CON[name] + a + n]

        def V(name, j, rows=slice(0, P)):
            return cols[rows, COL[name] + j:COL[name] + j + 1]

        def stat_(kind, i, n=1):
            return stat[:, kind * 2 * H2 + i:kind * 2 * H2 + i + n]

        def weighed(eng, a, it=0):
            if a < ADA1:
                eng.wait_ge(ada_dve, ADA_DVE.index(a) + 1)
            elif a < ADA_ALT:
                eng.wait_ge(ada_pool, a - ADA1 + 1)
            elif a % 2:
                eng.wait_ge(ada_dve, len(ADA_DVE) + (a - ADA_ALT) // 2 + 1 + it)
            else:
                eng.wait_ge(ada_pool, ADA_ALT - ADA1 + (a - ADA_ALT) // 2 + 1 + it)

        def ada_in(eng, a, it=0):
            if AR <= a < ADA1 - AR:
                eng.wait_ge(ada_early[a - AR], 16)
                return raw[:, a - AR, :]
            eng.wait_ge(ada_loaded[a % AR], 16 if a < AR else 16 * (a // AR - 1) + 16 * it)
            return ada_w[:, a % AR, :]

        def weigh_waits(eng, a, it):
            src = ada_in(eng, a, it)
            if 2 <= a < ADA1:
                if a - 2 in ADA_DVE:
                    eng.wait_ge(ada_used, a - 1)
            elif a >= 2:
                eng.wait_ge(ada_used, a - 1 + 2 * it)
            return src

        def lo_done(eng, c, it=0):
            first, end = POOL_LO
            if first <= c < end:
                eng.wait_ge(lo_pool, c - first + 1 + 4 * it)
            else:
                eng.wait_ge(lo_ready, c + 1 - (end - first if c >= end else 0) + 4 * it)

        block = ctx.enter_context(nc.Block())

        def wait_full(eng, name, it=0):
            use = bank_use[name]
            if use.chunk is None:
                eng.wait_ge(filled[use.b], use.fill + it)
            else:
                eng.wait_ge(chunk_used, use.chunk + 1 + 4 * it)
            return banks[use.b]

        def wait_drain(eng, drain, it=0):
            name, b, n = drain
            eng.wait_ge(drained[b] if b is not None else signals[name], n + it)

        def wait_drained(eng, name, it=0):
            wait_drain(eng, bank_use[name].drain, it)

        def drain_of(name):
            sem_name, b, _ = bank_use[name].drain
            return drained[b] if b is not None else signals[sem_name]

        @block.sync
        def _(sp):
            sp.dma_start(cols[:, :], cols_d).then_inc(cols_in, 16)
            sp.dma_start(con[:, 0:NEARLY], con_d[:, 0:NEARLY]).then_inc(ones_in, 16)

            def load_ada(a, it=0):
                if ADA1 - AR <= a < ADA1 + AR:
                    sp.wait_ge(ada_used, (a - (ADA1 - AR) if a < ADA1 else a - AR) + 1)
                elif a >= ADA1 + AR:
                    weighed(sp, a - AR, it)
                sp.dma_start(ada_w[:, a % AR, :], ada_stream[ds(a + 2 * it, 1), :, :]
                             .rearrange("o p n -> p (o n)")).then_inc(ada_loaded[a % AR], 16)

            def load(c, it=0):
                if c >= RAW:
                    lo_done(sp, c - RAW, it)
                else:
                    sp.wait_ge(ada_used, AR + c + 1)
                sp.dma_start(raw[:, c % RAW, :], stream[ds(c + 4 * it, 1), :, :]
                             .rearrange("o p n -> p (o n)")).then_inc(loaded[c % RAW], 16)

            for a in range(AR):
                load_ada(a)
            for s in range(RAW):
                sp.dma_start(raw[:, s, :], ada_stream[AR + s, :, :]).then_inc(ada_early[s], 16)
            sp.dma_start(ctxT[:, :, :], ctxT_d).then_inc(ctx_in, 16)
            sp.dma_start(x[:, :, :], xT_d).then_inc(x_in, 16)
            for a in range(ADA1 - AR, ADA1):
                load_ada(a)
            sp.dma_start(con[:, NEARLY:NCON], con_d[:, NEARLY:NCON]).then_inc(con_in, 16)
            a = ADA1
            for c in range(FIRST["up0"]):
                load(c)
                for _ in range({1: 2, 3: 2, 5: 2, 6: 2, 9: 2, 10: 2}.get(c, 0)):
                    load_ada(a)
                    a += 1
            for a in range(a, ADA2):
                load_ada(a)
            c0 = FIRST["up0"]
            with sp.Fori(0, 5) as i:
                for j in range(4):
                    load(c0 + j, i)
                    if j < 2:
                        load_ada(ADA2 + j, i)
            for j in range(14):
                load(c0 + 20 + j)
                if j in (0, 5, 7, 9, 11):
                    a = ADA3 + 2 * (0, 5, 7, 9, 11).index(j)
                    load_ada(a)
                    load_ada(a + 1)
            c = c0 + 34
            for end in (POOL_LO[0] + RAW, POOL_LO[1] + RAW, NCH):
                steps = (end - c) // RAW
                with sp.Fori(0, steps) as i:
                    for j in range(RAW):
                        load(c + j, i)
                for c in range(c + RAW * steps, end):
                    load(c)
                c = end
            for k in range(KT):
                sp.wait_ge(res_ready, 32 + k + 1)
                sp.dma_start(out[k, :, :], x[:, k, :]).then_inc(sent, 16)
            sp.wait_ge(sent, 16 * KT)

        @block.tensor
        def _(pe):
            def fill(name):
                use = bank_use[name]
                if use.before is not None:
                    wait_drain(pe, use.before)
                return banks[use.b]

            def refill(name, it):
                use = bank_use[name]
                pe.wait_ge(drained[use.b], use.drain[2] - 1 + it)
                return banks[use.b]

            def full(ins, name):
                assert bank_use[name].chunk is None
                ins.then_inc(filled[bank_use[name].b], 1)

            def product(dst, whi, wlo, xhi, xlo, c, kts, need=None, it=0, start=True):
                pe.wait_ge(hi_ready, c + 1 + 4 * it)
                for i, k in enumerate(kts):
                    if need is not None:
                        need(k)
                    pe.matmul(dst, whi(k), xhi(k), start=start and i == 0, stop=False,
                              skip_group_check=True)
                    pe.matmul(dst, whi(k), xlo(k), start=False, stop=False, skip_group_check=True)
                lo_done(pe, c, it)
                for k in kts:
                    last = pe.matmul(dst, wlo(k), xhi(k), start=False, stop=k == kts[-1],
                                     skip_group_check=True)
                return last

            def wtile(c, j, width=2 * P):
                return [(lambda k, b=b: b[:, c % SPL, k * width + j * P:k * width + (j + 1) * P])
                        for b in (w_hi, w_lo)]

            def split_need(name):
                def need(k):
                    pe.wait_ge(h_hi_s, HN[f"{name}_{k}"])
                    pe.wait_ge(h_lo_s, HN[f"{name}_{k}"])
                return need

            hh = (lambda k: h_hi[:, k, :], lambda k: h_lo[:, k, :])
            hc = (lambda k: hc_hi[:, k, :], lambda k: hc_lo[:, k, :])
            hm = (lambda k: m_hi[:, k, :], lambda k: m_lo[:, k, :])
            hq = (lambda k: h2_hi[:, k, :], lambda k: h2_lo[:, k, :])

            def two_tiles(c, name, need, operand=hh, it=None, kts=range(KT), by_k=False):
                dst = fill(name) if it is None else refill(name, it)
                it = 0 if it is None else it
                if by_k:
                    pe.wait_ge(hi_ready, c + 1 + 4 * it)
                    for k in kts:
                        need(k)
                        for j in range(2):
                            for part in operand:
                                pe.matmul(dst[:, j * T:(j + 1) * T], wtile(c, j)[0](k), part(k),
                                          start=k == kts[0] and j == 0 and part is operand[0],
                                          stop=False, skip_group_check=True)
                    lo_done(pe, c, it)
                    for j in range(2):
                        for k in kts:
                            last = pe.matmul(dst[:, j * T:(j + 1) * T], wtile(c, j)[1](k),
                                             operand[0](k), start=False, stop=True,
                                             skip_group_check=True)
                for j in range(0 if by_k else 2):
                    last = product(dst[:, j * T:(j + 1) * T], *wtile(c, j), *operand, c, kts,
                                   need, it)
                last.then_inc(chunk_used, 1)

            two_rows = banks[5][:, 0:2 * ADA].rearrange("p (v t) -> p t v", v=2)

            def modulation(a):
                src = ada_in(pe, a)
                for j in range(2):
                    for k in range(KT):
                        last = pe.matmul(two_rows[:, 2 * a + j, :],
                                         src[:, (2 * k + j) * P:(2 * k + j + 1) * P],
                                         cs[:, 2 * k:2 * k + 2], start=k == 0, stop=k == KT - 1,
                                         skip_group_check=True)
                last.then_inc(ada_used, 1)

            def modulation_sums(a):
                weighed(pe, a)
                for v in range(2):
                    for j in range(2):
                        last = pe.matmul(two_rows[:, 2 * a + j, v:v + 1],
                                         macc[:, 1 - v, j * P:(j + 1) * P], one[:, :],
                                         start=True, stop=True, skip_group_check=True)
                last.then_inc(ada_used, 1)

            def modulation_sum(a, it=0):
                weighed(pe, a, it)
                for j in range(2):
                    last = pe.matmul(banks[5][:, ds(2 * a + j + 4 * it, 1)],
                                     macc[:, a % 2, j * P:(j + 1) * P], one[:, :],
                                     start=True, stop=True, skip_group_check=True)
                last.then_inc(ada_used, 1)

            def modulation_pair(a, it=0):
                modulation_sum(a, it)
                modulation_sum(a + 1, it)

            def mean_square(name, *parts):
                dst = fill(name)
                for where, srcs in parts:
                    rows = srcs[0].shape[0]
                    for i, src in enumerate(srcs):
                        last = pe.matmul(dst[0:rows, where], C("ones")[0:rows, 0:rows], src,
                                         start=i == 0, stop=i == len(srcs) - 1, skip_group_check=True)
                full(last, name)

            halves = lambda a: [a[:, 0:T], a[:, T:2 * T]]

            def norm(r):
                pe.wait_ge(acc_ready, 3 * r + 6)
                mean_square(f"ms_{r}", (slice(0, T), halves(acc)))

            def late_norm(r):
                pe.wait_ge(acc_ready, 3 * r + 6)
                dst = fill(f"ms_{r}")
                for i, src in enumerate(halves(acc)):
                    pe.matmul(dst[:, 0:T], C("ones"), src, start=i == 0, stop=i == 1,
                              skip_group_check=True)
                for t in range(TT):
                    for i in range(2):
                        last = pe.matmul(dst[:, T + t:T + t + 1],
                                         acc[:, i * T + t * P:i * T + (t + 1) * P], C("ones", 0, 1),
                                         start=i == 0, stop=i == 1, skip_group_check=True)
                full(last, f"ms_{r}")

            pe.wait_ge(cs_ready, 1)
            for a in range(ADA1):
                if a == ADA1 - 1:
                    pe.wait_ge(ones_in, 16)
                    pe.wait_ge(acc_ready, 6)
                    mean_square("ms_0", (slice(0, T), halves(acc_c)), (slice(T, 2 * T), halves(acc)))
                if a in ADA_DVE:
                    modulation_sums(a)
                else:
                    modulation(a)
            pe.wait_ge(con_in, 16)

            need = split_need("n0")
            c = FIRST["w_in"]

            def ctx_and_x(c, j, name):
                dst = fill(name)
                for half, op in ((0, hc), (1, hh)):
                    last = product(dst[:, half * T:(half + 1) * T], *wtile(c, j), *op, c, range(KT), need)
                return last

            fill("ada_b")
            modulation_sum(ADA1)
            full(ctx_and_x(c, 0, "ckv0"), "ckv0")
            modulation_sum(ADA1 + 1)
            ctx_and_x(c, 1, "ckv1").then_inc(chunk_used, 1)
            full(ctx_and_x(c + 1, 0, "kr"), "kr")
            modulation_sum(ADA1 + 2)
            cq = fill("cq01")
            product(cq[:, 0:T], *wtile(c + 1, 1), *hh, c + 1, range(KT)).then_inc(chunk_used, 1)
            pe.wait_ge(lat_sq, CKV)
            mean_square("ms_kv", (slice(0, 2 * T), [qg[:, 0, :], qg[:, 1, :]]))
            full(product(cq[:, T:2 * T], *wtile(c + 2, 0), *hh, c + 2, range(KT)), "cq01")
            product(fill("cq2")[:, 0:T], *wtile(c + 2, 1), *hh, c + 2, range(KT)).then_inc(chunk_used, 1)
            pe.wait_ge(krg_s, 1)
            full(pe.matmul(fill("krot")[0:QKH, 0:T], C("rot")[NOPE:QKH, 0:QKH], krg[NOPE:QKH, T:2 * T],
                           start=True, stop=True), "krot")
            modulation_sum(ADA1 + 3)
            two_tiles(c + 3, "f01", None)
            modulation_sum(ADA1 + 4)
            pe.wait_ge(lat_sq, CKV + 2)
            mean_square("ms_cq", (slice(0, T), [qg[:, 0, 0:T], qg[:, 0, T:2 * T], qg[:, 1, 0:T]]))
            two_tiles(c + 4, "f23", None)
            modulation_sum(ADA1 + 5)

            c = FIRST["w_uk"]
            ckv = (lambda k: ckv_hi[:, k, :], lambda k: ckv_lo[:, k, :])

            squares_bank, ROWS = fill("ms_kq"), len(BCAST)

            def add_row(n):
                pe.wait_ge(*((ksq_s, n + 1) if n < MLA_H else (qsq_s, n - MLA_H + 1)))
                last = pe.matmul(squares_bank[0:ROWS, :], C("sel", ROWS - 1 - n, ROWS)[0:QKH, :],
                                 ksq[0:QKH, n % 2, :], start=n == 0, stop=n == ROWS - 1,
                                 skip_group_check=True)
                if n < ROWS - 1:
                    last.then_inc(kq_sum, 1)
                else:
                    full(last, "ms_kq")

            for h in range(MLA_H):
                last = product(fill(f"k{h}"), *wtile(c, h, MLA_H * P), *ckv, c, range(CKV),
                               split_need("ckv"))
                if h < MLA_H - 1:
                    full(last, f"k{h}")
                else:
                    last.then_inc(chunk_used, 1)
                if h == 0:
                    pe.wait_ge(krg_s, 3)
                else:
                    add_row(h - 1)
                if h == MLA_H // 2:
                    modulation_sum(ADA1 + 6)

            cqx = (lambda k: cq_hi[:, k, :], lambda k: cq_lo[:, k, :])

            def rotate(j):
                full(pe.matmul(fill(f"qrot{j}")[0:QKH, :], C("rot")[0:QKH, 0:QKH], qg[0:QKH, j % 2, :],
                               start=True, stop=True), f"qrot{j}")

            for j in range(MLA_H // 2):
                c = FIRST["w_uq"] + j // 2
                dst = fill(f"q{j}")
                for i in range(2):
                    last = product(dst[:, i * T:(i + 1) * T], *wtile(c, 2 * (j % 2) + i, 4 * P), *cqx, c,
                                   range(CQ), split_need("cq"))
                if j % 2:
                    last.then_inc(chunk_used, 1)
                else:
                    full(last, f"q{j}")
                add_row(MLA_H - 1 + j)
                if j:
                    rotate(j - 1)
                if j == 1:
                    modulation_sum(ADA1 + 7)
            add_row(ROWS - 1)
            rotate(MLA_H // 2 - 1)

            def values(dst, c, width, xs, t, kts, it=0):
                pe.wait_ge(hi_ready, c + 1 + 4 * it)
                lo_done(pe, c, it)
                n = 0
                for k in kts:
                    xhi, xlo = (f(k)[:, t * P:(t + 1) * P] for f in xs)
                    whi, wlo = (b[:, c % SPL, k * width:(k + 1) * width] for b in (w_hi, w_lo))
                    for a, b in ((xhi, whi), (xhi, wlo), (xlo, whi)):
                        n += 1
                        last = pe.matmul(dst, a, b, start=n == 1, stop=n == 3 * len(kts),
                                         skip_group_check=True)
                return last

            c = FIRST["w_uv"]
            for t in range(4):
                last = values(fill(f"v0_{t}"), c, MLA_H * VH, ckv, t, range(CKV))
                if t < 3:
                    full(last, f"v0_{t}")
                else:
                    last.then_inc(chunk_used, 1)

            modulation_pair(ADA_ALT)
            pe.wait_ge(krs_s, 1)
            for name in BCAST:
                row = int(name[1]) + (MLA_H if name[0] == "q" else 0)
                full(pe.matmul(fill(f"rs_{name}")[0:QKH, :],
                               C("onehot", row, 1)[0:ROWS, :].to_broadcast([ROWS, QKH]), rs_b[0:ROWS, :],
                               start=True, stop=True), f"rs_{name}")


            def score0(s):
                h, t = divmod(s, 2)
                pe.wait_ge(kT_s, h + 1)
                pe.wait_ge(qT_s, h // 2 + 1)
                full(pe.matmul(fill(f"s0_{s}"), qT[0:QKH, h, t * P:(t + 1) * P], kT[0:QKH, h, :],
                               start=True, stop=True), f"s0_{s}")

            def weigh0(s):
                h, t = divmod(s, 2)
                name = f"o0_{s // 4}"
                dst = banks[bank_use[name].b] if s % 4 else fill(name)
                pe.wait_ge(pT_s, s + 1)
                if s == 0:
                    for n in range(4):
                        wait_drained(pe, f"v0_{n}")
                rows = slice(VH * (h % 2), VH * (h % 2) + VH)
                for k in range(4):
                    last = pe.matmul(dst[rows, t * P:(t + 1) * P], v0[:, k, h * VH:(h + 1) * VH],
                                     pT0[:, s % 2, k * P:(k + 1) * P], start=k == 0, stop=k == 3,
                                     skip_group_check=True)
                if s % 4 == 3:
                    full(last, name)

            def fourier(g, step):
                if step == 0:
                    wait_drained(pe, ("f01", "f23")[g // 2])
                    dst = fill(f"dft_a{g}")
                    for t in range(TT):
                        last = pe.matmul(dst[:, t * T:(t + 1) * T], uF[:, g, t * P:(t + 1) * P],
                                         C("dft_c"), start=True, stop=True, skip_group_check=True)
                    full(last, f"dft_a{g}")
                else:
                    wait_drained(pe, f"dft_a{g}")
                    dst = fill(f"dft_y{g}")
                    for n, (t, part) in enumerate((t, part) for t in range(TT) for part in range(2)):
                        last = pe.matmul(dst[:, 0:T], ab[:, g % 2, t, part * P:(part + 1) * P],
                                         C("dft_n", (2 * part + t) * T, T), start=n == 0, stop=n == 3,
                                         skip_group_check=True)
                    full(last, f"dft_y{g}")

            steps = 2 * MLA_H
            for s in range(3):
                score0(s)
            for s in range(steps + 1):
                if s in PAIR_AT:
                    modulation_pair(ADA_ALT + 2 + 2 * PAIR_AT.index(s))
                if s < steps:
                    if s % 4 < 2:
                        fourier(s // 4, s % 4)
                    dst = fill(f"pT0_{s}")
                    pe.wait_ge(pn_s, s + 1)
                    for k in range(4):
                        last = pe.transpose(dst[:, k * P:(k + 1) * P], p0[:, s % 3, k * P:(k + 1) * P],
                                            C("ident"))
                    full(last, f"pT0_{s}")
                if s + 3 < steps:
                    score0(s + 3)
                if s:
                    weigh0(s - 1)

            def mixer_order(k):
                pe.wait_ge(h_hi_s, HN[f"o_{k}" if k < 4 else f"y_{k - 4}"])
                pe.wait_ge(h_lo_s, HN[f"o_{k}" if k < 4 else f"y_{k - 4}"])

            for n in range(4):
                two_tiles(FIRST["w_out0"] + n, f"w_out0_{n}", mixer_order)

            def ffn(r):
                _, up, down = LAYERS[r]
                c = FIRST[up]
                need = split_need(f"n{2 * r + 1}")
                rounds = 5 if r < 2 else 4
                if r < 2:
                    for j in range(4):
                        fill(f"{up}_{j}")
                else:
                    for j in range(4):
                        two_tiles(c + j, f"{up}_{j}", need)
                        if j == 0:
                            late_norm(2 * r + 1)
                with pe.Fori(0 if r < 2 else 1, rounds) as i:
                    for j in range(4):
                        two_tiles(c + j, f"{up}_{j}", need, it=i, by_k=r < 2 and j == 0)
                    if r == 0:
                        modulation_pair(ADA2, i)
                if r < 2:
                    for j in range(2):
                        two_tiles(c + 20 + j, f"{up}_{4 + j}", need)

                c = FIRST[down]
                base = U0[r]

                def depth(kg, n_k, g=None):
                    first = isinstance(kg, int) and kg == 0
                    it = 0 if isinstance(kg, int) and g is None else g
                    for n in range(4):
                        cc = c + n + (4 * kg if isinstance(kg, int) else 4)
                        dst = fill(f"{down}_{n}") if first else banks[n]
                        pe.wait_ge(hi_ready, cc + 1 + 4 * it)
                        if n == 0:
                            pairs = 4 * kg + n_k // 2 if isinstance(kg, int) else 8 + 4 * it
                            pe.wait_ge(u_hi_s, base + pairs)
                            pe.wait_ge(u_lo_s, base + pairs)
                        for part in range(2):
                            if part:
                                lo_done(pe, cc, it)
                            for j in range(2):
                                whi, wlo = wtile(cc, j)
                                out_ = dst[:, j * T:(j + 1) * T]
                                for k in range(n_k):
                                    if isinstance(kg, int):
                                        hi, lo = u_hi[:, 8 * kg + k, :], u_lo[:, 8 * kg + k, :]
                                    else:
                                        hi, lo = (u[:, ds(8 + k + 8 * it, 1), :]
                                                  .rearrange("p o t -> p (o t)") for u in (u_hi, u_lo))
                                    fresh = first and not part and j == 0 and k == 0
                                    if part == 0:
                                        pe.matmul(out_, whi(k), hi, start=fresh, stop=False,
                                                  skip_group_check=True)
                                        pe.matmul(out_, whi(k), lo, start=False, stop=False,
                                                  skip_group_check=True)
                                    else:
                                        last = pe.matmul(out_, wlo(k), hi, start=False, stop=True,
                                                         skip_group_check=True)
                        last.then_inc(chunk_used, 1)
                        if r == 0 and cc - c in MOD_SUM_AT:
                            modulation_pair(ADA3 + 2 * MOD_SUM_AT.index(cc - c))

                depth(0, 8)
                if r < 2:
                    depth(1, 8)
                    depth(2, UT1 - 16)
                else:
                    with pe.Fori(0, 3) as g:
                        depth(None, 8, g)

            norm(1)
            ffn(0)

            norm(2)
            need = split_need("n2")

            def convolution0():
                dst = fill("conv0")
                wait_drained(pe, "b_a0")
                pe.wait_ge(taps_s, CONV)
                for i in range(CONV):
                    last = pe.matmul(dst[:, 0:T], taps[:, i, :], conf[:, 0, i:i + T], start=i == 0,
                                     stop=i == CONV - 1, skip_group_check=True)
                full(last, "conv0")

            def group_mean(n):
                pe.wait_ge(conv_s, n + 1)
                mean_square(f"ms_conf{n}", (slice(0, T), [cacc[:, n, :]]))

            def group_variance(n):
                pe.wait_ge(csq_s, n + 1)
                mean_square(f"var_conf{n}", (slice(0, T), [csq[:, n % 2, :]]))

            c = FIRST["b_in"]
            for n in range(4):
                two_tiles(c + n, f"b_a{n}", need, by_k=n == 0)
            convolution0()
            for n in range(4):
                two_tiles(c + 4 + n, f"b_s{n}", need)
            group_mean(0)
            two_tiles(c + 8, "b_b0", need)
            group_variance(0)
            group_mean(1)
            two_tiles(c + 9, "b_b1", need)
            group_variance(1)
            group_mean(2)
            group_mean(3)
            group_variance(2)
            group_variance(3)

            def mixer1_order(k):
                pe.wait_ge(h_hi_s, HN[f"conf_{k}" if k < 4 else f"sc_{k - 4}"])
                pe.wait_ge(h_lo_s, HN[f"conf_{k}" if k < 4 else f"sc_{k - 4}"])

            for n in range(4):
                two_tiles(FIRST["w_out1"] + n, f"w_out1_{n}", mixer1_order, hm,
                          kts=(4, 5, 6, 7, 0, 1, 2, 3), by_k=n == 0)
            norm(3)
            ffn(1)

            def attention(r):
                base = 16 * (r - 1)

                def score(h):
                    rows = slice(HD * (h % 2), HD * (h % 2) + HD)
                    dst = fill(f"s{r}_{h}")
                    for t, (a, n) in enumerate(((0, P), (P, 2 * P))):
                        last = pe.matmul(dst[:, a:a + n], q2[rows, h // 2, t * P:(t + 1) * P],
                                         k2[rows, h // 2, 0:n], start=True, stop=r == 2,
                                         skip_group_check=True)
                        if r == 3:
                            last = pe.matmul(dst[:, a:a + n],
                                             C("onehot", h, 1)[0:H2, :].to_broadcast([H2, P]),
                                             crow[0:H2, 0:n], start=False, stop=True,
                                             skip_group_check=True)
                    full(last, f"s{r}_{h}")

                def weigh(h):
                    name = f"o{r}_{h // 2}"
                    dst = banks[bank_use[name].b] if h % 2 else fill(name)
                    pe.wait_ge(pT_s, base + h + 1)
                    rows = slice(HD * (h % 2), HD * (h % 2) + HD)
                    pe.matmul(dst[rows, 0:T], v2[:, 0, h * HD:(h + 1) * HD], pT2[:, h % 2, 0:T],
                              start=True, stop=False, skip_group_check=True)
                    last = pe.matmul(dst[rows, P:T], v2[:, 1, h * HD:(h + 1) * HD],
                                     pT2[:, h % 2, T:3 * P], start=False, stop=True,
                                     skip_group_check=True)
                    if h % 2:
                        full(last, name)

                for h in range(4):
                    score(h)
                for h in range(H2 + 1):
                    if h < H2:
                        dst = fill(f"pT{r}_{h}")
                        pe.wait_ge(pn_s, base + h + 1)
                        for k in range(3):
                            last = pe.transpose(dst[:, k * P:(k + 1) * P],
                                                p2[:, h % 4, k * P:(k + 1) * P], C("ident"))
                        full(last, f"pT{r}_{h}")
                    if h + 4 < H2:
                        score(h + 4)
                    if h:
                        weigh(h - 1)

            need = split_need("n4")
            for n in range(8):
                two_tiles(FIRST["moba_qk"] + n, f"qk2_{n}", need)
                if n == 0:
                    late_norm(4)

            def value_blocks(r):
                for n in range(4):
                    c = FIRST[("moba_v", "fox_v")[r - 2]] + n
                    dst = fill(f"v{r}_{n}")
                    for t in range(TT):
                        last = values(dst[:, t * T:(t + 1) * T], c, 2 * P, hh, t, range(KT))
                    last.then_inc(chunk_used, 1)

            value_blocks(2)
            for n in range(4):
                for name in (f"qk2_{n}", f"qk2_{n + 4}", f"v2_{n}"):
                    wait_drained(pe, name)
            attention(2)
            need = split_need("o2")
            for n in range(4):
                two_tiles(FIRST["w_o0"] + n, f"w_o0_{n}", need, hq)
            ffn(2)

            need = split_need("n6")
            for n in range(4):
                two_tiles(FIRST["fox_k"] + n, f"qk3_{n}", need)
                if n == 0:
                    late_norm(6)
            value_blocks(3)
            pe.wait_ge(wf_s, 2)
            dst = fill("z")
            for t in range(TT):
                n = 0
                for k in range(KT):
                    xhi, xlo = (b[:, k, t * P:(t + 1) * P] for b in (h_hi, h_lo))
                    whi, wlo = (b[:, k * H2:(k + 1) * H2] for b in (wf_hi, wf_lo))
                    for a, b in ((xhi, whi), (xhi, wlo), (xlo, whi)):
                        n += 1
                        last = pe.matmul(dst[:, t * H2:(t + 1) * H2], a, b, start=n == 1,
                                         stop=n == 3 * KT, skip_group_check=True)
            full(last, "z")
            need = split_need("n6q")
            for n in range(4):
                two_tiles(FIRST["fox_q"] + n, f"qq_{n}", need, hq)
            pe.wait_ge(lf_s, 1)
            dst = fill("cum_col")
            lf0, lf1 = lf[:, 0, 0:H2], lf[:, 0, H2:2 * H2]
            pe.matmul(dst[:, 0:H2], C("tri", 0, P), lf0, start=True, stop=True, skip_group_check=True)
            pe.matmul(dst[:, H2:2 * H2], C("tri", P, P), lf0, start=True, stop=False,
                      skip_group_check=True)
            full(pe.matmul(dst[:, H2:2 * H2], C("tri", 0, P), lf1, start=False, stop=True,
                           skip_group_check=True), "cum_col")
            dst = fill("cum_row")
            pe.matmul(dst[0:H2, 0:T], lf0, C("tri"), start=True, stop=False, skip_group_check=True)
            full(pe.matmul(dst[0:H2, P:T], lf1, C("tri", 0, P), start=False, stop=True,
                           skip_group_check=True), "cum_row")
            for n in range(4):
                for name in (f"qk3_{n}", f"v3_{n}", f"qq_{n}"):
                    wait_drained(pe, name)
            wait_drained(pe, "cum_row")
            attention(3)
            need = split_need("o3")
            for n in range(4):
                two_tiles(FIRST["w_o1"] + n, f"w_o1_{n}", need, hq)
            ffn(3)
            norm(8)

        @block.scalar
        def _(act):
            def split_hi(c, it=0):
                act.wait_ge(loaded[c % RAW], 16 * (c // RAW + 1) + 16 * it)
                if c >= SPL:
                    act.wait_ge(chunk_used, c - SPL + 1 + 4 * it)
                act.copy(w_hi[:, c % SPL, :], raw[:, c % RAW, :]).then_inc(hi_ready, 1)

            def split_after(c, it=0):
                if c + SPL < NCH:
                    split_hi(c + SPL, it)

            def squares(src, q, n, total):
                if q >= 2:
                    act.wait_ge(res_ready, 4 * (q - 2) + n + 1)
                if n == 0 and q >= 2:
                    wait_full(act, f"ms_{q - 2}")
                if 3 * q + n > 1 and n:
                    act.wait_ge(acc_ready, 3 * q + n - 1)
                act.activation(total[:, :] if n == 0 else sq[:, :],
                               src[:, 2 * n:2 * n + 2, :].rearrange("p a t -> p (a t)"),
                               ACT.Square).then_inc(sq_ready, 1)

            def root(name, dst, width, count):
                src = wait_full(act, name)
                rows = dst.shape[0]
                act.activation(dst, src[0:rows, 0:width], ACT.Sqrt, bias=C("eps")[0:rows, :],
                               scale=1.0 / count).then_inc(drain_of(name), 1)

            def hi_of(name, dst, src, shift=None):
                act.wait_ge(t_ready, TN[name])
                if shift is None:
                    act.copy(dst, src).then_inc(h_hi_s, 1)
                else:
                    act.activation(dst, src, ACT.Identity, bias=shift).then_inc(h_hi_s, 1)

            def norm_tiles(r, shift=None, name=None, hi=None):
                name, hi = name or f"n{r}", h_hi if hi is None else hi
                for k in range(KT):
                    hi_of(f"{name}_{k}", hi[:, k, :], tmp[:, k % 3, 0:T],
                          None if shift is None else shift(k))

            def norm(r, shift=None):
                root(f"ms_{r}", rstd[:, 0:T], T, D)
                norm_tiles(r, shift)

            act.wait_ge(cols_in, 16)
            act.activation(cs[:, :], cols[:, COL["c"]:COL["c"] + 2 * KT], ACT.Silu).then_inc(cs_ready, 1)
            act.wait_ge(ctx_in, 16)
            for n in range(4):
                squares(ctxT, 0, n, acc_c)
            act.wait_ge(x_in, 16)
            for n in range(4):
                squares(x, 1, n, acc)
            split_hi(0)
            split_hi(1)
            act.wait_ge(ones_in, 16)
            root("ms_0", rstd[:, :], 2 * T, D)
            act.wait_ge(con_in, 16)
            wait_drained(act, "ada_a")
            for k in range(KT):
                act.wait_ge(t_ready, TN[f"n0_{k}"])
                act.activation(hc_hi[:, k, :], tmp[:, k % 3, 0:T], ACT.Identity, bias=ada[:, 1, k:k + 1])
                act.activation(h_hi[:, k, :], tmp[:, k % 3, T:2 * T], ACT.Identity,
                               bias=ada[:, 0, k:k + 1]).then_inc(h_hi_s, 1)

            c = FIRST["w_in"]
            for j in range(CKV):
                src = wait_full(act, f"ckv{j}")
                act.activation(qg[:, j, :], src[:, :], ACT.Square).then_inc(lat_sq, 1)
            split_after(c)
            rope = slice(NOPE, QKH)
            src = wait_full(act, "kr")
            act.activation(krg[rope, :], src[rope, :], ACT.Identity,
                           scale=V("k_norm", 0, rope)).then_inc(krg_s, 1)
            for i in range(2):
                act.activation(ksq[rope, i, :], src[rope, :], ACT.Square).then_inc(krg_s, 1)
            split_after(c + 1)
            root("ms_kv", rstd[:, :], 2 * T, CKV * P)
            for j in range(CKV):
                hi_of(f"ckv_{j}", ckv_hi[:, j, :], tmp[:, j, :])
            src = wait_full(act, "cq01")
            act.activation(qg[:, 0, :], src[:, :], ACT.Square).then_inc(lat_sq, 1)
            src = wait_full(act, "cq2")
            act.activation(qg[:, 1, 0:T], src[:, 0:T], ACT.Square).then_inc(lat_sq, 1)
            split_after(c + 2)

            def fourier_input(name, g):
                src = wait_full(act, name)
                act.copy(uF[:, g:g + 2, :].rearrange("p g t -> p (g t)"), src[:, :])\
                   .then_inc(drain_of(name), 1)

            fourier_input("f01", 0)
            split_after(c + 3)
            root("ms_cq", rstd[:, 0:T], T, CQ * P)
            for j in range(CQ):
                hi_of(f"cq_{j}", cq_hi[:, j, :], tmp[:, j, 0:T])
            fourier_input("f23", 2)
            split_after(c + 4)

            for h in range(MLA_H):
                src = wait_full(act, f"k{h}")
                if h >= 2:
                    act.wait_ge(kq_sum, h - 1)
                act.activation(ksq[0:NOPE, h % 2, :], src[0:NOPE, :], ACT.Square).then_inc(ksq_s, 1)
                act.activation(kT[0:NOPE, h, :], src[0:NOPE, :], ACT.Identity,
                               scale=V("k_norm", 0, slice(0, NOPE))).then_inc(drain_of(f"k{h}"), 1)
            split_after(FIRST["w_uk"])

            for j in range(MLA_H // 2):
                src = wait_full(act, f"q{j}")
                if j >= 2:
                    act.wait_ge(qrot_s, j - 1)
                act.activation(qg[0:QKH, j % 2, :], src[0:QKH, :], ACT.Identity,
                               scale=V("q_norm", 0, slice(0, QKH)))
                act.wait_ge(kq_sum, MLA_H + j - 1)
                act.activation(ksq[0:QKH, j % 2, :], src[0:QKH, :], ACT.Square).then_inc(qsq_s, 1)
                if j % 2:
                    split_after(FIRST["w_uq"] + j // 2)
            root("ms_kq", rs_b[0:len(BCAST), :], 2 * T, QKH)

            for t in range(4):
                src = wait_full(act, f"v0_{t}")
                act.copy(v0[:, t, :], src[:, :]).then_inc(drain_of(f"v0_{t}"), 1)
            split_after(FIRST["w_uv"])

            def hi_from(name, dst, bank_name):
                src = wait_full(act, bank_name)
                act.copy(dst, src[:, 0:T]).then_inc(h_hi_s, 1)

            S0 = float(QKH) ** -0.5
            steps = 2 * MLA_H

            def exponentials0(s):
                act.wait_ge(nb_s, s + 1)
                if s >= 3:
                    wait_full(act, f"pT0_{s - 3}")
                src = wait_full(act, f"s0_{s}")
                act.activation(p0[:, s % 3, :], src[:, :], ACT.Exp, bias=stat_(1, s), scale=S0,
                               accum_out=stat_(2, s)).then_inc(p_s, 1)

            exponentials0(0)
            for s in range(steps + 2):
                if s + 1 < steps:
                    exponentials0(s + 1)
                if s and s <= steps:
                    src = wait_full(act, f"pT0_{s - 1}")
                    act.copy(pT0[:, (s - 1) % 2, :], src[:, :]).then_inc(pT_s, 1)
                g = s // 4
                if s % 4 == 0 and g < FG:
                    src = wait_full(act, f"dft_a{g}")
                    act.copy(ab[:, g % 2, :, :].rearrange("p t c -> p (t c)"), src[:, :])\
                       .then_inc(drain_of(f"dft_a{g}"), 1)
                if s % 4 == 1:
                    if g:
                        hi_from(f"o_{g - 1}", h_hi[:, g - 1, :], f"o0_{g - 1}")
                    if g < FG:
                        hi_from(f"y_{g}", h_hi[:, 4 + g, :], f"dft_y{g}")

            def scaled_hi(k, gain, dst=h_hi):
                act.activation(dst[:, k, :], x[:, k, :], ACT.Identity, scale=gain(k)).then_inc(h_hi_s, 1)

            def residual(stage, c, gain=None):
                for n in range(4):
                    if n < 3:
                        split_after(c + n)
                    if gain is not None:
                        act.wait_ge(res_ready, 4 * stage + n + 1)
                        scaled_hi(2 * n, gain)
                        scaled_hi(2 * n + 1, gain)
                    squares(x, stage + 2, n, acc)

            def ffn(r):
                _, up, down = LAYERS[r]
                c = FIRST[up]

                def pair_hi(j, pair, it):
                    wait_drained(act, f"{up}_{j}", it)
                    act.copy(u_hi[:, pair, :], u_t[:, j // 2 % 2, :]
                             .rearrange("p (a t) -> p a t", a=2)).then_inc(u_hi_s, 1)

                def step(j, cc, it, pair):
                    if r < 2:
                        if j % 2 == 0:
                            src = wait_full(act, f"{up}_{j}", it)
                            act.activation(silu_b[:, :], src[:, :], ACT.Silu)\
                               .then_inc(drain_of(f"{up}_{j}"), 1)
                            split_after(cc, it)
                        else:
                            split_after(cc, it)
                            pair_hi(j, pair, it)
                    else:
                        split_after(cc, it)
                        wait_drained(act, f"{up}_{j}", it)
                        act.wait_ge(u_lo_s, U0[r] + j - 1 + 4 * it)
                        act.activation(u_t[:, j % 2, :], silu_b[:, :], ACT.Square)
                        act.activation(u_hi[:, pair, :], silu_b[:, :].rearrange("p (a t) -> p a t", a=2),
                                       ACT.Square).then_inc(u_hi_s, 1)

                act.preload_act_table(ACT.Silu if r < 2 else ACT.Square)
                with act.Fori(0, 5 if r < 2 else 4) as i:
                    for j in range(4):
                        step(j, c + j, i, ds(4 * i + 2 * (j // 2), 2) if r < 2 else ds(8 * i + 2 * j, 2))
                if r < 2:
                    for j in range(2):
                        step(4 + j, c + 20 + j, 0, slice(20, 22))
                c = FIRST[down]
                if r < 2:
                    for kc in range(8):
                        split_after(c + kc)
                    residual(2 * r + 1, c + 8, own("attn_norm") if r == 1 else None)
                else:
                    with act.Fori(0, 3) as i:
                        for n in range(4):
                            split_after(c + n, i)
                    residual(2 * r + 1, c + 12, own("kv_norm") if r == 2 else None)

            own = lambda name, layer=0: (lambda k: V(name, layer * KT + k))
            residual(0, FIRST["w_out0"])
            norm(1, lambda k: ada[:, 0, 3 * KT + k:3 * KT + k + 1])
            split_after(FIRST["w_out0"] + 3)
            ffn(0)

            wait_drained(act, "ada_c")
            norm(2, lambda k: ada[:, 2, k:k + 1])
            split_after(FIRST["down0"] + 11)
            c = FIRST["b_in"]

            def diagonals(first, end):
                for i in range(first, end):
                    act.activation(taps[:, i, :], C("ident"), ACT.Identity, scale=V("conf_dw", 4 * i))\
                       .then_inc(taps_s, 1)

            def centred_square(n):
                act.wait_ge(cen_s, n + 1)
                if n >= 2:
                    wait_full(act, f"var_conf{n - 2}")
                act.activation(csq[:, n % 2, :], cln[:, n, :], ACT.Square).then_inc(csq_s, 1)

            def group_root(n):
                if n >= 2:
                    act.wait_ge(cn_s, n - 1)
                root(f"var_conf{n}", rstd[:, (n % 2) * T:(n % 2 + 1) * T], T, P)

            diagonals(0, 11)
            for n in range(8):
                name = f"b_a{n}" if n < 4 else f"b_s{n - 4}"
                src = wait_full(act, name)
                if n >= 2:
                    wait_drained(act, f"b_a{n - 2}" if n < 6 else f"b_s{n - 6}")
                if n < 4:
                    act.activation(sig[:, n % 2, :], src[:, T:2 * T], ACT.Sigmoid).then_inc(sig_s, 1)
                else:
                    act.copy(sig[:, n % 2, :], src[:, T:2 * T]).then_inc(sig_s, 1)
                split_after(c + n)
                if n < 2:
                    diagonals(11 + 10 * n, 21 + 10 * n)
            centred_square(0)
            split_after(c + 8)
            group_root(0)
            centred_square(1)
            split_after(c + 9)
            for n in range(2):
                hi_of(f"sc_{n}", m_hi[:, 4 + n, :], tmp[:, n % 3, 0:T])
            group_root(1)
            centred_square(2)
            centred_square(3)
            for n in range(2, 4):
                hi_of(f"sc_{n}", m_hi[:, 4 + n, :], tmp[:, n % 3, 0:T])
            group_root(2)
            group_root(3)
            for n in range(4):
                act.wait_ge(cn_s, n + 1)
                act.activation(cln[:, n, :], cacc[:, n, :], ACT.Silu, bias=V("ln_b", n))\
                   .then_inc(cact_s, 1)
                act.wait_ge(cact_s, n + 1)
                act.copy(m_hi[:, n, :], cln[:, n, :]).then_inc(h_hi_s, 1)
            residual(2, FIRST["w_out1"])
            norm(3, lambda k: ada[:, 2, 3 * KT + k:3 * KT + k + 1])
            split_after(FIRST["w_out1"] + 3)
            ffn(1)

            def values_out(name, dst):
                src = wait_full(act, name)
                for t in range(TT):
                    last = act.activation(dst[:, t, :], src[:, t * T:(t + 1) * T], ACT.Identity,
                                          scale=rstd[:, T + t:T + t + 1])
                last.then_inc(drain_of(name), 1)

            def attention(r):
                base = 16 * (r - 1)

                def exponentials(h):
                    act.wait_ge(nb_s, base + h + 1)
                    for t, (a, n) in enumerate(((0, P), (P, 2 * P))):
                        last = act.activation(p2[:, h % 4, a:a + n], p2[:, h % 4, a:a + n], ACT.Exp,
                                              bias=stat_(1, 2 * h + t), scale=HD ** -0.5,
                                              accum_out=stat_(2, 2 * h + t))
                    last.then_inc(p_s, 1)

                exponentials(0)
                exponentials(1)
                for h in range(H2 + 2):
                    if h + 2 < H2:
                        exponentials(h + 2)
                    if h and h <= H2:
                        src = wait_full(act, f"pT{r}_{h - 1}")
                        act.copy(pT2[:, (h - 1) % 2, :], src[:, 0:3 * P]).then_inc(pT_s, 1)
                    if h % 2 == 1 and h > 1:
                        j = h // 2 - 1
                        hi_from(f"o{r}_{j}", h2_hi[:, j, :], f"o{r}_{j}")

            split_after(FIRST["down1"] + 11)
            root("ms_4", rstd[:, 0:T + TT], T + TT, D)
            for n in range(8):
                split_after(FIRST["moba_qk"] + n)
            act.wait_ge(rs_s, 1)
            for n in range(4):
                values_out(f"v2_{n}", v2[:, :, n * T:(n + 1) * T])
                split_after(FIRST["moba_v"] + n)
            attention(2)
            residual(4, FIRST["w_o0"], own("mlp_norm"))
            split_after(FIRST["w_o0"] + 3)
            root("ms_5", rstd[:, 0:T + TT], T + TT, D)
            ffn(2)

            split_after(FIRST["down2"] + 15)
            root("ms_6", rstd[:, 0:T + TT], T + TT, D)
            act.copy(wf_hi[:, :], cols[:, COL["w_f"]:COL["w_f"] + KT * H2]).then_inc(wf_s, 1)
            for n in range(4):
                split_after(FIRST["fox_k"] + n)
                for k in (2 * n, 2 * n + 1):
                    scaled_hi(k, own("attn_norm", 1), h2_hi)
            act.wait_ge(rs_s, 3)
            for n in range(4):
                values_out(f"v3_{n}", v2[:, :, n * T:(n + 1) * T])
                split_after(FIRST["fox_v"] + n)
            wait_drained(act, "z")
            act.activation(lf[:, 2, :], lf[:, 1, :], ACT.Abs).then_inc(lfa_s, 1)
            act.wait_ge(lfa_s, 1)
            act.activation(lf[:, 0, :], lf[:, 2, :], ACT.Exp, scale=-1.0).then_inc(lfa_s, 1)
            act.wait_ge(lfa_s, 2)
            act.activation(lf[:, 2, :], lf[:, 0, :], ACT.Ln, bias=C("ones", 0, 1)).then_inc(lfa_s, 1)
            for n in range(4):
                split_after(FIRST["fox_q"] + n)
            attention(3)
            residual(6, FIRST["w_o1"], own("mlp_norm", 1))
            split_after(FIRST["w_o1"] + 3)
            root("ms_7", rstd[:, 0:T + TT], T + TT, D)
            ffn(3)
            root("ms_8", rstd[:, 0:T], T, D)

        @block.vector
        def _(dve):
            order = [0]

            def link(ins):
                order[0] += 1
                ins.then_inc(v_own, 1)
                dve.wait_ge(v_own, order[0])

            def split_lo(c, it=0):
                if POOL_LO[0] <= c < POOL_LO[1]:
                    return
                dve.wait_ge(hi_ready, c + 1 + 4 * it)
                dve.tensor_tensor(w_lo[:, c % SPL, :], raw[:, c % RAW, :],
                                  w_hi[:, c % SPL, :].bitcast(F32), ALU.subtract).then_inc(lo_ready, 1)

            def split_after(c, it=0):
                if c + SPL < NCH:
                    split_lo(c + SPL, it)

            def add_squares(q, n, total):
                dve.wait_ge(sq_ready, 4 * q + n + 1)
                if n > 1:
                    dve.wait_ge(acc_ready, 3 * q + n - 1)
                dve.tensor_tensor(total[:, :], total[:, :], sq[:, :], ALU.add).then_inc(acc_ready, 1)

            def inverse(name, buf):
                wait_drained(dve, name)
                link(dve.reciprocal(buf, buf))

            def lo_of(name, dst, src, hi, shift=None):
                dve.wait_ge(h_hi_s, HN[name])
                dve.wait_ge(t_ready, TN[name])
                if shift is None:
                    dve.tensor_tensor(dst, src, hi.bitcast(F32), ALU.subtract).then_inc(h_lo_s, 1)
                else:
                    dve.scalar_tensor_tensor(dst, src, shift, hi.bitcast(F32), ALU.add,
                                             ALU.subtract).then_inc(h_lo_s, 1)

            def norm_tiles(name, scale, shift=None, hi=h_hi, lo=h_lo):
                dve.wait_ge(h_lo_s, HN[f"{name}_0"] - 1)
                for k in range(KT + 1):
                    if 3 <= k < KT:
                        dve.wait_ge(h_lo_s, HN[f"{name}_{k - 3}"])
                    if k < KT:
                        dve.scalar_tensor_tensor(tmp[:, k % 3, 0:T], x[:, k, :], scale(k), rstd[:, 0:T],
                                                 ALU.mult, ALU.mult).then_inc(t_ready, 1)
                    if k:
                        lo_of(f"{name}_{k - 1}", lo[:, k - 1, :], tmp[:, (k - 1) % 3, 0:T],
                              hi[:, k - 1, :], None if shift is None else shift(k - 1))

            def norm(r, scale, shift=None):
                inverse(f"ms_{r}", rstd[:, 0:T])
                norm_tiles(f"n{r}", scale, shift)

            def modulation(name, v, a, n, src_at):
                layer = v // 2
                last = dve.tensor_tensor(ada[:, v, a:a + n], banks[5][:, src_at:src_at + n],
                                         cols[:, COL["ada_b"] + layer * ADA + a:
                                              COL["ada_b"] + layer * ADA + a + n], ALU.add)
                return last

            def gains(v, norm_name, layer, at):
                return dve.scalar_tensor_tensor(
                    gain[:, 1 if v == 1 else 0, :], ada[:, v, at:at + KT], 1.0,
                    cols[:, COL[norm_name] + layer * KT:COL[norm_name] + (layer + 1) * KT],
                    ALU.add, ALU.mult)

            def weigh_both(a):
                src, before = weigh_waits(dve, a, 0), (2 * KT - 1) * ADA_DVE.index(a)
                for k in range(KT):
                    w = src[:, 2 * k * P:2 * (k + 1) * P]
                    for v in range(2):
                        by = cs[:, 2 * k + 1 - v:2 * k + 2 - v]
                        if k == 0:
                            ins = dve.tensor_scalar(macc[:, v, :], w, by, None, ALU.mult)
                        else:
                            dve.wait_ge(dve_own, before + 2 * (k - 1) + v + 1)
                            ins = dve.scalar_tensor_tensor(macc[:, v, :], w, by, macc[:, v, :],
                                                           ALU.mult, ALU.add)
                        ins.then_inc(ada_dve if (k, v) == (KT - 1, 1) else dve_own, 1)

            def weigh(a, it=0, ks=range(KT)):
                before = (2 * KT - 1) * len(ADA_DVE) + (KT - 1) * ((a - ADA_ALT) // 2)
                dst = macc[:, 1, :]
                for k in ks:
                    if k == 0:
                        weigh_waits(dve, a, it)
                        dve.tensor_scalar(dst, ada_w[:, a % AR, 0:2 * P], cs[:, 0:1], None, ALU.mult)\
                           .then_inc(dve_own, 1)
                    else:
                        dve.wait_ge(dve_own, before + k + (KT - 1) * it)
                        dve.scalar_tensor_tensor(dst, ada_w[:, a % AR, 2 * k * P:2 * (k + 1) * P],
                                                 cs[:, 2 * k:2 * k + 1], dst, ALU.mult, ALU.add)\
                           .then_inc(ada_dve if k == KT - 1 else dve_own, 1)

            link(dve.memset(one[:, :], 1.0))
            dve.wait_ge(cs_ready, 1)
            for a in ADA_DVE:
                weigh_both(a)
            for n in range(1, 4):
                add_squares(0, n, acc_c)
            for n in range(1, 4):
                add_squares(1, n, acc)
            inverse("ms_0", rstd[:, :])
            dve.wait_ge(cols_in, 16)
            dve.wait_ge(ada_used, ADA1)
            link(modulation("ada_a", 1, 0, 2 * KT, ADA))
            modulation("ada_a", 0, 0, 2 * KT, 0).then_inc(drain_of("ada_a"), 1)
            wait_drained(dve, "ada_a")
            link(gains(1, "norm1", 0, KT))
            link(gains(0, "norm1", 0, KT))
            dve.wait_ge(x_in, 16)
            dve.wait_ge(ctx_in, 16)
            for k in range(KT + 1):
                if 3 <= k < KT:
                    dve.wait_ge(h_lo_s, HN[f"n0_{k - 3}"])
                if k < KT:
                    dve.scalar_tensor_tensor(tmp[:, k % 3, 0:T], ctxT[:, k, :], gain[:, 1, k:k + 1],
                                             rstd[:, 0:T], ALU.mult, ALU.mult)
                    dve.scalar_tensor_tensor(tmp[:, k % 3, T:2 * T], x[:, k, :], gain[:, 0, k:k + 1],
                                             rstd[:, T:2 * T], ALU.mult, ALU.mult).then_inc(t_ready, 1)
                if k:
                    j = k - 1
                    dve.wait_ge(h_hi_s, HN[f"n0_{j}"])
                    dve.wait_ge(t_ready, TN[f"n0_{j}"])
                    dve.scalar_tensor_tensor(hc_lo[:, j, :], tmp[:, j % 3, 0:T], ada[:, 1, j:j + 1],
                                             hc_hi[:, j, :].bitcast(F32), ALU.add, ALU.subtract)
                    dve.scalar_tensor_tensor(h_lo[:, j, :], tmp[:, j % 3, T:2 * T], ada[:, 0, j:j + 1],
                                             h_hi[:, j, :].bitcast(F32), ALU.add,
                                             ALU.subtract).then_inc(h_lo_s, 1)
                if k == KT // 2:
                    split_lo(0)
            split_lo(1)
            dve.wait_ge(con_in, 16)

            def latents(name, n, width, gain_name, src, hi, lo):
                dve.wait_ge(h_lo_s, HN[f"{name}_0"] - 1)
                for j in range(n):
                    dve.scalar_tensor_tensor(tmp[:, j, 0:width], src(j), V(gain_name, j),
                                             rstd[:, 0:width], ALU.mult, ALU.mult).then_inc(t_ready, 1)
                for j in range(n):
                    lo_of(f"{name}_{j}", lo[:, j, :], tmp[:, j, 0:width], hi[:, j, :])

            c = FIRST["w_in"]
            split_after(c)
            split_after(c + 1)
            inverse("ms_kv", rstd[:, :])
            latents("ckv", CKV, 2 * T, "kv_ln", lambda j: banks[j][:, :], ckv_hi, ckv_lo)
            rope = slice(NOPE, QKH)
            src = wait_full(dve, "krot")
            dve.wait_ge(krg_s, 1)
            link(dve.tensor_tensor(kr[rope, 0:T], src[rope, 0:T], C("rope_s")[rope, :], ALU.mult))
            link(dve.tensor_tensor(kr[rope, T:2 * T], krg[rope, T:2 * T], C("rope_c")[rope, :], ALU.mult))
            dve.tensor_tensor(kr[rope, T:2 * T], kr[rope, T:2 * T], kr[rope, 0:T], ALU.add)\
               .then_inc(drain_of("krot"), 1)
            wait_drained(dve, "krot")
            dve.tensor_copy(kr[rope, 0:T], krg[rope, 0:T]).then_inc(kr_s, 1)
            split_after(c + 2)
            split_after(c + 3)
            inverse("ms_cq", rstd[:, 0:T])
            latents("cq", CQ, T, "q_ln", lambda j: (banks[3][:, 0:T], banks[3][:, T:2 * T],
                                                     banks[6][:, 0:T])[j], cq_hi, cq_lo)
            split_after(c + 4)

            split_after(FIRST["w_uk"])

            for j in range(MLA_H // 2):
                two = lambda a: a.rearrange("p (i t) -> p i t", i=2)
                table = lambda name: C(name)[0:QKH, :].rearrange("p (o t) -> p o t", o=1)\
                    .broadcast_to([QKH, 2, T])
                src = wait_full(dve, f"qrot{j}")
                dve.wait_ge(qsq_s, j + 1)
                if j:
                    dve.wait_ge(qrot_s, j)
                else:
                    dve.wait_ge(h_lo_s, HN[f"cq_{CQ - 1}"])
                dve.tensor_tensor(two(tmp[0:QKH, 0, :]), two(qg[0:QKH, j % 2, :]), table("rope_c"),
                                  ALU.mult)
                dve.tensor_tensor(two(tmp[0:QKH, 1, :]), two(src[0:QKH, :]), table("rope_s"), ALU.mult)\
                   .then_inc(drain_of(f"qrot{j}"), 1)
                wait_drained(dve, f"qrot{j}")
                dve.tensor_tensor(qT[0:QKH, 2 * j:2 * j + 2, :].rearrange("p i t -> p (i t)"),
                                  tmp[0:QKH, 0, :], tmp[0:QKH, 1, :], ALU.add).then_inc(qrot_s, 1)
                if j % 2:
                    split_after(FIRST["w_uq"] + j // 2)
            weigh(ADA_ALT + 1)
            wait_drained(dve, "ms_kq")
            dve.reciprocal(rs_b[0:len(BCAST), :], rs_b[0:len(BCAST), :]).then_inc(krs_s, 1)
            split_after(FIRST["w_uv"])
            for name in BCAST:
                src, n = wait_full(dve, f"rs_{name}"), int(name[1])
                if name[0] == "k":
                    wait_drained(dve, name)
                    dve.wait_ge(kTr_s, n + 1)
                    dst = kT[0:QKH, n, :]
                else:
                    dve.wait_ge(qrot_s, n + 1)
                    dst = qT[0:QKH, 2 * n:2 * n + 2, :].rearrange("p i t -> p (i t)")
                dve.tensor_tensor(dst, dst, src[0:QKH, :], ALU.mult).then_inc(drain_of(f"rs_{name}"), 1)

            def lo_from(name, dst, hi, bank_name):
                dve.wait_ge(h_hi_s, HN[name])
                src = banks[bank_use[bank_name].b]
                dve.tensor_tensor(dst, src[:, 0:T], hi.bitcast(F32), ALU.subtract).then_inc(h_lo_s, 1)

            def maximum0(s):
                src = wait_full(dve, f"s0_{s}")
                link(dve.reduce_max(stat_(0, s), src[:, :], AX))
                dve.tensor_scalar(stat_(1, s), stat_(0, s), -float(QKH) ** -0.5, None, ALU.mult)\
                   .then_inc(nb_s, 1)

            steps = 2 * MLA_H
            maximum0(0)
            maximum0(1)
            for s in range(steps + 2):
                if s < steps:
                    dve.wait_ge(p_s, s + 1)
                    link(dve.reciprocal(stat_(3, s), stat_(2, s)))
                    dve.tensor_scalar(p0[:, s % 3, :], p0[:, s % 3, :], stat_(3, s), None, ALU.mult)\
                       .then_inc(pn_s, 1)
                if s + 2 < steps:
                    maximum0(s + 2)
                if s + 1 in PAIR_AT:
                    weigh(ADA_ALT + 3 + 2 * PAIR_AT.index(s + 1))
                g = s // 4
                if s % 4 == 1:
                    if g:
                        lo_from(f"o_{g - 1}", h_lo[:, g - 1, :], h_hi[:, g - 1, :], f"o0_{g - 1}")
                    if g < FG:
                        lo_from(f"y_{g}", h_lo[:, 4 + g, :], h_hi[:, 4 + g, :], f"dft_y{g}")
            dve.wait_ge(ada_used, NADA)
            modulation("ada_b", 0, 2 * KT, ADA - 2 * KT, 2 * KT).then_inc(drain_of("ada_b"), 1)
            wait_drained(dve, "ada_b")

            def scaled_lo(name, k, scale, hi=h_hi, lo=h_lo):
                dve.wait_ge(h_hi_s, HN[f"{name}_{k}"])
                dve.scalar_tensor_tensor(lo[:, k, :], x[:, k, :], scale(k), hi[:, k, :].bitcast(F32),
                                         ALU.mult, ALU.subtract).then_inc(h_lo_s, 1)

            def late_inverse(r):
                wait_drained(dve, f"ms_{r}")
                dve.reciprocal(rstd[:, 0:T + TT], rstd[:, 0:T + TT]).then_inc(rs_s, 1)
                dve.wait_ge(rs_s, r - 3)

            def by_rstd(name, dst):
                src = wait_full(dve, name)
                dve.tensor_tensor(dst, src[:, :].rearrange("p (a t) -> p a t", a=2), rstd_two, ALU.mult)\
                   .then_inc(drain_of(name), 1)

            rstd_two = rstd[:, 0:T].rearrange("p (o t) -> p o t", o=1).broadcast_to([P, 2, T])

            def residual(stage, c, names, gate=None, scale=None):
                for n in range(4):
                    src = wait_full(dve, names[n])
                    if gate is None:
                        two = x[:, 2 * n:2 * n + 2, :].rearrange("p a t -> p (a t)")
                        dve.tensor_tensor(two, two, src[:, :], ALU.add).then_inc(res_ready, 1)
                    else:
                        for j in range(2):
                            last = dve.scalar_tensor_tensor(
                                x[:, 2 * n + j, :], src[:, j * T:(j + 1) * T], gate(2 * n + j),
                                x[:, 2 * n + j, :], ALU.mult, ALU.add)
                        last.then_inc(res_ready, 1)
                    if n < 3:
                        split_after(c + n)
                    if scale is not None:
                        dve.wait_ge(res_ready, 4 * stage + n + 1)
                        for k in (2 * n, 2 * n + 1):
                            scaled_lo(f"n{stage + 1}", k, scale)
                    if n:
                        add_squares(stage + 2, n, acc)

            def ffn(r, gate=None):
                _, up, down = LAYERS[r]
                c = FIRST[up]

                def step(j, cc, it, pair, count):
                    if r < 2 and j % 2 == 0:
                        split_after(cc, it)
                        if r == 0 and j == 2:
                            weigh(ADA2 + 1, it, range(KT // 2, KT))
                        return
                    slot = (j // 2 if r < 2 else j) % 2
                    if r < 2:
                        dve.wait_ge(u_lo_s, count - 1)
                        wait_drained(dve, f"{up}_{j - 1}", it)
                        src = wait_full(dve, f"{up}_{j}", it)
                        dve.tensor_tensor(u_t[:, slot, :], silu_b[:, :], src[:, :], ALU.mult)\
                           .then_inc(drain_of(f"{up}_{j}"), 1)
                    else:
                        dve.wait_ge(u_hi_s, count - 1)
                        src = wait_full(dve, f"{up}_{j}", it)
                        dve.scalar_tensor_tensor(silu_b[:, :].rearrange("p (a t) -> p a t", a=2),
                                                 src[:, :].rearrange("p (a t) -> p a t", a=2), 0.0,
                                                 rstd_two, ALU.max, ALU.mult)\
                           .then_inc(drain_of(f"{up}_{j}"), 1)
                    split_after(cc, it)
                    dve.wait_ge(u_hi_s, count)
                    dve.tensor_tensor(u_lo[:, pair, :],
                                      u_t[:, slot, :].rearrange("p (a t) -> p a t", a=2),
                                      u_hi[:, pair, :].bitcast(F32), ALU.subtract).then_inc(u_lo_s, 1)
                    if r == 0 and j == 1:
                        weigh(ADA2 + 1, it, range(KT // 2))

                with dve.Fori(0, 5 if r < 2 else 4) as i:
                    for j in range(4):
                        if r < 2:
                            step(j, c + j, i, ds(4 * i + 2 * (j // 2), 2), U0[r] + j // 2 + 1 + 2 * i)
                        else:
                            step(j, c + j, i, ds(8 * i + 2 * j, 2), U0[r] + j + 1 + 4 * i)
                if r < 2:
                    for j in range(2):
                        step(4 + j, c + 20 + j, 0, slice(20, 22), U0[r] + 11)
                if r == 0:
                    weigh(ADA3 + 1)
                c = FIRST[down]
                names = [f"{down}_{n}" for n in range(4)]
                if r < 2:
                    for kc in range(8):
                        split_after(c + kc)
                        if r == 0 and kc % 2:
                            weigh(ADA3 + 3 + 2 * (kc // 2))
                    residual(2 * r + 1, c + 8, names, gate, own("attn_norm", 0) if r == 1 else None)
                else:
                    with dve.Fori(0, 3) as i:
                        for n in range(4):
                            split_after(c + n, i)
                    residual(2 * r + 1, c + 12, names, gate, own("kv_norm") if r == 2 else None)

            col = lambda v, a: (lambda k: ada[:, v, a * KT + k:a * KT + k + 1])
            own = lambda name, layer=0: (lambda k: V(name, layer * KT + k))
            link(gains(0, "norm2", 0, 4 * KT))
            residual(0, FIRST["w_out0"], [f"w_out0_{n}" for n in range(4)], col(0, 2))
            norm(1, lambda k: gain[:, 0, k:k + 1], col(0, 3))
            split_after(FIRST["w_out0"] + 3)
            ffn(0, col(0, 5))

            dve.wait_ge(ada_used, 2 * NADA)
            modulation("ada_c", 2, 0, ADA, ADA).then_inc(drain_of("ada_c"), 1)
            wait_drained(dve, "ada_c")
            link(gains(2, "norm1", 1, KT))
            norm(2, lambda k: gain[:, 0, k:k + 1], col(2, 0))
            split_after(FIRST["down0"] + 11)
            for a in range(2):
                dve.memset(conf[:, :, a * (PAD + T):a * (PAD + T) + PAD], 0.0)
                link(dve.memset(scin[:, :, a * (T + 1):a * (T + 1) + 1], 0.0))

            def gated(n, name, dst):
                src = wait_full(dve, name)
                dve.wait_ge(sig_s, n + 1)
                dve.tensor_tensor(dst, src[:, 0:T], sig[:, n % 2, :], ALU.mult)\
                   .then_inc(drain_of(name), 1)
                wait_drained(dve, name)

            wrote = {}

            def tap(kind, n, i):
                dst, src = (cacc[:, n, :], conf[:, n, i:i + T]) if kind == "conf" else \
                    (scacc[:, n, :], scin[:, n, i:i + T])
                w = V("conf_dw" if kind == "conf" else "sc_dw", 4 * i + n)
                if i == 0 and kind == "conf":
                    ins = dve.tensor_scalar(dst, src, w, V("conf_b", n), ALU.mult, ALU.add)
                elif i == 0:
                    ins = dve.tensor_scalar(dst, src, w, None, ALU.mult)
                else:
                    dve.wait_ge(v_own, wrote[kind, n])
                    ins = dve.scalar_tensor_tensor(dst, src, w, dst, ALU.mult, ALU.add)
                if kind == "conf" and i == CONV - 1:
                    ins.then_inc(conv_s, 1)
                else:
                    order[0] += 1
                    ins.then_inc(v_own, 1)
                    wrote[kind, n] = order[0]

            def conf_input(n):
                gated(n, f"b_a{n}", conf[:, n, PAD:PAD + T])

            def centre(n):
                src = wait_full(dve, f"ms_conf{n}")
                dve.wait_ge(conv_s, n + 1)
                dve.scalar_tensor_tensor(cln[:, n, :], src[:, 0:T], -1.0 / P, cacc[:, n, :], ALU.mult,
                                         ALU.add).then_inc(cen_s, 1)

            conf_input(0)
            conf_input(1)
            for i in range(8):
                tap("conf", 1, i)
            conf_input(2)
            for i in range(12):
                tap("conf", 2, i)
                tap("conf", 1, 8 + i)
            conf_input(3)
            for i in range(20, CONV - 1):
                tap("conf", 1, i)
                tap("conf", 2, i - 8)
            src = wait_full(dve, "conv0")
            dve.tensor_scalar(cacc[:, 0, :], src[:, 0:T], V("conf_b", 0), None, ALU.add)\
               .then_inc(drain_of("conv0"), 1)
            tap("conf", 2, 22)
            tap("conf", 1, CONV - 1)
            for i in range(8):
                tap("conf", 3, i)
                tap("conf", 2, 23 + i)
            at = 8
            for n in range(4):
                gated(4 + n, f"b_s{n}", scin[:, n, 1:1 + T])
                for i in range(SCONV):
                    tap("sc", n, i)
                    for at in range(at, min(at + 2, CONV)):
                        tap("conf", 3, at)
                    at += 1
            centre(0)

            def short_product(n):
                src = wait_full(dve, f"b_b{n // 2}")
                dve.wait_ge(v_own, wrote["sc", n])
                dve.wait_ge(h_lo_s, HN["sc_0"] - 1 + n // 3)
                dve.tensor_tensor(tmp[:, n % 3, 0:T], src[:, (n % 2) * T:(n % 2 + 1) * T],
                                  scacc[:, n, :], ALU.mult).then_inc(t_ready, 1)

            def short_lo(n):
                lo_of(f"sc_{n}", m_lo[:, 4 + n, :], tmp[:, n % 3, 0:T], m_hi[:, 4 + n, :])

            centre(1)
            short_product(0)
            short_product(1)
            centre(2)
            centre(3)
            short_lo(0)
            short_lo(1)
            short_product(2)
            short_product(3)
            short_lo(2)
            short_lo(3)
            for n in range(4):
                half = rstd[:, (n % 2) * T:(n % 2 + 1) * T]
                inverse(f"var_conf{n}", half)
                dve.wait_ge(cen_s, n + 1)
                dve.scalar_tensor_tensor(cacc[:, n, :], cln[:, n, :], V("ln_g", n), half, ALU.mult,
                                         ALU.mult).then_inc(cn_s, 1)
            for n in range(4):
                dve.wait_ge(h_hi_s, HN[f"conf_{n}"])
                dve.tensor_tensor(m_lo[:, n, :], cln[:, n, :], m_hi[:, n, :].bitcast(F32),
                                  ALU.subtract).then_inc(h_lo_s, 1)
            link(gains(2, "norm2", 1, 4 * KT))
            residual(2, FIRST["w_out1"], [f"w_out1_{n}" for n in range(4)], col(2, 2))
            norm(3, lambda k: gain[:, 0, k:k + 1], col(2, 3))
            split_after(FIRST["w_out1"] + 3)
            ffn(1, col(2, 5))

            def attention(r):
                base = 16 * (r - 1)

                def maximum(h):
                    src = wait_full(dve, f"s{r}_{h}")
                    if h >= 4:
                        wait_full(dve, f"pT{r}_{h - 4}")
                    if r == 2:
                        dve.scalar_tensor_tensor(p2[:, h % 4, :], C("alibi"),
                                                 2.0 ** (-8.0 * (h + 1) / H2) * HD ** 0.5,
                                                 src[:, 0:3 * P], ALU.mult, ALU.add)\
                           .then_inc(drain_of(f"s{r}_{h}"), 1)
                    else:
                        for t, (a, n) in enumerate(((0, P), (P, 2 * P))):
                            last = dve.scalar_tensor_tensor(
                                p2[:, h % 4, a:a + n], src[:, a:a + n],
                                ccol[:, t * H2 + h:t * H2 + h + 1], C("mask", a, n), ALU.add, ALU.add)
                        last.then_inc(drain_of(f"s{r}_{h}"), 1)
                    wait_drained(dve, f"s{r}_{h}")
                    for t, (a, n) in enumerate(((0, P), (P, 2 * P))):
                        last = dve.reduce_max(stat_(0, 2 * h + t), p2[:, h % 4, a:a + n], AX)
                    link(last)
                    dve.tensor_scalar(stat_(1, 2 * h, 2), stat_(0, 2 * h, 2), -HD ** -0.5, None,
                                      ALU.mult).then_inc(nb_s, 1)

                for h in range(3):
                    maximum(h)
                for h in range(H2 + 2):
                    if h < H2:
                        dve.wait_ge(p_s, base + h + 1)
                        link(dve.reciprocal(stat_(3, 2 * h, 2), stat_(2, 2 * h, 2)))
                        for t, (a, n) in enumerate(((0, P), (P, 2 * P))):
                            last = dve.tensor_scalar(p2[:, h % 4, a:a + n], p2[:, h % 4, a:a + n],
                                                     stat_(3, 2 * h + t), None, ALU.mult)
                        last.then_inc(pn_s, 1)
                    if h + 3 < H2:
                        maximum(h + 3)
                    if h % 2 == 1 and h > 1:
                        j = h // 2 - 1
                        lo_from(f"o{r}_{j}", h2_lo[:, j, :], h2_hi[:, j, :], f"o{r}_{j}")

            split_after(FIRST["down1"] + 11)
            late_inverse(4)
            for n in range(8):
                by_rstd(f"qk2_{n}", (q2, k2)[n // 4][:, 2 * (n % 4):2 * (n % 4) + 2, :])
                split_after(FIRST["moba_qk"] + n)
            for n in range(4):
                split_after(FIRST["moba_v"] + n)
            attention(2)
            residual(4, FIRST["w_o0"], [f"w_o0_{n}" for n in range(4)],
                     scale=own("mlp_norm", 0))
            split_after(FIRST["w_o0"] + 3)
            late_inverse(5)
            ffn(2)

            split_after(FIRST["down2"] + 15)
            late_inverse(6)
            dve.wait_ge(wf_s, 1)
            dve.tensor_tensor(wf_lo[:, :], cols[:, COL["w_f"]:COL["w_f"] + KT * H2],
                              wf_hi[:, :].bitcast(F32), ALU.subtract).then_inc(wf_s, 1)
            for n in range(4):
                by_rstd(f"qk3_{n}", k2[:, 2 * n:2 * n + 2, :])
                split_after(FIRST["fox_k"] + n)
                for k in (2 * n, 2 * n + 1):
                    scaled_lo("n6q", k, own("attn_norm", 1), h2_hi, h2_lo)
            for n in range(4):
                split_after(FIRST["fox_v"] + n)
            src = wait_full(dve, "z")
            for t in range(TT):
                last = dve.scalar_tensor_tensor(lf[:, 1, t * H2:(t + 1) * H2],
                                                src[:, t * H2:(t + 1) * H2], rstd[:, T + t:T + t + 1],
                                                cols[:, COL["b_f"]:COL["b_f"] + H2], ALU.mult, ALU.add)
            last.then_inc(drain_of("z"), 1)
            dve.wait_ge(lfa_s, 3)
            dve.scalar_tensor_tensor(lf[:, 0, :], lf[:, 1, :], 0.0, lf[:, 2, :], ALU.min,
                                     ALU.subtract).then_inc(lf_s, 1)
            for n in range(4):
                by_rstd(f"qq_{n}", q2[:, 2 * n:2 * n + 2, :])
                split_after(FIRST["fox_q"] + n)
            src = wait_full(dve, "cum_col")
            dve.tensor_scalar(ccol[:, :], src[:, 0:TT * H2], HD ** 0.5, None, ALU.mult)\
               .then_inc(drain_of("cum_col"), 1)
            src = wait_full(dve, "cum_row")
            dve.tensor_scalar(crow[0:H2, :], src[0:H2, 0:T], -HD ** 0.5, None, ALU.mult)\
               .then_inc(drain_of("cum_row"), 1)
            wait_drained(dve, "cum_row")
            attention(3)
            residual(6, FIRST["w_o1"], [f"w_o1_{n}" for n in range(4)],
                     scale=own("mlp_norm", 1))
            split_after(FIRST["w_o1"] + 3)
            late_inverse(7)
            ffn(3)
            inverse("ms_8", rstd[:, 0:T])
            for k in range(KT):
                dve.scalar_tensor_tensor(x[:, k, :], x[:, k, :], V("final", k), rstd[:, 0:T],
                                         ALU.mult, ALU.mult).then_inc(res_ready, 1)

        @block.gpsimd
        def _(pool):
            def weigh(a, it=0):
                m = a - ADA1 if a < ADA_ALT else ADA_ALT - ADA1 + (a - ADA_ALT) // 2
                w = ada_w[:, a % AR, :]
                own = lambda n: pool.wait_ge(pool_own, 3 * m + n + 3 * it)
                weigh_waits(pool, a, it)
                by_k = lambda v: v.rearrange("p (k n) -> p k n", k=KT)
                pool.tensor_tensor(by_k(w), by_k(w), by_k(cs[:, :])[:, :, 0:1].broadcast_to([P, KT, 2 * P]),
                                   ALU.mult).then_inc(pool_own, 1)
                for n, half in enumerate((KT * P, KT * P // 2)):
                    own(n + 1)
                    pool.tensor_tensor(w[:, 0:half], w[:, 0:half], w[:, half:2 * half], ALU.add)\
                        .then_inc(pool_own, 1)
                own(3)
                pool.tensor_tensor(macc[:, a % 2, :], w[:, 0:2 * P], w[:, 2 * P:4 * P], ALU.add)\
                    .then_inc(ada_pool, 1)

            pool.wait_ge(cs_ready, 1)
            for a in range(ADA1, ADA_ALT):
                weigh(a)
            pool.wait_ge(ada_pool, ADA_ALT - ADA1)
            pool.wait_ge(kr_s, 1)
            rope = slice(NOPE, QKH)
            for h in range(MLA_H):
                pool.tensor_copy(kT[rope, h, :], kr[rope, :]).then_inc(kTr_s, 1)
            pool.wait_ge(kTr_s, MLA_H)
            for a in range(ADA_ALT, ADA2, 2):
                weigh(a)
            with pool.Fori(0, 5) as i:
                weigh(ADA2, i)
            for a in range(ADA3, 2 * NADA, 2):
                weigh(a)
            first, end = POOL_LO
            for c in range(first, end):
                pool.wait_ge(hi_ready, c + 1)
                pool.tensor_tensor(w_lo[:, c % SPL, :], raw[:, c % RAW, :],
                                   w_hi[:, c % SPL, :].bitcast(F32), ALU.subtract).then_inc(lo_pool, 1)


def columns(vector):
    v = np.asarray(vector, np.float32).reshape(-1, P)
    return v.T


def full_depth(w):
    return w.reshape(KT, P, -1, 2 * P).transpose(2, 1, 0, 3).reshape(-1, P, CH)


def by_depth(w):
    k = -(-w.shape[0] // D)
    w = np.concatenate([w, np.zeros((k * D - w.shape[0], D), w.dtype)])
    return w.reshape(k, KT, P, 4, 2 * P).transpose(0, 3, 2, 1, 4).reshape(-1, P, CH)


def padded(w):
    return np.concatenate([w, np.zeros((P, CH - w.shape[1]), w.dtype)], 1)[None]


def pad_last(w, before, after):
    return np.pad(w, [(0, 0)] * (w.ndim - 1) + [(before, after)])


def constants():
    con = np.zeros((P, NCON), np.float32)

    def put(name, value, a=0):
        con[:value.shape[0], CON[name] + a:CON[name] + a + value.shape[1]] = value

    put("ident", np.eye(P))
    put("ones", np.ones((P, P)))
    i, t = np.arange(P), np.arange(T)
    w = 2 * np.pi * np.outer(i, i) / P
    put("dft_c", np.concatenate([np.cos(w), np.sin(w)], 1))
    w = 2 * np.pi * np.outer(t, t) / T
    for part, m in enumerate((np.cos(w), -np.sin(w))):
        for j in range(TT):
            put("dft_n", m[j * P:(j + 1) * P] / np.sqrt(T * P), (2 * part + j) * T)
    half = ROPE // 2
    rot = np.zeros((QKH, QKH))
    for j in range(half):
        rot[NOPE + half + j, NOPE + j] = -1
        rot[NOPE + j, NOPE + half + j] = 1
    put("rot", rot)
    inv = (10000.0 ** (-np.arange(ROPE // 4, dtype=np.float32) / (ROPE // 4))).astype(np.float32)
    angle = np.concatenate([np.outer(inv, t // 64), np.outer(inv, t % 64)]).astype(np.float32)
    put("rope_c", np.concatenate([np.ones((NOPE, T)), np.cos(angle), np.cos(angle)]))
    put("rope_s", np.concatenate([np.zeros((NOPE, T)), np.sin(angle), np.sin(angle)]))
    q = np.concatenate([i[:, None] - i[None], P + i[:, None] - t[None]], 1)
    put("alibi", np.where(q < 0, NEG, -q))
    put("mask", np.where(q < 0, NEG, 0.0))
    put("tri", (i[:, None] <= t[None]).astype(np.float32))
    put("onehot", np.eye(H2))
    put("sel", np.eye(1, 23, 11).repeat(P, 0))
    put("eps", np.full((P, 1), EPS))
    return con


def kernel(**inputs):
    import concourse.bacc as bacc
    from concourse.bass_utils import run_bass_kernel_spmd

    a = {name: np.asarray(value) for name, value in inputs.items()}
    w_in = a["a_w_in"][0]
    z = lambda n: np.zeros((D, n), w_in.dtype)
    latents = w_in[:, 0:672]
    first = np.concatenate([latents[:, 384:640], z(64), latents[:, 640:672], z(32), latents[:, 0:384],
                            w_in[:, 672:]], 1)
    heads = lambda w, k: pad_last(w, 0, P - w.shape[-1]).reshape(k, P, -1)
    w_uk = heads(a["a_w_uk"][0], CKV).transpose(1, 0, 2).reshape(P, -1)
    w_uq = heads(a["a_w_uq"][0], CQ).reshape(CQ, P, 2, 4 * P).transpose(2, 1, 0, 3).reshape(2, P, -1)
    w_uv = a["a_w_uv"][0].reshape(CKV, P, -1).transpose(1, 0, 2).reshape(P, -1)

    def two_by_two(*ws):
        n = ws[0].shape[1] // P
        return full_depth(np.stack([w.reshape(D, n, P) for w in ws], 2).reshape(D, -1))

    def swiglu_up(layer):
        one, three = full_depth(a["ffn_w1"][layer]), full_depth(a["ffn_w3"][layer])
        return np.stack([one, three], 1).reshape(-1, P, CH)

    b_in = np.split(a["b_w_in"][0], 5, 1)
    qkv, kv = a["moba_w_qkv_2"][0], a["w_kv_2"]
    stream = np.concatenate([
        full_depth(first), padded(w_uk), padded(w_uq[0]), padded(w_uq[1]), padded(w_uv),
        full_depth(a["a_w_out"][0]), swiglu_up(0), by_depth(a["ffn_w2"][0]),
        two_by_two(b_in[0], b_in[1]), two_by_two(b_in[3], b_in[4]), full_depth(b_in[2]),
        full_depth(a["b_w_out"][0]), swiglu_up(1), by_depth(a["ffn_w2"][1]),
        full_depth(qkv), full_depth(a["w_o_2"][0]), full_depth(a["w_up_2"][0]), by_depth(a["w_down_2"][0]),
        full_depth(kv), full_depth(a["fox_w_q_2"][0]), full_depth(a["w_o_2"][1]),
        full_depth(a["w_up_2"][1]), by_depth(a["w_down_2"][1])])
    assert stream.shape[0] == NCH
    ada_stream = np.concatenate([full_depth(w) for w in a["ada_w"]])

    parts = {"norm1": columns(a["norm1_g"]), "norm2": columns(a["norm2_g"]), "ada_b": columns(a["ada_b"]),
             "q_ln": columns(a["a_q_ln_g"]), "kv_ln": columns(a["a_kv_ln_g"]),
             "q_norm": columns(pad_last(a["a_q_norm_g"], 0, P - QKH)),
             "k_norm": columns(pad_last(a["a_k_norm_g"], 0, P - QKH)),
             "conf_dw": columns(a["b_conf_dw"][0]), "conf_b": columns(a["b_conf_dw_b"]),
             "ln_g": columns(a["b_conf_ln_g"]), "ln_b": columns(a["b_conf_ln_b"]),
             "sc_dw": columns(a["b_sc_dw"][0]), "attn_norm": columns(a["attn_norm_2"]),
             "kv_norm": columns(a["kv_norm_2"]), "mlp_norm": columns(a["mlp_norm_2"]),
             "final": columns(a["final_norm_2"]), "b_f": np.repeat(a["b_f_2"][None], P, 0),
             "c": np.stack([columns(a["c"][0]), columns(a["c_ctx"])], 2).reshape(P, -1),
             "w_f": a["w_f_2"].reshape(KT, P, H2).transpose(1, 0, 2).reshape(P, -1)}
    by_tile = lambda t: t[0].T.reshape(KT, P, T).transpose(1, 0, 2)
    arrays = {"stream": stream, "ada_stream": ada_stream, "x": by_tile(a["x"]), "ctx": by_tile(a["ctx"]),
              "cols": np.concatenate([parts[name] for name, _ in COLS], 1), "con": constants()}
    arrays = {f"in_{name}": np.ascontiguousarray(v) for name, v in arrays.items()}

    nc = bacc.Bacc("TRN2", target_bir_lowering=False, num_devices=1)
    args = [nc.dram_tensor(name, v.shape, F32, kind="ExternalInput").ap() for name, v in arrays.items()]
    out = nc.dram_tensor("out_0", (KT, P, T), F32, kind="ExternalOutput").ap()
    program(nc, *args, out)
    got = run_bass_kernel_spmd(nc, [arrays], core_ids=[0]).results[0]["out_0"]
    return np.ascontiguousarray(np.asarray(got).reshape(D, T).T.reshape(1, T, D))
```
